# Optimizing a Trainium2 kernel written in Bass

```python
import jax, jax.numpy as jnp
from jax import lax
import numpy as np
import math

D_MODEL = 2048
BATCH = 1
SEQ = 256
DEPTH = 1

CHUNK = 64
PLE_DIM = 256
DN_HEADS = 16
DN_HEAD_DIM = 128
DN_WIDTH = DN_HEADS * DN_HEAD_DIM
SHORT_CONV = 4
CONV_CH = D_MODEL
CONV_KERNEL = 31
N_BRANCHES = 2
EPS = 1e-6
IN_SIZES = (3 * DN_WIDTH,
            DN_WIDTH,
            DN_HEADS,
            DN_HEADS,
            2 * CONV_CH,
            CONV_CH,
            N_BRANCHES * D_MODEL)
IN_COLS = sum(IN_SIZES)


def _split_points():
    return np.cumsum(np.array(IN_SIZES))[:-1].tolist()

def rmsnorm(x, g):
    xf = x.astype(jnp.float32)
    y = xf * lax.rsqrt(jnp.mean(xf * xf, axis=-1, keepdims=True) + EPS)
    return (y * g.astype(jnp.float32)).astype(x.dtype)

def layernorm(x, g, b):
    xf = x.astype(jnp.float32)
    mu = jnp.mean(xf, axis=-1, keepdims=True)
    var = jnp.mean(jnp.square(xf - mu), axis=-1, keepdims=True)
    y = (xf - mu) * lax.rsqrt(var + EPS)
    return (y * g.astype(jnp.float32) + b.astype(jnp.float32)).astype(x.dtype)

def l2norm(x):
    return x * lax.rsqrt(jnp.sum(x * x, axis=-1, keepdims=True) + EPS)

def causal_depthwise_conv(x, w):
    K = w.shape[0]
    xp = jnp.pad(x, ((0, 0), (K - 1, 0), (0, 0)))
    return lax.conv_general_dilated(
        xp, w[:, None, :].astype(x.dtype), window_strides=(1,), padding='VALID',
        dimension_numbers=('NWC', 'WIO', 'NWC'), feature_group_count=x.shape[-1])

def gated_delta_chunked(q, k, v, g, beta):
    B, S, H, Dk = q.shape
    nc = S // CHUNK

    def to_chunks(t):
        t = t.reshape((B, nc, CHUNK, H) + t.shape[3:])
        return jnp.moveaxis(t, 3, 1)

    q, k, v = to_chunks(q) * (Dk ** -0.5), to_chunks(k), to_chunks(v)
    g, beta = to_chunks(g), to_chunks(beta)
    gc = jnp.cumsum(g, axis=-1)
    idx = jnp.arange(CHUNK)
    causal = idx[:, None] >= idx[None, :]
    strict = idx[:, None] > idx[None, :]
    decay = jnp.exp(jnp.where(causal, gc[..., :, None] - gc[..., None, :], -jnp.inf))
    kb = k * beta[..., None]
    A = jnp.einsum('bhnid,bhnjd->bhnij', kb, k) * decay * strict
    eye = jnp.eye(CHUNK, dtype=jnp.float32)
    T = lax.linalg.triangular_solve(eye + A, jnp.broadcast_to(eye, A.shape),
                                    left_side=True, lower=True, unit_diagonal=True)
    u = jnp.einsum('bhnij,bhnjd->bhnid', T, v * beta[..., None])
    w = jnp.einsum('bhnij,bhnjd->bhnid', T, kb * jnp.exp(gc)[..., None])
    qk = jnp.einsum('bhnid,bhnjd->bhnij', q, k) * decay
    q_dec = q * jnp.exp(gc)[..., None]
    g_last = gc[..., -1]
    k_end = k * jnp.exp(g_last[..., None] - gc)[..., None]
    xs = tuple(jnp.moveaxis(t, 2, 0) for t in (u, w, qk, q_dec, k_end, g_last))

    def step(Sst, inp):
        u_n, w_n, qk_n, qd_n, ke_n, gl_n = inp
        v_new = u_n - jnp.einsum('bhid,bhde->bhie', w_n, Sst)
        o = jnp.einsum('bhid,bhde->bhie', qd_n, Sst) + jnp.einsum('bhij,bhje->bhie', qk_n, v_new)
        Sst = Sst * jnp.exp(gl_n)[..., None, None] + jnp.einsum('bhid,bhie->bhde', ke_n, v_new)
        return Sst, o

    S0 = jnp.zeros((B, H, Dk, v.shape[-1]), jnp.float32)
    _, o = lax.scan(step, S0, xs)
    return jnp.transpose(o, (1, 0, 3, 2, 4)).reshape(B, S, H, v.shape[-1])

def first_inputs(seed: int = 0) -> dict:
    key = jax.random.key(seed)
    ks = jax.random.split(key, 24)
    f32 = jnp.float32
    nrm = lambda k, shape, s: jax.random.normal(k, shape, f32) * s
    gain = lambda k, shape: 1.0 + 0.05 * jax.random.normal(k, shape, f32)
    dt = jnp.exp(jax.random.uniform(ks[7], (DEPTH, DN_HEADS), f32, np.log(1e-3), np.log(1e-1)))
    return {
        "x": nrm(ks[0], (BATCH, SEQ, D_MODEL), 1.0),
        "p": nrm(ks[1], (DEPTH, BATCH, SEQ, PLE_DIM), 1.0),
        "g_pre": gain(ks[2], (DEPTH, D_MODEL)),
        "w_in": nrm(ks[3], (DEPTH, D_MODEL, IN_COLS), D_MODEL ** -0.5),
        "b_gate": nrm(ks[4], (DEPTH, N_BRANCHES * D_MODEL), 0.02),
        "w_conv_qkv": nrm(ks[5], (DEPTH, SHORT_CONV, 3 * DN_WIDTH), SHORT_CONV ** -0.5),
        "a_log": jnp.log(jax.random.uniform(ks[6], (DEPTH, DN_HEADS), f32, 1.0, 16.0)),
        "dt_bias": dt + jnp.log(-jnp.expm1(-dt)),
        "g_dn_out": gain(ks[8], (DEPTH, DN_HEAD_DIM)),
        "w_dw": nrm(ks[9], (DEPTH, CONV_KERNEL, CONV_CH), CONV_KERNEL ** -0.5),
        "b_dw": nrm(ks[10], (DEPTH, CONV_CH), 0.02),
        "ln_g": gain(ks[11], (DEPTH, CONV_CH)),
        "ln_b": nrm(ks[12], (DEPTH, CONV_CH), 0.02),
        "w_br_a": nrm(ks[13], (DEPTH, DN_WIDTH, D_MODEL), DN_WIDTH ** -0.5),
        "w_br_b": nrm(ks[14], (DEPTH, CONV_CH, D_MODEL), CONV_CH ** -0.5),
        "w_out": nrm(ks[15], (DEPTH, D_MODEL, D_MODEL), D_MODEL ** -0.5),
        "g_post": gain(ks[16], (DEPTH, D_MODEL)),
        "w_ple_gate": nrm(ks[17], (DEPTH, D_MODEL, D_MODEL), D_MODEL ** -0.5),
        "w_ple_proj": nrm(ks[18], (DEPTH, PLE_DIM, D_MODEL), PLE_DIM ** -0.5),
        "g_ple": gain(ks[19], (DEPTH, D_MODEL)),
    }

def first_block(x, p, g_pre, w_in, b_gate, w_conv_qkv, a_log, dt_bias, g_dn_out, w_dw, b_dw,
              ln_g, ln_b, w_br_a, w_br_b, w_out, g_post, w_ple_gate, w_ple_proj, g_ple):
    B, S, _ = x.shape
    f32 = jnp.float32
    for i in range(DEPTH):
        h = rmsnorm(x, g_pre[i])
        proj = h @ w_in[i]
        qkv, z_a, b_raw, a_raw, glu_in, z_b, gate_logits = jnp.split(proj, _split_points(), axis=-1)

        qkv = jax.nn.silu(causal_depthwise_conv(qkv, w_conv_qkv[i]))
        q, k, v = jnp.split(qkv, 3, axis=-1)
        heads = lambda t: t.reshape(B, S, DN_HEADS, DN_HEAD_DIM).astype(f32)
        q, k, v = l2norm(heads(q)), l2norm(heads(k)), heads(v)
        beta = jax.nn.sigmoid(b_raw.astype(f32))
        g_log = -jnp.exp(a_log[i].astype(f32)) * jax.nn.softplus(a_raw.astype(f32) + dt_bias[i].astype(f32))
        o_a = gated_delta_chunked(q, k, v, g_log, beta)
        o_a = rmsnorm(o_a, g_dn_out[i]).reshape(B, S, DN_WIDTH).astype(x.dtype) * jax.nn.silu(z_a)
        y_a = o_a @ w_br_a[i]

        u = jax.nn.glu(glu_in, axis=-1)
        u = causal_depthwise_conv(u, w_dw[i]) + b_dw[i]
        u = jax.nn.silu(layernorm(u, ln_g[i], ln_b[i])) * jax.nn.silu(z_b)
        y_b = u @ w_br_b[i]

        gate_a, gate_b = jnp.split(jax.nn.sigmoid(gate_logits + b_gate[i]), N_BRANCHES, axis=-1)
        mixed = (gate_a * y_a + gate_b * y_b) @ w_out[i]
        x = x + rmsnorm(mixed, g_post[i])

        e = p[i] @ w_ple_proj[i]
        x = x + rmsnorm(jax.nn.sigmoid(x @ w_ple_gate[i]) * e, g_ple[i])
    return x


DEPTH_2 = 2

N_MEM = 256
N_A_LAYERS = DEPTH_2 // 2
N_B_LAYERS = DEPTH_2 - N_A_LAYERS
HEAD_DIM = 128
MIX_WIDTH = D_MODEL
MEM_HEADS = 4
MEM_WIDTH = MEM_HEADS * HEAD_DIM
BRANCH_WIDTH = MIX_WIDTH - MEM_WIDTH
POOL_WINDOWS = (2, 4, 8, 16)
N_POOL_GROUPS = len(POOL_WINDOWS)
POOL_GROUP = BRANCH_WIDTH // N_POOL_GROUPS
MOBA_HEADS = BRANCH_WIDTH // HEAD_DIM
MOBA_BLOCK = 256
MOBA_TOPK = 3
Q_CHUNK = 64
IN_WIDTH = 2 * BRANCH_WIDTH + 2 * MEM_WIDTH
DEEPNORM_ALPHA = (2 * DEPTH_2) ** 0.25
DEEPNORM_BETA = (8 * DEPTH_2) ** -0.25
LN_EPS = 1e-5


def layer_norm(x, g, b):
    xf = x.astype(jnp.float32)
    mu = xf.mean(-1, keepdims=True)
    var = jnp.square(xf - mu).mean(-1, keepdims=True)
    return ((xf - mu) * lax.rsqrt(var + LN_EPS) * g + b).astype(x.dtype)

def multiscale_pool(u, pool_w, pool_scale):
    B, S, _ = u.shape
    uf = u.astype(jnp.float32)
    cs = jnp.concatenate([jnp.zeros((B, 1, BRANCH_WIDTH), jnp.float32),
                          jnp.cumsum(uf, axis=1)], axis=1)
    t = jnp.arange(S)
    outs = []
    for g, w in enumerate(POOL_WINDOWS):
        sl = slice(g * POOL_GROUP, (g + 1) * POOL_GROUP)
        csg = cs[:, :, sl]
        lo = jnp.maximum(t + 1 - w, 0)
        cnt = (t + 1 - lo).astype(jnp.float32)
        outs.append((csg[:, 1:] - csg[:, lo]) / cnt[None, :, None] - uf[:, :, sl])
    pooled = jnp.stack(outs, axis=2).astype(u.dtype)
    mixed = jnp.einsum('bsgc,gcd->bsgd', pooled, pool_w).reshape(B, S, BRANCH_WIDTH)
    return mixed * pool_scale

def memory_attention(mq, mem, w_mem_kv):
    B, S, _ = mq.shape
    M = mem.shape[1]
    mk, mv = jnp.split(mem @ w_mem_kv, 2, axis=-1)
    q = mq.reshape(B, S, MEM_HEADS, HEAD_DIM)
    k = mk.reshape(B, M, MEM_HEADS, HEAD_DIM)
    v = mv.reshape(B, M, MEM_HEADS, HEAD_DIM)
    s = jnp.einsum('bshd,bmhd->bhsm', q, k).astype(jnp.float32) * (HEAD_DIM ** -0.5)
    p = jax.nn.softmax(s, axis=-1).astype(v.dtype)
    return jnp.einsum('bhsm,bmhd->bshd', p, v).reshape(B, S, MEM_WIDTH)

def moba_shared_kv(h, w_kv):
    B, S, _ = h.shape
    k, v = jnp.split(h @ w_kv, 2, axis=-1)
    nb = -(-S // MOBA_BLOCK)
    pad = nb * MOBA_BLOCK - S
    k = k.reshape(B, S, MOBA_HEADS, HEAD_DIM).transpose(0, 2, 1, 3)
    v = v.reshape(B, S, MOBA_HEADS, HEAD_DIM).transpose(0, 2, 1, 3)
    k = jnp.pad(k, ((0, 0), (0, 0), (0, pad), (0, 0)))
    v = jnp.pad(v, ((0, 0), (0, 0), (0, pad), (0, 0)))
    k_blocks = k.reshape(B, MOBA_HEADS, nb, MOBA_BLOCK, HEAD_DIM)
    v_blocks = v.reshape(B, MOBA_HEADS, nb, MOBA_BLOCK, HEAD_DIM)
    k_mean = k_blocks.astype(jnp.float32).mean(axis=3).astype(k.dtype)
    return k_blocks, v_blocks, k_mean

def moba_attention(q_in, k_blocks, v_blocks, k_mean):
    B, S, _ = q_in.shape
    H = MOBA_HEADS
    nb = k_blocks.shape[2]
    n_sel = min(MOBA_TOPK, nb)
    scale = HEAD_DIM ** -0.5
    q = q_in.reshape(B, S, H, HEAD_DIM).transpose(0, 2, 1, 3)
    b_idx = jnp.arange(B)[:, None, None, None]
    h_idx = jnp.arange(H)[None, :, None, None]
    blk_ids = jnp.arange(nb)
    blk_offs = jnp.arange(MOBA_BLOCK)

    def chunk(c):
        start = c * Q_CHUNK
        qc = lax.dynamic_slice_in_dim(q, start, Q_CHUNK, axis=2)
        own = start // MOBA_BLOCK
        q_pos = start + jnp.arange(Q_CHUNK)
        gate = jnp.einsum('bhqd,bhnd->bhqn', qc, k_mean).astype(jnp.float32)
        gate = jnp.where(blk_ids < own, gate, -jnp.inf)
        _, sel = lax.top_k(gate, n_sel)
        valid = sel < own
        kg = k_blocks[b_idx, h_idx, sel]
        vg = v_blocks[b_idx, h_idx, sel]
        s_sel = jnp.einsum('bhqd,bhqjkd->bhqjk', qc, kg).astype(jnp.float32) * scale
        s_sel = jnp.where(valid[..., None], s_sel, -jnp.inf)
        s_sel = s_sel.reshape(B, H, Q_CHUNK, n_sel * MOBA_BLOCK)
        k_own = lax.dynamic_index_in_dim(k_blocks, own, axis=2, keepdims=False)
        v_own = lax.dynamic_index_in_dim(v_blocks, own, axis=2, keepdims=False)
        s_own = jnp.einsum('bhqd,bhkd->bhqk', qc, k_own).astype(jnp.float32) * scale
        k_pos = own * MOBA_BLOCK + blk_offs
        s_own = jnp.where(k_pos[None, :] <= q_pos[:, None], s_own, -jnp.inf)
        p = jax.nn.softmax(jnp.concatenate([s_sel, s_own], axis=-1), axis=-1).astype(v_blocks.dtype)
        p_sel = p[..., :n_sel * MOBA_BLOCK].reshape(B, H, Q_CHUNK, n_sel, MOBA_BLOCK)
        p_own = p[..., n_sel * MOBA_BLOCK:]
        return (jnp.einsum('bhqjk,bhqjkd->bhqd', p_sel, vg)
                + jnp.einsum('bhqk,bhkd->bhqd', p_own, v_own))

    out = lax.map(chunk, jnp.arange(S // Q_CHUNK))
    return out.transpose(1, 0, 3, 2, 4).reshape(B, S, H * HEAD_DIM)

def second_inputs(seed: int = 0) -> dict:
    key = jax.random.key(seed)
    ks = jax.random.split(key, 10)
    f32 = jnp.float32
    nrm = jax.random.normal
    x = nrm(ks[0], (BATCH, SEQ, D_MODEL), f32)
    mem = nrm(ks[1], (BATCH, N_MEM, D_MODEL), f32)
    w_in = nrm(ks[2], (DEPTH_2, D_MODEL, IN_WIDTH), f32) * D_MODEL ** -0.5
    w_out = nrm(ks[3], (DEPTH_2, MIX_WIDTH, D_MODEL), f32) * (MIX_WIDTH ** -0.5 * DEEPNORM_BETA)
    w_mem_kv = nrm(ks[4], (DEPTH_2, D_MODEL, 2 * MEM_WIDTH), f32) * D_MODEL ** -0.5
    ln_g = 1.0 + 0.02 * nrm(ks[5], (DEPTH_2, D_MODEL), f32)
    ln_b = 0.02 * nrm(ks[6], (DEPTH_2, D_MODEL), f32)
    pool_w = nrm(ks[7], (N_A_LAYERS, N_POOL_GROUPS, POOL_GROUP, POOL_GROUP), f32) * POOL_GROUP ** -0.5
    pool_scale = 1.0 + 0.02 * nrm(ks[8], (N_A_LAYERS, BRANCH_WIDTH), f32)
    w_kv_shared = nrm(ks[9], (D_MODEL, 2 * BRANCH_WIDTH), f32) * D_MODEL ** -0.5
    return {"x": x, "mem": mem, "w_in": w_in, "w_out": w_out, "w_mem_kv": w_mem_kv,
            "ln_g": ln_g, "ln_b": ln_b, "pool_w": pool_w, "pool_scale": pool_scale,
            "w_kv_shared": w_kv_shared}

def second_block(x, mem, w_in, w_out, w_mem_kv, ln_g, ln_b, pool_w, pool_scale, w_kv_shared):
    h = x
    split_at = [BRANCH_WIDTH, 2 * BRANCH_WIDTH, 2 * BRANCH_WIDTH + MEM_WIDTH]
    for i in range(DEPTH_2):
        if i == N_A_LAYERS:
            k_blocks, v_blocks, k_mean = moba_shared_kv(h, w_kv_shared)
        u = h @ w_in[i]
        branch_in, gate_b, mem_q, gate_m = jnp.split(u, split_at, axis=-1)
        if i < N_A_LAYERS:
            branch = multiscale_pool(branch_in, pool_w[i], pool_scale[i])
        else:
            branch = moba_attention(branch_in, k_blocks, v_blocks, k_mean)
        mem_o = memory_attention(mem_q, mem, w_mem_kv[i])
        mixed = jnp.concatenate([branch * jax.nn.silu(gate_b), mem_o * jax.nn.silu(gate_m)], axis=-1)
        y = mixed @ w_out[i]
        h = layer_norm(DEEPNORM_ALPHA * h + y, ln_g[i], ln_b[i])
    return h


def setup_inputs(seed=0):
    out = dict(first_inputs(seed))
    for name, value in second_inputs(seed + 1).items():
        if name != "x":
            out[name + "_2"] = value
    return out


def reference(
    x, p, g_pre, w_in, b_gate, w_conv_qkv, a_log, dt_bias, g_dn_out, w_dw, b_dw, ln_g, ln_b,
    w_br_a, w_br_b, w_out, g_post, w_ple_gate, w_ple_proj, g_ple, mem_2, w_in_2, w_out_2,
    w_mem_kv_2, ln_g_2, ln_b_2, pool_w_2, pool_scale_2, w_kv_shared_2,
):
    x = first_block(
        x, p, g_pre, w_in, b_gate, w_conv_qkv, a_log, dt_bias, g_dn_out, w_dw, b_dw, ln_g, ln_b,
        w_br_a, w_br_b, w_out, g_post, w_ple_gate, w_ple_proj, g_ple,
    )
    return second_block(
        x, mem_2, w_in_2, w_out_2, w_mem_kv_2, ln_g_2, ln_b_2, pool_w_2, pool_scale_2,
        w_kv_shared_2,
    )


_drawn_inputs = setup_inputs


def setup_inputs(seed=0):
    import zlib

    import numpy as np

    out = dict(_drawn_inputs(seed))
    spreads = {}
    factors = {'b_gate': 8.0,
     'b_dw': 3.751,
     'ln_g': 2.9,
     'ln_b': 8.0,
     'pool_scale_2': 23.804,
     'g_dn_out': 2.844,
     'mem_2': 3.883,
     'w_mem_kv_2': 3.765}
    for name, (base, spread) in spreads.items():
        noise = np.random.default_rng([zlib.crc32(name.encode()), seed]).standard_normal(out[name].shape)
        drawn = base * np.exp(spread * noise) if base else spread * noise
        out[name] = __import__('jax').numpy.asarray(drawn.astype(out[name].dtype))
    for name, factor in factors.items():
        out[name] = (out[name] * factor).astype(out[name].dtype)
    return out
```

```python
from contextlib import ExitStack

import numpy as np

import concourse.bass as bass
from concourse import mybir

F32 = mybir.dt.float32
F32R = mybir.dt.float32r
ALU = mybir.AluOpType
ACT = mybir.ActivationFunctionType
AX = mybir.AxisListType

P = 128
D = 2048
S = 256
TT = S // P
KC = D // P
NB = 512
UNITS = 4
UK = KC // UNITS
AHEAD = 6
HEADS = 16
LEVELS = 7
SHORT, LONG = 4, 31
EPS, LN_EPS = 1e-6, 1e-5
RSQ = float(P) ** -0.5
POOL_WINDOWS = (2, 4, 8, 16)
PG = 384
MEM_HEADS = 4
MOBA_HEADS = 12
ALPHA = 4.0 ** 0.25

COL_A, COL_BA, COL_B = 0, 4 * D, 4 * D + 2 * HEADS
COL_GATE_B = COL_B + 4 * D

BLK_A = 0
BLK_B = BLK_A + HEADS
BLK_GB = BLK_B + KC
BLK_Y = BLK_GB + 4
BLK_MEM0 = BLK_Y + 8
BLK_OUT = BLK_MEM0 + 2
BLK_MEM1 = BLK_OUT + 4
BLK_PLE = BLK_MEM1 + 2
BLK_IN0 = BLK_PLE + 4
BLK_OUT0 = BLK_IN0 + 8
BLK_KV = BLK_OUT0 + 4
BLK_IN1 = BLK_KV + 6
BLK_OUT1 = BLK_IN1 + 8
BLK_END = BLK_OUT1 + 4

IN_ORDER = (0, 1, 2, 6, 3, 4, 5, 7)

CH_GPRE, CH_LNG, CH_LNB, CH_BDW = 0, 16, 32, 48
CH_SHORT = 64
CH_LONG = CH_SHORT + SHORT * 3 * HEADS
CH_END = CH_LONG + LONG * KC
ROW_TILES = [(CH_GPRE, 64), (CH_SHORT, 96), (CH_SHORT + 96, 96)] + [(CH_LONG + 124 * i, 124) for i in range(4)]

K_ID, K_TRI, K_ONE, K_LVL = 0, P, 2 * P, 3 * P
K_LVL0T = K_LVL + LEVELS * P
K_END = K_LVL0T + P


def shape_constants():
    i = np.arange(P)
    levels = []
    for m in [1 << n for n in range(LEVELS)]:
        same = (i[:, None] // (2 * m)) == (i[None, :] // (2 * m))
        levels.append(-(same & ((i[:, None] // m) % 2 == 1) & ((i[None, :] // m) % 2 == 0)).astype(np.float32))
    parts = [np.eye(P), i[:, None] <= i[None, :], np.ones((P, P)), *levels, levels[0].T]
    return np.ascontiguousarray(np.concatenate([np.asarray(x, np.float32) for x in parts], axis=1))


def pool_bands():
    s = np.arange(S)
    out = np.zeros((S, len(POOL_WINDOWS), S), np.float32)
    for g, w in enumerate(POOL_WINDOWS):
        lo = np.maximum(s + 1 - w, 0)
        inside = (s[:, None] >= lo[None, :]) & (s[:, None] <= s[None, :])
        out[:, g, :] = inside / (s + 1 - lo)[None, :].astype(np.float32) - np.eye(S, dtype=np.float32)
    return out


def causal_mask():
    i = np.arange(S)
    return np.where(i[None, :] <= i[:, None], 0.0, -1e30).astype(np.float32)


def program(nc, t, out, ctx):
    w_in = t["w_in"][0].rearrange("(k p) n -> p k n", p=P)
    square = {n: t[n][0].rearrange("(k p) n -> p k n", p=P) for n in ("w_br_a", "w_br_b", "w_out", "w_ple_gate")}
    w_in2 = [t["w_in_2"][i].rearrange("(k p) n -> p k n", p=P) for i in range(2)]
    w_out2 = [t["w_out_2"][i].rearrange("(k p) n -> p k n", p=P) for i in range(2)]
    w_mem = [t["w_mem_kv_2"][i].rearrange("(k p) n -> p k n", p=P) for i in range(2)]
    w_kv = t["w_kv_shared_2"].rearrange("(k p) n -> p k n", p=P)
    tokens = lambda a: a.rearrange("(t p) n -> p t n", p=P)

    gc_rows = nc.dram_tensor("gc_rows", (TT * HEADS, P), F32, kind="Internal").ap()
    gate_a_dram = nc.dram_tensor("gate_a_tanh", (S, D), F32, kind="Internal").ap()

    kib = 1024
    spot = [17 * kib]

    def sb(name, shape, dt=F32):
        h = nc.alloc_sbuf_tensor_at(name, shape, dt, offset=spot[0])
        spot[0] += (4 * int(np.prod(shape[1:])) + 31) // 32 * 32
        assert spot[0] <= nc.sbuf_usable_end
        return h

    def region(size):
        at = spot[0]
        spot[0] += size
        return at

    raw = sb("raw", [P, UNITS, UK, NB])
    w_hi = sb("w_hi", [P, 2, UK, NB], F32R)
    w_lo = sb("w_lo", [P, 2, UK, NB], F32R)
    in_hi = sb("in_hi", [P, KC, S], F32R)
    in_lo = sb("in_lo", [P, KC, S], F32R)
    at_a = spot[0]
    oa_hi = sb("oa_hi", [P, KC, S], F32R)
    oa_lo = sb("oa_lo", [P, KC, S], F32R)
    at_b = spot[0]
    ub_hi = sb("ub_hi", [P, KC, S], F32R)
    ub_lo = sb("ub_lo", [P, KC, S], F32R)
    const = sb("const", [P, K_END])
    chan = sb("chan", [P, CH_END])
    head_all = sb("head_all", [P, HEADS, 12])
    half_g = sb("half_g", [P, P])
    small = sb("small", [P, 64])
    eps_col = sb("eps_col", [P, 1])
    halfpow = sb("halfpow", [P, 8])
    pool_eps = sb("pool_eps", [P, 8])
    at_g = spot[0]

    spot[0] = at_a
    x_tok = sb("x_tok", [P, TT, D])
    hs_tok = sb("hs_tok", [P, TT, D])
    spot[0] = at_b
    rows = sb("rows", [P, len(ROW_TILES), P])
    ba_raw = sb("ba_raw", [P, KC, 2 * HEADS])
    ba_hi = sb("ba_hi", [P, KC, 2 * HEADS], F32R)
    ba_lo = sb("ba_lo", [P, KC, 2 * HEADS], F32R)
    sgl = sb("sgl", [P, 16, 32])
    dt_b = sb("dt_b", [P, HEADS])
    alog_b = sb("alog_b", [P, HEADS])
    gcT = sb("gcT", [TT * HEADS, P])

    spot[0] = at_b
    gc_b = sb("gc_b", [P, TT * HEADS, P])
    proj = sb("proj", [P, TT, NB])
    conv_in = sb("conv_in", [P, 3, SHORT - 1 + S + 1])
    conv = sb("conv", [P, 3, S])
    conv_th = sb("conv_th", [P, 3, S])
    dexp = sb("dexp", [P, TT, P])
    spot[0] = at_g
    tok = sb("tok", [P, TT, 3, P])
    scaled = sb("scaled", [P, TT, 3, P])
    z_th = sb("z_th", [P, TT, P])
    z2 = sb("z2", [P, TT, P])
    at_kq = spot[0]
    kq = sb("kq", [P, 2, TT, 3, P])
    at_ap = spot[0]
    ap = sb("ap", [P, 2, TT, 2, P])
    vb = sb("vb", [P, 2, TT, P])
    kend = sb("kend", [P, 2, P])
    zs = sb("zs", [P, 2, TT, P])
    tri = sb("tri", [P, 2 * TT, P])
    xm = sb("xm", [P, TT, P])
    xmT = sb("xmT", [P, TT, P])
    vn0, s1, r1, vn1, oq = (sb(n, [P, P]) for n in ("vn0", "s1", "r1", "vn1", "oq"))
    o_t = sb("o_t", [P, TT, P])
    og = sb("og", [P, TT, P])
    junk = sb("junk", [P, P])
    cw = sb("cw", [P, SHORT, 3])
    hst = sb("hst", [P, 2, 12])
    ssq = sb("ssq", [P, 2 * TT])
    rn = sb("rn", [P, 2 * TT])
    scal = sb("scal", [P, 12])
    oss = sb("oss", [P, TT])
    orn = sb("orn", [P, TT])

    at_free = spot[0]

    spot[0] = at_b
    zb = sb("zb", [P, KC, S])
    ub = sb("ub", [P, KC, S])
    spot[0] = at_g
    bproj = sb("bproj", [P, TT, NB])
    upad = sb("upad", [P, 2, LONG - 1 + S + 2])
    z2b = sb("z2b", [P, TT, P])
    bg = sb("bg", [P, P])
    cwl = sb("cwl", [P, LONG + 1])
    assert spot[0] <= at_kq
    spot[0] = at_kq
    acc = sb("acc", [P, 2, S])
    glu2 = sb("glu2", [P, TT, P])
    assert spot[0] <= at_kq + 4 * TT * 3 * P
    spot[0] = at_ap
    tap = sb("tap", [P, 2, S])
    assert spot[0] <= at_ap + 4 * TT * 2 * P
    spot[0] = at_free
    bth = sb("bth", [P, TT, 3, P])
    acc_p = sb("acc_p", [P, S])
    assert spot[0] <= nc.sbuf_usable_end

    spot[0] = at_a
    mem_hi = sb("mem_hi", [P, KC, S], F32R)
    mem_lo = sb("mem_lo", [P, KC, S], F32R)
    spot[0] = at_a
    u0 = sb("u0", [P, TT, 3 * NB])
    pooled = sb("pooled", [P, 12, S])
    mqT0 = sb("mqT0", [P, MEM_HEADS, S])
    pscale = sb("pscale", [P, 2, PG])
    spot[0] = at_a
    kT1 = sb("kT1", [P, MOBA_HEADS, S])
    v1_ = sb("v1_", [P, TT, 3 * NB])
    mqT1 = sb("mqT1", [P, MEM_HEADS, S])
    stage1 = sb("stage1", [P, TT, NB])
    assert spot[0] <= at_b
    spot[0] = at_a
    ln_b0 = sb("ln_b0", [P, D])
    spot[0] = at_a
    ln_vec_a = sb("ln_vec_a", [P, 2, D])
    spot[0] = at_b
    mo = sb("mo", [P, TT, D])
    xr = sb("xr", [P, TT, D])
    spot[0] = at_g
    gb = sb("gb", [P, TT, D])
    spot[0] = at_g
    mkT = sb("mkT", [P, 2, MEM_HEADS, S])
    mv = sb("mv", [P, 2, TT, NB])
    at_v = spot[0]
    vec = sb("vec", [P, D])
    spot[0] = at_v
    mem_tok = sb("mem_tok", [P, 2, TT, NB])
    spot[0] = at_v
    bands = sb("bands", [P, TT, len(POOL_WINDOWS), S])
    at_s = spot[0]
    spot[0] = at_v
    qT1 = sb("qT1", [P, MOBA_HEADS, S])
    mask = sb("mask", [P, TT, S])
    spot[0] = at_s
    sqb = sb("sqb", [P, 2, 4, S])
    mub = sb("mub", [P, S])
    rsb = sb("rsb", [P, S])
    spot[0] = at_s
    gat = sb("gat", [P, 2, TT, NB])
    mix = sb("mix", [P, TT, NB])
    spot[0] = at_s
    stage0 = sb("stage0", [P, TT, NB])
    wpp = sb("wpp", [P, 2, NB])
    pT = sb("pT", [P, 2, S])
    p_tok = sb("p_tok", [P, TT, S])
    spot[0] -= 4 * TT * S
    junk2 = sb("junk2", [P, NB])
    spot[0] = at_s + 4096
    pool_w = sb("pool_w", [P, 3, PG])
    sc = sb("sc", [P, TT, S])
    probT = sb("probT", [P, TT, S])
    st = sb("st", [P, 96])
    sgst = st[:, 0:TT * 4 * 6]
    assert spot[0] <= nc.sbuf_usable_end

    pairs = [nc.alloc_psum_tensor(f"pair{i}", [P, TT, NB], F32) for i in range(2)]
    QA, QB, RA, RB = (nc.alloc_psum_tensor(n, [P, NB], F32) for n in ("QA", "QB", "RA", "RB"))

    ident, triu = const[:, K_ID:K_ID + P], const[:, K_TRI:K_TRI + P]
    ones = const[:, K_ONE:K_ONE + P]
    level = lambda l: const[:, K_LVL + l * P:K_LVL + (l + 1) * P]
    level0T = const[:, K_LVL0T:K_LVL0T + P]

    def both(x):
        return x.unsqueeze(1).broadcast_to([P, TT, P])

    sem = nc.alloc_semaphore
    w_loaded = [sem(f"w_loaded{u}") for u in range(UNITS)]
    hi_ready = [sem(f"hi_ready{u}") for u in range(UNITS)]
    lo_ready = [sem(f"lo_ready{u}") for u in range(UNITS)]
    chunk_used = sem("chunk_used")
    psum_ready, psum_free = sem("psum_ready"), sem("psum_free")
    names = ("rows_in", "x_in", "ba_in", "rows_cols", "chan_ready", "x_ss", "x_rms", "x_scaled",
             "ba_split", "ba_lo_ready", "ba_done", "ba_out", "sg_v", "sg_a", "sg_exp", "sg_g", "gc_done", "gc_copied",
             "gcT_done", "gc_stored", "head_ready", "turned", "turned_hi", "turned_lo",
             "pads_ready", "zs_ready", 
             "z_tanh", "z_gated", "qkv_cols", "conv_filled", "cw_staged", "head_staged", "conv_tanh", "silu_done",
             "qkv_tokens", "tok_ready", "norms_summed", "pool_a", "scal_ready", "tok_scaled", "kq_cols", "kq_ready",
             "decay_diff", "decay_exp", "decay_ready", "kk_done", "ap_ready",
             "a_turned", "t_first", "v0_done", "v0_ready", "s1_done", "s1_ready", "kq_s1", "r1_ready", "oq_ready",
             "v1_done", "v1_ready", "o_done", "o_ready", "o_summed", "pool_b", "xT_ready", "og_ready", "og_cols", "oa_hi_done",
             "oa_lo_done",
             "bg_loaded", "gate_biased", "b_tanh", "glu_ready", "gate_a_stored", "b_cols", "b_cols_taken", "cwl_staged",
             "pool_taps", "u_summed", "u_ready", )
    s = {n: sem(n) for n in names}
    tap_done, x_done, x_ready, d_done, t_ready = (sem(n) for n in ("tap_done", "x_done", "x_ready", "d_done", "t_ready"))
    for n in ("gb_tanh", "mean_ready", "centred", "squared", "var_done", 
              "rstd_ready", "ln_scaled", "ln_affine", "ln_tanh", "ln_silu", "ln_gated", "ub_hi_done", "ub_lo_done",
              "gat_loaded0", "gat_loaded1", "mix_ready", "mem_loaded0", "mem_loaded1", "vec_loaded", "heads_done",
              "heads_taken", "mo_summed", "mo_scaled", "ms_ready", "ms_rms", "x_added",
              "pT_ready", "wpp_loaded", "e_done", "pr_ready", 
              "pool_done", "pool_ready", "pw_loaded", "pw_ready",
              "scores_done", "scores_masked", "max_ready", "probs_ready", "sums_inverted", "probs_turned",
              "probT_ready", "attended", "att_ready", "gate_tanh", "mixed_ready", "stats_ready",
              "aggr_ready", "ln_pool", "ln_normed", "ln_gain", "ln_done", "out_stored", ):
        s[n] = sem(n)
    long_tap = [sem(f"long_tap{i}") for i in range(2)]
    tap_ready = [sem(f"tap_ready{i}") for i in range(2)]

    def reach(eng, which, value):
        if not isinstance(value, int) or value > 0:
            eng.wait_ge(which, value)

    def load_unit(sp, blk, u, src):
        reach(sp, lo_ready[u], UK * blk)
        sp.dma_start(raw[:, u], src).then_inc(w_loaded[u], 16)

    def load_heads(sp, blk, base, h):
        for u in range(UNITS):
            reach(sp, lo_ready[u], UK * blk)
            for g in range(4):
                sp.dma_start(raw[:, u, :, g * P:(g + 1) * P],
                             w_in[:, u * UK:(u + 1) * UK, bass.ds(base + g * D + h * P, P)]).then_inc(w_loaded[u], 16)

    def load_block(sp, blk, w, col):
        for u in range(UNITS):
            load_unit(sp, blk, u, w[:, u * UK:(u + 1) * UK, bass.ds(col, NB)])

    def loads(blk):
        if isinstance(blk, int) and blk >= BLK_GB:
            return 64 * BLK_GB + 16 * (blk + 1 - BLK_GB)
        return 64 * blk + 64

    def hi_piece(act, blk, q):
        u = q // UK
        if q % UK == 0:
            act.wait_ge(w_loaded[u], loads(blk))
        if q == 2 * UK - 1:
            reach(act, psum_ready, blk)
        elif q < 2 * UK:
            reach(act, chunk_used, (KC - 1) * blk - (2 * UK - 2 - q))
        else:
            reach(act, chunk_used, (KC - 1) * blk + q - 2 * UK + 1)
        act.activation(w_hi[:, u % 2, q % UK], raw[:, u, q % UK], ACT.Copy).then_inc(hi_ready[u], 1)

    def lo_piece(dve, blk, q):
        u = q // UK
        dve.wait_ge(hi_ready[u], UK * blk + q % UK + 1)
        dve.tensor_tensor(w_lo[:, u % 2, q % UK], raw[:, u, q % UK], w_hi[:, u % 2, q % UK].bitcast(F32), ALU.subtract)\
           .then_inc(lo_ready[u], 1)

    def ahead(blk, q, step):
        if q + AHEAD < KC:
            return blk, q + AHEAD
        return blk + 1, q + AHEAD - KC

    def pe_block(pe, blk, parity, hi, lo, between=None):
        for q in range(KC):
            u = q // UK
            if q == 0:
                reach(pe, psum_free, blk - 1)
            pe.wait_ge(lo_ready[u], UK * blk + q % UK + 1)
            for tile in range(TT):
                o = pairs[parity][:, tile]
                xh, xl = hi[:, q, tile * P:(tile + 1) * P], lo[:, q, tile * P:(tile + 1) * P]
                wh, wl = w_hi[:, u % 2, q % UK], w_lo[:, u % 2, q % UK]
                pe.matmul(o, xh, wh, start=(q == 0), stop=False)
                pe.matmul(o, xh, wl, start=False, stop=False)
                mm = pe.matmul(o, xl, wh, start=False, stop=(q == KC - 1))
                if tile == TT - 1 and q == KC - 1:
                    mm.then_inc(psum_ready, 1)
                elif tile == TT - 1:
                    mm.then_inc(chunk_used, 1)
                if between:
                    between(2 * q + tile)

    def act_block(act, blk, between=None):
        for q in range(KC):
            b, p = ahead(blk, q, 1)
            if not isinstance(b, int) or b < BLK_END:
                hi_piece(act, b, p)
            if between:
                between(2 * q)
                between(2 * q + 1)

    def dve_block(dve, blk, between=None):
        for q in range(KC):
            if between:
                between(2 * q)
                between(2 * q + 1)
            b, p = ahead(blk, q, 1)
            if not isinstance(b, int) or b < BLK_END:
                lo_piece(dve, b, p)

    def keys_pe(pe, h, par, hs):
        if hs == 3:
            pe.wait_ge(psum_free, BLK_A + h + 1)
            reach(pe, s["ap_ready"], h)
            for c in range(3):
                bank = QB[:, 0:S] if c == 2 else QA[:, c * S:(c + 1) * S]
                for tile in range(TT):
                    mm = pe.transpose(bank[:, tile * P:(tile + 1) * P], proj[:, tile, c * P:(c + 1) * P], ident)
            mm.then_inc(s["qkv_cols"], 1)
        if hs == 15:
            pe.wait_ge(s["silu_done"], h + 1)
            for tile in range(TT):
                for c in range(3):
                    mm = pe.transpose((QA, QB)[tile][:, c * P:(c + 1) * P], conv[:, c, tile * P:(tile + 1) * P], ident)
            mm.then_inc(s["qkv_tokens"], 1)
        if hs == 25:
            pe.wait_ge(s["tok_scaled"], h + 1)
            for tile in range(TT):
                for c in range(3):
                    mm = pe.transpose((QA, QB)[tile][:, c * P:(c + 1) * P], scaled[:, tile, c], ident)
            mm.then_inc(s["kq_cols"], 1)
        if hs == 28:
            pe.wait_ge(s["kq_ready"], h + 1)
            for tile in range(TT):
                mm = pe.matmul(QA[:, tile * S:(tile + 1) * S], kq[:, par, tile, 2],
                               kq[:, par, tile, 0:2].rearrange("p c n -> p (c n)"), start=True, stop=True)
            mm.then_inc(s["kk_done"], 1)

    def keys_act(act, h, par, hs):
        if hs == 0:
            act.wait_ge(psum_ready, h + 1 + BLK_A)
            reach(act, s["qkv_cols"], h)
            reach(act, s["z_gated"], h)
            act.activation(proj[:, 0], pairs[par][:, 0], ACT.Copy)
            act.activation(proj[:, 1], pairs[par][:, 1], ACT.Copy).then_inc(psum_free, 1)
        if hs == 1:
            act.wait_ge(psum_free, BLK_A + h + 1)
            act.activation(z_th[:, :, :], proj[:, :, 3 * P:4 * P], ACT.Tanh, scale=0.5).then_inc(s["z_tanh"], 1)
        if hs == 12:
            act.wait_ge(tap_done, SHORT * h + SHORT)
            act.activation(conv_th[:, :, :], conv[:, :, :], ACT.Tanh, scale=0.5).then_inc(s["conv_tanh"], 1)
        if hs == 15:
            act.wait_ge(s["qkv_tokens"], h + 1)
            act.activation(tok[:, 0].rearrange("p c n -> p (c n)"), QA[:, 0:3 * P], ACT.Copy)
            act.activation(tok[:, 1].rearrange("p c n -> p (c n)"), QB[:, 0:3 * P], ACT.Copy)\
               .then_inc(s["tok_ready"], 1)
        if hs == 16:
            act.wait_ge(s["tok_ready"], h + 1)
            reach(act, s["scal_ready"], h)
            for tile in range(TT):
                for c in range(2):
                    reach(act, s["norms_summed"], 4 * h + 2 * tile + c)
                    act.activation(junk[:, :], tok[:, tile, c], ACT.Square,
                                   accum_out=ssq[:, 2 * tile + c:2 * tile + c + 1]).then_inc(s["norms_summed"], 1)
        if hs == 25:
            act.wait_ge(s["kq_cols"], h + 1)
            for tile in range(TT):
                ins = act.activation(kq[:, par, tile].rearrange("p c n -> p (c n)"), (QA, QB)[tile][:, 0:3 * P], ACT.Copy)
            ins.then_inc(s["kq_ready"], 1)
        if hs == 4:
            act.wait_ge(s["decay_diff"], h + 1)
            act.activation(dexp[:, :, :], dexp[:, :, :], ACT.Exp).then_inc(s["decay_exp"], 1)

    def keys_pool(pool, h, par):
        reach(pool, s["og_ready"], h - 1)
        reach(pool, s["ap_ready"], h - 1)
        reach(pool, tap_done, SHORT * h)
        pool.tensor_copy(hst[:, par], head_all[:, bass.ds(h, 1)].rearrange("p a n -> p (a n)"))\
            .then_inc(s["head_staged"], 1)
        taps = chan[:, CH_SHORT:CH_LONG].rearrange("p (k c h) -> p k c h", k=SHORT, c=3)
        pool.tensor_copy(cw[:, :, :], taps[:, :, :, bass.ds(h, 1)].rearrange("p k c a -> p k (c a)"))\
            .then_inc(s["cw_staged"], 1)
        pool.wait_ge(s["norms_summed"], 4 * h + 4)
        reach(pool, s["tok_scaled"], h)
        pool.tensor_tensor(rn[:, :], ssq[:, :], pool_eps[:, 0:4], ALU.add).then_inc(s["pool_a"], 1)
        pool.wait_ge(s["pool_a"], 2 * h + 1)
        pool.tensor_tensor(rn[:, :], rn[:, :], halfpow[:, 0:4], ALU.pow).then_inc(s["pool_a"], 1)
        pool.wait_ge(s["head_staged"], h + 1)
        pool.wait_ge(s["pool_a"], 2 * h + 2)
        r = rn[:, :].rearrange("p (t c) -> p c t", t=TT)
        pool.tensor_tensor(scal[:, 2:4], r[:, 1], hst[:, par, 0:2], ALU.mult)
        pool.tensor_tensor(scal[:, 4:6], r[:, 1], hst[:, par, 10:12], ALU.mult)
        pool.tensor_scalar(scal[:, 0:2], r[:, 0], RSQ, None, ALU.mult)
        pool.tensor_copy(scal[:, 6:8], r[:, 1]).then_inc(s["scal_ready"], 1)

    def keys_dve(dve, h, par, hs):
        if hs == 2:
            dve.wait_ge(s["z_tanh"], h + 1)
            dve.scalar_tensor_tensor(z2[:, :, :], z_th[:, :, :], 1.0, proj[:, :, 3 * P:4 * P], ALU.add, ALU.mult)\
               .then_inc(s["z_gated"], 1)
        if hs == 3:
            dve.wait_ge(s["head_staged"], h + 1)
            reach(dve, s["decay_ready"], h)
            for tile in range(TT):
                ins = dve.tensor_scalar(dexp[:, tile], gc_b[:, bass.ds(tile * HEADS + h, 1)].rearrange("p a n -> p (a n)"),
                                        hst[:, par, 4 + tile:5 + tile], 0.0, ALU.subtract, ALU.min)
            ins.then_inc(s["decay_diff"], 1)
        if hs == 4:
            dve.wait_ge(s["qkv_cols"], h + 1)
            dve.tensor_copy(conv_in[:, 0:2, SHORT - 1:SHORT - 1 + S], QA[:, :].rearrange("p (c n) -> p c n", c=2))
            dve.tensor_copy(conv_in[:, 2, SHORT - 1:SHORT - 1 + S], QB[:, 0:S]).then_inc(s["conv_filled"], 1)
        if hs in (5, 7, 9, 11):
            k = (hs - 5) // 2
            if k == 0:
                dve.wait_ge(s["conv_filled"], h + 1)
                dve.wait_ge(s["cw_staged"], h + 1)
                reach(dve, s["qkv_tokens"], h)
            else:
                dve.wait_ge(tap_done, SHORT * h + k)
            for c in range(3):
                src = conv_in[:, c, k:k + S]
                if k == 0:
                    ins = dve.tensor_scalar(conv[:, c], src, cw[:, k, c:c + 1], None, ALU.mult)
                else:
                    ins = dve.scalar_tensor_tensor(conv[:, c], src, cw[:, k, c:c + 1], conv[:, c], ALU.mult, ALU.add)
            ins.then_inc(tap_done, 1)
        if hs == 8:
            dve.wait_ge(s["decay_exp"], h + 1)
            dve.tensor_tensor(dexp[:, :, :], dexp[:, :, :], both(triu), ALU.mult).then_inc(s["decay_ready"], 1)
        if hs == 10:
            dve.wait_ge(s["z_gated"], h + 1)
            reach(dve, s["og_ready"], h - 1)
            dve.tensor_tensor(zs[:, par], z2[:, :, :], both(half_g[:, :]), ALU.mult).then_inc(s["zs_ready"], 1)
        if hs == 12:
            dve.wait_ge(s["conv_tanh"], h + 1)
            dve.scalar_tensor_tensor(conv[:, :, :], conv_th[:, :, :], 1.0, conv[:, :, :], ALU.add, ALU.mult)\
               .then_inc(s["silu_done"], 1)
        if hs == 22:
            dve.wait_ge(s["tok_ready"], h + 1)
            dve.wait_ge(s["scal_ready"], h + 1)
            reach(dve, s["kq_cols"], h)
            for tile in range(TT):
                for c, part, at in ((0, 1, 2), (1, 0, 0), (2, 1, 6)):
                    dve.tensor_scalar(scaled[:, tile, c], tok[:, tile, part], scal[:, at + tile:at + tile + 1], None, ALU.mult)
                dve.tensor_scalar(vb[:, par, tile], tok[:, tile, 2], hst[:, par, 2 + tile:3 + tile], None, ALU.mult)
            dve.tensor_scalar(kend[:, par], tok[:, 0, 1], scal[:, 4:5], None, ALU.mult).then_inc(s["tok_scaled"], 1)
        if hs == 28:
            dve.wait_ge(s["kk_done"], h + 1)
            dve.wait_ge(s["decay_ready"], h + 1)
            dve.tensor_tensor(ap[:, par].rearrange("p t c n -> p c t n"),
                              QA[:, :].rearrange("p (t c n) -> p c t n", t=TT, c=2),
                              dexp[:, :, :].unsqueeze(1).broadcast_to([P, 2, TT, P]), ALU.mult).then_inc(s["ap_ready"], 1)

    X_AT = {2: 1, 5: 2, 7: 3, 10: 4, 12: 5, 15: 6}
    T_AT = {3: 1, 6: 2, 8: 3, 11: 4, 13: 5, 16: 6}

    def every(h, l):
        return LEVELS * h + l + 1

    def inner(h, l):
        return (LEVELS - 1) * h + l

    def rule_pe(pe, h, par, hs):
        if hs == 0:
            pe.wait_ge(s["ap_ready"], h + 1)
            reach(pe, s["oa_lo_done"], h)
            for tile in range(TT):
                mm = pe.transpose(RA[:, tile * P:(tile + 1) * P], ap[:, par, tile, 0], ident)
            mm.then_inc(s["a_turned"], 1)
        if hs in X_AT:
            l = X_AT[hs]
            pe.wait_ge(t_ready, every(h, l - 1))
            for tile in range(TT):
                mm = pe.matmul(RA[:, tile * P:(tile + 1) * P], ap[:, par, tile, 0], tri[:, tile], start=True, stop=True)
            mm.then_inc(x_done, 1)
        if hs in T_AT:
            l = T_AT[hs]
            pe.wait_ge(x_ready, every(h, l))
            for tile in range(TT):
                if l < LEVELS - 1:
                    pe.matmul(RB[:, tile * P:(tile + 1) * P], tri[:, TT + tile], xm[:, tile], start=True, stop=True)
                mm = pe.matmul(RB[:, (TT + tile) * P:(TT + tile + 1) * P], xm[:, tile], tri[:, TT + tile], start=True, stop=True)
            mm.then_inc(d_done, 1)
        if hs == 18:
            pe.wait_ge(t_ready, every(h, LEVELS - 1))
            pe.matmul(RA[:, 0:P], tri[:, TT], vb[:, par, 0], start=True, stop=True).then_inc(s["v0_done"], 1)
        if hs == 20:
            pe.wait_ge(s["v0_ready"], h + 1)
            pe.matmul(RA[:, P:2 * P], kend[:, par], vn0[:, :], start=True, stop=True).then_inc(s["s1_done"], 1)
            pe.matmul(RB[:, 0:P], ap[:, par, 0, 1], vn0[:, :], start=True, stop=True)
        if hs == 21:
            pe.wait_ge(s["s1_ready"], h + 1)
            pe.matmul(RB[:, P:2 * P], kq[:, par, 1, 1], s1[:, :], start=True, stop=True)
            pe.matmul(RA[:, 0:P], kq[:, par, 1, 0], s1[:, :], start=True, stop=True).then_inc(s["kq_s1"], 1)
        if hs == 23:
            pe.wait_ge(s["r1_ready"], h + 1)
            pe.matmul(RA[:, P:2 * P], tri[:, TT + 1], r1[:, :], start=True, stop=True).then_inc(s["v1_done"], 1)
        if hs == 24:
            pe.wait_ge(s["v1_ready"], h + 1)
            pe.wait_ge(s["oq_ready"], h + 1)
            pe.matmul(RB[:, 2 * P:3 * P], ap[:, par, 1, 1], vn1[:, :], start=True, stop=True).then_inc(s["o_done"], 1)
        if hs == 31:
            pe.wait_ge(s["og_ready"], h + 1)
            for tile in range(TT):
                mm = pe.transpose(RA[:, tile * P:(tile + 1) * P], og[:, tile], ident)
            mm.then_inc(s["og_cols"], 1)

    def rule_act(act, h, par, hs):
        if hs == 18:
            act.wait_ge(s["v0_done"], h + 1)
            act.activation(vn0[:, :], RA[:, 0:P], ACT.Copy).then_inc(s["v0_ready"], 1)
        if hs == 20:
            act.wait_ge(s["s1_done"], h + 1)
            act.activation(s1[:, :], RA[:, P:2 * P], ACT.Copy).then_inc(s["s1_ready"], 1)
        if hs == 21:
            act.wait_ge(s["kq_s1"], h + 1)
            act.activation(oq[:, :], RB[:, P:2 * P], ACT.Copy, scale=hst[:, par, 7:8]).then_inc(s["oq_ready"], 1)
        if hs == 23:
            act.wait_ge(s["v1_done"], h + 1)
            act.activation(vn1[:, :], RA[:, P:2 * P], ACT.Copy).then_inc(s["v1_ready"], 1)
        if hs == 25:
            act.wait_ge(s["o_ready"], h + 1)
            reach(act, s["pool_b"], 2 * h)
            for tile in range(TT):
                reach(act, s["o_summed"], 2 * h + tile)
                act.activation(og[:, tile], o_t[:, tile], ACT.Square, accum_out=oss[:, tile:tile + 1])\
                   .then_inc(s["o_summed"], 1)
        if hs == 31:
            act.wait_ge(s["og_cols"], h + 1)
            act.activation(oa_hi[:, bass.ds(h, 1)].rearrange("p a n -> p (a n)"), RA[:, 0:S], ACT.Copy)\
               .then_inc(s["oa_hi_done"], 1)

    def rule_pool(pool, h):
        pool.wait_ge(s["o_summed"], 2 * h + 2)
        reach(pool, s["og_ready"], h)
        pool.tensor_tensor(orn[:, :], oss[:, :], pool_eps[:, 4:6], ALU.add).then_inc(s["pool_b"], 1)
        pool.wait_ge(s["pool_b"], 2 * h + 1)
        pool.tensor_tensor(orn[:, :], orn[:, :], halfpow[:, 0:2], ALU.pow).then_inc(s["pool_b"], 1)

    def rule_dve(dve, h, par, hs):
        if hs == 0:
            dve.wait_ge(s["ap_ready"], h + 1)
            reach(dve, s["v1_done"], h)
            dve.tensor_tensor(xmT[:, :, :], ap[:, par, :, 0], both(level0T), ALU.mult).then_inc(s["xT_ready"], 1)
            dve.wait_ge(s["a_turned"], h + 1)
            dve.tensor_tensor(xm[:, :, :], RA[:, 0:S].rearrange("p (t n) -> p t n", t=TT), both(level(0)), ALU.mult)\
               .then_inc(x_ready, 1)
            dve.wait_ge(s["xT_ready"], h + 1)
            dve.tensor_tensor(tri[:, TT:2 * TT], xmT[:, :, :], both(ident), ALU.add).then_inc(s["t_first"], 1)
            dve.wait_ge(x_ready, every(h, 0))
            dve.tensor_tensor(tri[:, 0:TT], xm[:, :, :], both(ident), ALU.add).then_inc(t_ready, 1)
        if hs in X_AT:
            l = X_AT[hs]
            dve.wait_ge(x_done, inner(h, l))
            dve.tensor_tensor(xm[:, :, :], RA[:, 0:S].rearrange("p (t n) -> p t n", t=TT), both(level(l)), ALU.mult)\
               .then_inc(x_ready, 1)
        if hs in T_AT:
            l = T_AT[hs]
            dve.wait_ge(d_done, inner(h, l))
            a = 0 if l < LEVELS - 1 else TT
            dve.wait_ge(t_ready, every(h, l - 1))
            dve.tensor_tensor(tri[:, a:], tri[:, a:], RB[:, a * P:].rearrange("p (t n) -> p t n", n=P), ALU.add)\
               .then_inc(t_ready, 1)
        if hs == 21:
            dve.wait_ge(s["kq_s1"], h + 1)
            dve.scalar_tensor_tensor(r1[:, :], RA[:, 0:P], hst[:, par, 9:10], vb[:, par, 1], ALU.mult, ALU.add)\
               .then_inc(s["r1_ready"], 1)
        if hs == 24:
            dve.wait_ge(s["o_done"], h + 1)
            dve.tensor_copy(o_t[:, 0], RB[:, 0:P])
            dve.tensor_tensor(o_t[:, 1], RB[:, 2 * P:3 * P], oq[:, :], ALU.add).then_inc(s["o_ready"], 1)
        if hs == 30:
            dve.wait_ge(s["pool_b"], 2 * h + 2)
            for tile in range(TT):
                ins = dve.scalar_tensor_tensor(og[:, tile], o_t[:, tile], orn[:, tile:tile + 1], zs[:, par, tile],
                                               ALU.mult, ALU.mult)
            ins.then_inc(s["og_ready"], 1)
        if hs == 31:
            dve.wait_ge(s["oa_hi_done"], h + 1)
            to = bass.ds(h, 1)
            dve.tensor_tensor(oa_lo[:, to].rearrange("p a n -> p (a n)"), RA[:, 0:S],
                              oa_hi[:, to].rearrange("p a n -> p (a n)").bitcast(F32), ALU.subtract)\
               .then_inc(s["oa_lo_done"], 1)

    POOL_TAPS = 8
    DVE_TAPS = LONG - POOL_TAPS

    def group_sp(sp, j):
        if isinstance(j, int) and j == 0:
            sp.wait_ge(s["zs_ready"], HEADS)
        reach(sp, s["gate_biased"], j)
        sp.dma_start(bg[:, :], t["b_gate"][0:1, bass.ds(j * P, P)].rearrange("a n -> (a n)").partition_broadcast(P))\
          .then_inc(s["bg_loaded"], 16)

    def group_out_sp(sp, j):
        sp.wait_ge(s["b_tanh"], j + 1)
        sp.dma_start(tokens(gate_a_dram)[:, :, bass.ds(j * P, P)], bth[:, :, 2]).then_inc(s["gate_a_stored"], 16)

    def group_pe(pe, j, par, hs):
        if hs == 5:
            pe.wait_ge(s["glu_ready"], j + 1)
            reach(pe, s["b_cols_taken"], j)
            for n, src in enumerate((glu2, z2b)):
                for tile in range(TT):
                    mm = pe.transpose(QA[:, n * S + tile * P:n * S + (tile + 1) * P], src[:, tile], ident)
            mm.then_inc(s["b_cols"], 1)

    def group_act(act, j, par, hs):
        if hs == 0:
            act.wait_ge(psum_ready, BLK_B + j + 1)
            reach(act, s["glu_ready"], j)
            if isinstance(j, int) and j == 0:
                act.wait_ge(s["tok_scaled"], HEADS)
                act.wait_ge(s["kq_cols"], HEADS)
            act.activation(bproj[:, 0], pairs[par][:, 0], ACT.Copy)
            act.activation(bproj[:, 1], pairs[par][:, 1], ACT.Copy).then_inc(psum_free, 1)
        if hs == 1:
            act.wait_ge(s["gate_biased"], j + 1)
            reach(act, s["gate_a_stored"], 16 * j)
            act.activation(bth[:, :, :, :].rearrange("p t c n -> p t (c n)"), bproj[:, :, P:NB], ACT.Tanh, scale=0.5)\
               .then_inc(s["b_tanh"], 1)
        if hs == 5:
            act.wait_ge(s["b_cols"], j + 1)
            reach(act, s["u_ready"], j - 1)
            act.activation(upad[:, par, LONG - 1:LONG - 1 + S], QA[:, 0:S], ACT.Copy, scale=0.5)
            act.activation(zb[:, bass.ds(j, 1)].rearrange("p a n -> p (a n)"), QA[:, S:2 * S], ACT.Copy, scale=0.25)\
               .then_inc(s["b_cols_taken"], 1)
        if 8 <= hs < 8 + 2 * POOL_TAPS and hs % 2 == 0:
            n = (hs - 8) // 2
            k = DVE_TAPS + n
            if n == 0:
                if isinstance(j, int) and j == 0:
                    act.wait_ge(s["oa_lo_done"], HEADS - 1)
                act.wait_ge(s["b_cols_taken"], j + 1)
                act.wait_ge(s["cwl_staged"], j + 1)
            reach(act, s["pool_taps"], (POOL_TAPS - 1) * j + (max(n - 2, 1) if n >= 2 else 0))
            act.activation(tap[:, n % 2], upad[:, par, k:k + S], ACT.Copy, scale=cwl[:, k:k + 1])\
               .then_inc(tap_ready[n % 2], 1)

    def group_pool(pool, j, par):
        if isinstance(j, int) and j == 0:
            pool.wait_ge(s["tok_scaled"], HEADS)
            pool.wait_ge(s["kq_cols"], HEADS)
            pool.memset(upad[:, :, 0:LONG - 1], 0.0).then_inc(s["pads_ready"], 1)
            pool.wait_ge(s["zs_ready"], HEADS)
        reach(pool, s["u_summed"], j)
        reach(pool, s["pool_taps"], (POOL_TAPS - 1) * j)
        taps = chan[:, CH_LONG:CH_END].rearrange("p (k g) -> p k g", g=KC)
        pool.tensor_copy(cwl[:, LONG:LONG + 1], chan[:, bass.ds(CH_BDW + j, 1)])
        pool.tensor_copy(cwl[:, 0:LONG], taps[:, :, bass.ds(j, 1)].rearrange("p k a -> p (k a)")).then_inc(s["cwl_staged"], 1)
        reach(pool, s["u_ready"], j)
        for n in range(1, POOL_TAPS):
            if n == 1:
                pool.wait_ge(tap_ready[0], POOL_TAPS // 2 * j + 1)
            else:
                pool.wait_ge(s["pool_taps"], (POOL_TAPS - 1) * j + n - 1)
            pool.wait_ge(tap_ready[n % 2], POOL_TAPS // 2 * j + n // 2 + 1)
            pool.tensor_tensor(acc_p[:, :], tap[:, 0] if n == 1 else acc_p[:, :], tap[:, n % 2], ALU.add)\
                .then_inc(s["pool_taps"], 1)

    def group_dve(dve, j, par, hs):
        if hs == 0:
            dve.wait_ge(psum_free, BLK_B + j + 1)
            dve.wait_ge(s["bg_loaded"], 16 * j + 16)
            dve.tensor_tensor(bproj[:, :, 3 * P:NB], bproj[:, :, 3 * P:NB], both(bg[:, :]), ALU.add)\
               .then_inc(s["gate_biased"], 1)
        if hs == 2:
            dve.wait_ge(s["b_tanh"], j + 1)
            if isinstance(j, int) and j == 0:
                dve.wait_ge(s["zs_ready"], HEADS)
                dve.wait_ge(s["oa_lo_done"], HEADS - 1)
                dve.wait_ge(s["pads_ready"], 4)
            reach(dve, s["b_cols"], j)
            dve.scalar_tensor_tensor(glu2[:, :, :], bth[:, :, 0], 1.0, bproj[:, :, 0:P], ALU.add, ALU.mult)
            dve.scalar_tensor_tensor(z2b[:, :, :], bth[:, :, 1], 1.0, bproj[:, :, 2 * P:3 * P], ALU.add, ALU.mult)\
               .then_inc(s["glu_ready"], 1)
        if 6 <= hs < 6 + DVE_TAPS:
            k = hs - 6
            src, a = upad[:, par, k:k + S], acc[:, k % 2]
            if k == 0:
                dve.wait_ge(s["b_cols_taken"], j + 1)
                dve.wait_ge(s["cwl_staged"], j + 1)
                reach(dve, s["u_ready"], j)
                dve.tensor_scalar(a, src, cwl[:, 0:1], cwl[:, LONG:LONG + 1], ALU.mult, ALU.add).then_inc(long_tap[0], 1)
            elif k == 1:
                dve.tensor_scalar(a, src, cwl[:, 1:2], None, ALU.mult).then_inc(long_tap[1], 1)
            else:
                n = (DVE_TAPS + 1 - k % 2) // 2
                dve.wait_ge(long_tap[k % 2], n * j + k // 2)
                dve.scalar_tensor_tensor(a, src, cwl[:, k:k + 1], a, ALU.mult, ALU.add).then_inc(long_tap[k % 2], 1)
        if hs == 30:
            dve.wait_ge(long_tap[0], (DVE_TAPS + 1) // 2 * (j + 1))
            dve.wait_ge(long_tap[1], DVE_TAPS // 2 * (j + 1))
            dve.tensor_tensor(acc[:, 0], acc[:, 0], acc[:, 1], ALU.add).then_inc(s["u_summed"], 1)
        if hs == 31:
            dve.wait_ge(s["u_summed"], j + 1)
            dve.wait_ge(s["pool_taps"], (POOL_TAPS - 1) * (j + 1))
            dve.tensor_tensor(ub[:, bass.ds(j, 1)].rearrange("p a n -> p (a n)"), acc[:, 0], acc_p[:, :], ALU.add)\
               .then_inc(s["u_ready"], 1)

    BANKS = (QA, QB, RA, RB)

    def turn_pe(pe, base, src, first_wait, groups=range(KC // 2)):
        for g in groups:
            first_wait(g)
            reach(pe, s["turned_lo"], base + g - 3)
            for k in (2 * g, 2 * g + 1):
                for tile in range(TT):
                    mm = pe.transpose(BANKS[(base + g) % 4][:, (k % 2) * S + tile * P:(k % 2) * S + (tile + 1) * P],
                                      src(tile, k), ident)
            mm.then_inc(s["turned"], 1)

    def turn_act(act, base, hi, scale=None, factor=1.0, groups=range(KC // 2)):
        for g in groups:
            act.wait_ge(s["turned"], base + g + 1)
            if scale is None:
                ins = act.activation(hi[:, 2 * g:2 * g + 2].rearrange("p k n -> p (k n)"), BANKS[(base + g) % 4][:, :], ACT.Copy, scale=factor)
            else:
                for k in range(2):
                    ins = act.activation(hi[:, 2 * g + k], BANKS[(base + g) % 4][:, k * S:(k + 1) * S], ACT.Copy,
                                         scale=scale[:, 2 * g + k:2 * g + k + 1])
            ins.then_inc(s["turned_hi"], 1)

    def turn_dve(dve, base, hi, lo, scale=None, factor=1.0, groups=range(KC // 2)):
        for g in groups:
            dve.wait_ge(s["turned_hi"], base + g + 1)
            if scale is None:
                ins = dve.scalar_tensor_tensor(lo[:, 2 * g:2 * g + 2].rearrange("p k n -> p (k n)"), BANKS[(base + g) % 4][:, :], factor,
                                               hi[:, 2 * g:2 * g + 2].rearrange("p k n -> p (k n)").bitcast(F32),
                                               ALU.mult, ALU.subtract)
            else:
                for k in range(2):
                    ins = dve.scalar_tensor_tensor(lo[:, 2 * g + k], BANKS[(base + g) % 4][:, k * S:(k + 1) * S],
                                                   scale[:, 2 * g + k:2 * g + k + 1], hi[:, 2 * g + k].bitcast(F32),
                                                   ALU.mult, ALU.subtract)
            ins.then_inc(s["turned_lo"], 1)

    def start_sp(sp):
        sp.dma_start(const[:, :], t["shape_constants"]).then_inc(s["rows_in"], 16)
        sp.dma_start(x_tok[:, :, :], tokens(t["x"][0])).then_inc(s["x_in"], 16)
        sp.dma_start(ba_raw[:, :, :], w_in[:, :, COL_BA:COL_BA + 2 * HEADS]).then_inc(s["ba_in"], 16)
        vecs = [t[n].rearrange("a (r c) -> (a r) c", c=P) for n in ("g_pre", "ln_g", "ln_b", "b_dw")]
        for i, v in enumerate(vecs):
            sp.dma_start(rows[16 * i:16 * (i + 1), 0], v).then_inc(s["rows_in"], 16)
        short = t["w_conv_qkv"][0].rearrange("k (r c) -> (k r) c", c=P)
        long = t["w_dw"][0].rearrange("k (r c) -> (k r) c", c=P)
        for i, (at, n) in enumerate(ROW_TILES[1:], 1):
            src = short[at - CH_SHORT:at - CH_SHORT + n] if at < CH_LONG else long[at - CH_LONG:at - CH_LONG + n]
            sp.dma_start(rows[0:n, i], src).then_inc(s["rows_in"], 16)
        sp.dma_start(dt_b[:, :], t["dt_bias"][0].partition_broadcast(P)).then_inc(s["ba_in"], 16)
        sp.dma_start(alog_b[:, :], t["a_log"][0].partition_broadcast(P)).then_inc(s["ba_in"], 16)
        sp.dma_start(half_g[:, :], t["g_dn_out"][0].partition_broadcast(P)).then_inc(s["ba_in"], 16)

    def decays_sp(sp):
        sp.wait_ge(s["gc_copied"], 3)
        sp.dma_start(gc_rows, gcT[:, :]).then_inc(s["gc_stored"], 16)
        sp.wait_ge(s["gc_stored"], 16)
        sp.wait_ge(s["head_ready"], 1)
        sp.wait_ge(s["ba_done"], 1)
        sp.dma_start(gc_b[:, :, :], gc_rows.partition_broadcast(P)).then_inc(s["gc_stored"], 16)

    def start_pe(pe):
        pe.wait_ge(s["rows_in"], 16 * (4 + len(ROW_TILES)))
        for i, (at, n) in enumerate(ROW_TILES):
            reach(pe, s["chan_ready"], i - 1)
            pe.transpose((QA, QB)[i % 2][:, 0:n], rows[0:n, i], ident[0:n, 0:n]).then_inc(s["rows_cols"], 1)
        def first(g):
            if g == 0:
                pe.wait_ge(s["x_scaled"], 1)
                pe.wait_ge(s["chan_ready"], len(ROW_TILES))
        turn_pe(pe, 0, lambda tile, k: hs_tok[:, tile, k * P:(k + 1) * P], first)
        pe.wait_ge(s["turned_lo"], KC // 2)
        pe.wait_ge(s["ba_lo_ready"], 1)
        for tile, bank in enumerate((RA, RB)):
            for k in range(KC):
                xh, xl = in_hi[:, k, tile * P:(tile + 1) * P], in_lo[:, k, tile * P:(tile + 1) * P]
                pe.matmul(bank[:, 0:2 * HEADS], xh, ba_hi[:, k], start=(k == 0), stop=False)
                pe.matmul(bank[:, 0:2 * HEADS], xh, ba_lo[:, k], start=False, stop=False)
                mm = pe.matmul(bank[:, 0:2 * HEADS], xl, ba_hi[:, k], start=False, stop=(k == KC - 1))
        mm.then_inc(s["ba_done"], 1)

    def decays_pe(pe):
        pe.wait_ge(s["sg_g"], 1)
        pe.matmul(QA[:, 0:2 * HEADS], triu, sgl[:, 15], start=True, stop=True)
        pe.matmul(QB[:, 0:2 * HEADS], ones, sgl[:, 15], start=True, stop=True).then_inc(s["gc_done"], 1)
        pe.wait_ge(s["gc_copied"], 1)
        pe.transpose(QA[0:TT * HEADS, 0:P], sgl[:, 0], ident).then_inc(s["gcT_done"], 1)

    def start_act(act):
        act.wait_ge(s["x_in"], 16)
        for tile in range(TT):
            act.activation(hs_tok[:, tile], x_tok[:, tile], ACT.Square, accum_out=small[:, tile:tile + 1])\
               .then_inc(s["x_ss"], 1)
        act.wait_ge(s["ba_in"], 64)
        act.activation(ba_hi[:, :, :], ba_raw[:, :, :], ACT.Copy).then_inc(s["ba_split"], 1)
        act.wait_ge(s["chan_ready"], len(ROW_TILES))
        turn_act(act, 0, in_hi, scale=chan[:, CH_GPRE:CH_GPRE + KC])

    def decays_act(act):
        v = lambda i: sgl[:, i]
        act.wait_ge(s["ba_out"], 1)
        act.activation(v(2), v(1), ACT.Exp, scale=-1.0).then_inc(s["sg_a"], 1)
        act.wait_ge(s["ba_in"], 64)
        act.activation(v(14)[:, 0:HEADS], alog_b[:, :], ACT.Exp).then_inc(s["sg_a"], 1)
        act.activation(v(13), v(7), ACT.Tanh, scale=0.5).then_inc(s["sg_a"], 1)
        act.wait_ge(s["sg_exp"], 1)
        act.activation(v(5), v(3), ACT.Ln).then_inc(s["sg_a"], 1)
        act.wait_ge(s["gc_copied"], 2)
        hv = head_all[:, :, :].rearrange("p h (k t) -> p k t h", t=TT)
        w = lambda i: sgl[:, i].rearrange("p (t h) -> p t h", t=TT)
        act.activation(hv[:, 3], w(0), ACT.Exp).then_inc(s["sg_a"], 1)
        act.activation(hv[:, 5], w(1), ACT.Exp).then_inc(s["sg_a"], 1)

    def start_pool(pool):
        pool.memset(halfpow[:, :], -0.5).then_inc(s["pads_ready"], 1)
        pool.memset(eps_col[:, :], EPS).then_inc(s["pads_ready"], 1)
        pool.memset(pool_eps[:, 0:4], 4 * EPS)
        pool.memset(pool_eps[:, 4:6], P * EPS)
        pool.memset(conv_in[:, :, 0:SHORT - 1], 0.0).then_inc(s["pads_ready"], 1)
        pool.wait_ge(s["pads_ready"], 1)
        pool.wait_ge(s["x_ss"], TT)
        pool.tensor_scalar(small[:, 2:4], small[:, 0:2], 1.0 / D, EPS, ALU.mult, ALU.add).then_inc(s["x_rms"], 1)
        pool.wait_ge(s["x_rms"], 1)
        pool.tensor_tensor(small[:, 4:6], small[:, 2:4], halfpow[:, 0:2], ALU.pow).then_inc(s["x_rms"], 1)

    def start_dve(dve):
        for i, (at, n) in enumerate(ROW_TILES):
            dve.wait_ge(s["rows_cols"], i + 1)
            dve.tensor_copy(chan[:, at:at + n], (QA, QB)[i % 2][:, 0:n]).then_inc(s["chan_ready"], 1)
        dve.wait_ge(s["x_rms"], 2)
        for tile in range(TT):
            ins = dve.tensor_scalar(hs_tok[:, tile], x_tok[:, tile], small[:, 4 + tile:5 + tile], None, ALU.mult)
        ins.then_inc(s["x_scaled"], 1)
        dve.wait_ge(s["ba_split"], 1)
        dve.tensor_tensor(ba_lo[:, :, :], ba_raw[:, :, :], ba_hi[:, :, :].bitcast(F32), ALU.subtract)\
           .then_inc(s["ba_lo_ready"], 1)
        turn_dve(dve, 0, in_hi, in_lo, scale=chan[:, CH_GPRE:CH_GPRE + KC])

    def decays_dve(dve):
        n = [0]

        def then(ins):
            n[0] += 1
            ins.then_inc(s["sg_v"], 1)
            dve.wait_ge(s["sg_v"], n[0])

        v = lambda i: sgl[:, i]
        w = lambda i: sgl[:, i].rearrange("p (t h) -> p t h", t=TT)
        dve.wait_ge(s["ba_done"], 1)
        dve.wait_ge(s["ba_in"], 64)
        for tile, bank in enumerate((RA, RB)):
            dve.tensor_copy(w(7)[:, tile], bank[:, 0:HEADS])
            ins = dve.tensor_tensor(w(0)[:, tile], bank[:, HEADS:2 * HEADS], dt_b[:, :], ALU.add)
        then(ins)
        dve.tensor_scalar(v(12), v(0), 0.0, None, ALU.max)
        dve.scalar_tensor_tensor(v(1), v(0), -1.0, v(0), ALU.mult, ALU.max).then_inc(s["ba_out"], 1)
        then(dve.tensor_scalar(half_g[:, :], half_g[:, :], 0.5 * float(P) ** 0.5, None, ALU.mult))
        dve.wait_ge(s["sg_a"], 1)
        dve.tensor_scalar(v(3), v(2), 1.0, None, ALU.add).then_inc(s["sg_exp"], 1)
        dve.wait_ge(s["sg_exp"], 1)
        then(dve.tensor_scalar(v(4), v(3), -1.0, None, ALU.add))
        then(dve.tensor_scalar(v(6), v(4), 0.0, None, ALU.is_equal))
        then(dve.tensor_tensor(v(8), v(4), v(6), ALU.add))
        then(dve.reciprocal(v(9), v(8)))
        then(dve.tensor_tensor(v(10), v(9), v(2), ALU.mult))
        dve.wait_ge(s["sg_a"], 4)
        then(dve.tensor_tensor(v(11), v(10), v(5), ALU.mult))
        then(dve.tensor_tensor(v(8), v(6), v(2), ALU.mult))
        then(dve.tensor_tensor(v(11), v(11), v(8), ALU.add))
        then(dve.tensor_tensor(v(11), v(11), v(12), ALU.add))
        dve.scalar_tensor_tensor(w(15), w(11), -1.0, v(14)[:, 0:HEADS].unsqueeze(1).broadcast_to([P, TT, HEADS]),
                                 ALU.mult, ALU.mult).then_inc(s["sg_g"], 1)
        hv = head_all[:, :, :].rearrange("p h (k t) -> p k t h", t=TT)
        dve.tensor_scalar(hv[:, 0], w(13), 0.5, 0.5, ALU.mult, ALU.add)
        dve.tensor_scalar(hv[:, 1], w(13), 0.25, 0.25, ALU.mult, ALU.add)
        dve.wait_ge(s["gc_done"], 1)
        dve.tensor_copy(v(0), QA[:, 0:2 * HEADS]).then_inc(s["gc_copied"], 1)
        dve.wait_ge(s["gc_copied"], 1)
        dve.tensor_copy(hv[:, 2], w(0))
        dve.tensor_tensor(v(1), QB[:, 0:2 * HEADS], v(0), ALU.subtract).then_inc(s["gc_copied"], 1)
        dve.wait_ge(s["gcT_done"], 1)
        dve.tensor_copy(gcT[:, :], QA[0:TT * HEADS, 0:P]).then_inc(s["gc_copied"], 1)
        dve.wait_ge(s["sg_a"], 6)
        dve.tensor_scalar(hv[:, 4], hv[:, 3], -1.0, None, ALU.mult).then_inc(s["head_ready"], 1)

    def ready(eng, blk):
        eng.wait_ge(psum_ready, blk + 1)
        eng.wait_ge(psum_free, blk)

    VEC_GATE, VEC_POST, VEC_PLE, VEC_BANDS, VEC_LN0, VEC_MASK, VEC_LN1 = (16 * n for n in (1, 3, 5, 6, 8, 9, 11))
    whole = lambda x: (lambda tile, k: x[:, tile, k * P:(k + 1) * P])
    four = lambda a: a.rearrange("p k n -> p (k n)")
    cols = lambda n: slice(n * NB, (n + 1) * NB)
    row = lambda x: x.unsqueeze(1).broadcast_to([P, 4, S])
    tiles = lambda x, n: x.unsqueeze(1).broadcast_to([P, TT, n])

    TURN_Y, TURN_MEM, TURN_Y3, TURN_X1, TURN_X2, TURN_M0, TURN_H1, TURN_M1 = 8, 14, 16, 24, 32, 40, 48, 56

    LN0 = 32

    def norm_b_pe(pe, at):
        at -= LN0
        if 2 <= at < 6:
            c = at - 2
            for j in range(4 * c, 4 * c + 4):
                mm = pe.matmul(QA[:, 0:S], ones, ub[:, j], start=(j == 0), stop=(j == KC - 1))
            if c == 3:
                mm.then_inc(s["var_done"], 1)
        if 10 <= at < 18 and at % 2 == 0:
            c = (at - 10) // 2
            pe.wait_ge(s["squared"], c + 1)
            for n in range(4):
                mm = pe.matmul(QB[:, 0:S], ones, sqb[:, c % 2, n], start=(c + n == 0), stop=(c == 3 and n == 3))
            mm.then_inc(s["var_done"], 1)

    def norm_b_act(act, at):
        at -= LN0
        if at == 6:
            act.wait_ge(s["var_done"], 1)
            act.activation(mub[:, :], QA[:, 0:S], ACT.Copy, scale=1.0 / D).then_inc(s["mean_ready"], 1)
        if 8 <= at < 16 and at % 2 == 0:
            c = (at - 8) // 2
            act.wait_ge(s["centred"], c + 1)
            reach(act, s["var_done"], c if c >= 2 else 0)
            act.activation(sqb[:, c % 2], ub[:, 4 * c:4 * c + 4], ACT.Square).then_inc(s["squared"], 1)
        if at == 18:
            act.wait_ge(s["var_done"], 5)
            act.activation(rsb[:, :], QB[:, 0:S], ACT.Sqrt, scale=1.0 / D, bias=eps_col[:, :]).then_inc(s["mean_ready"], 1)
        if at >= 22 and (at - 22) % 8 == 0 and at < 22 + 32:
            c = (at - 22) // 8
            act.wait_ge(s["ln_scaled"], c + 1)
            for j in range(4 * c, 4 * c + 4):
                ins = act.activation(ub[:, j], ub[:, j], ACT.Identity, scale=chan[:, CH_LNG + j:CH_LNG + j + 1],
                                     bias=chan[:, CH_LNB + j:CH_LNB + j + 1])
            ins.then_inc(s["ln_affine"], 1)
        if at >= 23 and (at - 23) % 8 == 0 and at < 23 + 32:
            c = (at - 23) // 8
            act.wait_ge(s["ln_affine"], c + 1)
            reach(act, s["ln_silu"], c - 1)
            act.activation(sqb[:, c % 2], ub[:, 4 * c:4 * c + 4], ACT.Tanh, scale=0.5).then_inc(s["ln_tanh"], 1)
        if at >= 26 and (at - 26) % 8 == 0 and at < 26 + 32:
            c = (at - 26) // 8
            act.wait_ge(s["ln_gated"], c + 1)
            act.activation(ub_hi[:, 4 * c:4 * c + 4], ub[:, 4 * c:4 * c + 4], ACT.Copy).then_inc(s["ub_hi_done"], 1)

    def norm_b_dve(dve, at):
        at -= LN0
        if 7 <= at < 15 and at % 2 == 1:
            c = (at - 7) // 2
            dve.wait_ge(s["mean_ready"], 1)
            dve.tensor_tensor(ub[:, 4 * c:4 * c + 4], ub[:, 4 * c:4 * c + 4], row(mub[:, :]), ALU.subtract)\
               .then_inc(s["centred"], 1)
        if at == 18:
            dve.wait_ge(s["mean_ready"], 2)
            dve.reciprocal(rsb[:, :], rsb[:, :]).then_inc(s["rstd_ready"], 1)
        if at >= 20 and (at - 20) % 8 == 0 and at < 20 + 32:
            c = (at - 20) // 8
            dve.wait_ge(s["rstd_ready"], 1)
            dve.tensor_tensor(ub[:, 4 * c:4 * c + 4], ub[:, 4 * c:4 * c + 4], row(rsb[:, :]), ALU.mult)\
               .then_inc(s["ln_scaled"], 1)
        if at >= 24 and (at - 24) % 8 == 0 and at < 24 + 32:
            c = (at - 24) // 8
            x = ub[:, 4 * c:4 * c + 4]
            dve.wait_ge(s["ln_tanh"], c + 1)
            dve.scalar_tensor_tensor(four(x), four(sqb[:, c % 2]), 1.0, four(x), ALU.add, ALU.mult).then_inc(s["ln_silu"], 1)
        if at >= 25 and (at - 25) % 8 == 0 and at < 25 + 32:
            c = (at - 25) // 8
            x = ub[:, 4 * c:4 * c + 4]
            dve.wait_ge(s["ln_silu"], c + 1)
            dve.tensor_tensor(x, x, zb[:, 4 * c:4 * c + 4], ALU.mult).then_inc(s["ln_gated"], 1)
        if at >= 27 and (at - 27) % 8 == 0 and at < 27 + 32:
            c = (at - 27) // 8
            dve.wait_ge(s["ub_hi_done"], c + 1)
            dve.tensor_tensor(ub_lo[:, 4 * c:4 * c + 4], ub[:, 4 * c:4 * c + 4], ub_hi[:, 4 * c:4 * c + 4].bitcast(F32),
                              ALU.subtract).then_inc(s["ub_lo_done"], 1)

    def mem_head(layer, m):
        q = (mqT0, mqT1)[layer]
        return q[:, m], mkT[:, layer, m], lambda tile: mv[:, layer, tile, m * P:(m + 1) * P], False, 3 * NB + m * P

    def moba_head(m):
        return qT1[:, m], kT1[:, m], lambda tile: v1_[:, tile, m * P:(m + 1) * P], True, m * P

    ATTEND = [mem_head(0, m) for m in range(MEM_HEADS)] + [moba_head(m) for m in range(MOBA_HEADS)] \
        + [mem_head(1, m) for m in range(MEM_HEADS)]
    PERIOD = 8
    ATT_AT = {0: (BLK_IN0 + 5, 0, MEM_HEADS), 1: (BLK_IN1 + 3, MEM_HEADS, len(ATTEND) - MEM_HEADS)}

    def attention(at, step):
        for blk, first, n in ATT_AT.values():
            p, hs = divmod(at - 32 * (blk - BLK_GB), PERIOD)
            for second in (True, False):
                if at >= 32 * (blk - BLK_GB) and 0 <= p - second < n:
                    step(first + p - second, hs, second)

    def attend_pe(pe, i, hs, second):
        q, k, v, causal, to = ATTEND[i]
        if second and hs == 0:
            pe.wait_ge(s["probs_ready"], i + 1)
            reach(pe, s["probT_ready"], i)
            for key in range(TT):
                for tile in range(TT):
                    mm = pe.transpose(RB[:, key * S + tile * P:key * S + (tile + 1) * P], sc[:, tile, key * P:(key + 1) * P], ident)
            mm.then_inc(s["probs_turned"], 1)
        if second and hs == 3:
            pe.wait_ge(s["probT_ready"], i + 1)
            reach(pe, s["att_ready"], i)
            for tile in range(TT):
                n = tile + 1 if causal else TT
                for key in range(n):
                    mm = pe.matmul(QA[:, tile * P:(tile + 1) * P], probT[:, key, tile * P:(tile + 1) * P], v(key),
                                   start=(key == 0), stop=(key == n - 1))
            mm.then_inc(s["attended"], 1)
        if not second and hs == 4:
            reach(pe, s["scores_masked"], i)
            if i == 0:
                pe.wait_ge(s["heads_taken"], 6)
                pe.wait_ge(s["pw_ready"], len(POOL_WINDOWS))
            if i == MEM_HEADS:
                pe.wait_ge(s["heads_taken"], 16)
            if i == 2 * MEM_HEADS:
                pe.wait_ge(s["heads_taken"], 18)
            if i == len(ATTEND) - MEM_HEADS:
                pe.wait_ge(s["heads_taken"], 20)
            for tile in range(TT):
                mm = pe.matmul(RA[:, tile * S:(tile + 1) * S], q[:, tile * P:(tile + 1) * P], k, start=True, stop=True)
            mm.then_inc(s["scores_done"], 1)

    def attend_act(act, i, hs, second):
        to = ATTEND[i][4]
        mx, sums, inv = st[:, 48:50], st[:, 50:52], st[:, 52:54]
        if second and hs == 3:
            act.wait_ge(s["attended"], i + 1)
            act.wait_ge(s["sums_inverted"], i + 1)
            for tile in range(TT):
                ins = act.activation(mo[:, tile, to:to + P], QA[:, tile * P:(tile + 1) * P], ACT.Copy, scale=inv[:, tile:tile + 1])
            ins.then_inc(s["att_ready"], 1)
        if not second and hs == 5:
            act.wait_ge(s["max_ready"], 2 * i + 2)
            reach(act, s["sums_inverted"], i)
            for tile in range(TT):
                ins = act.activation(sc[:, tile], sc[:, tile], ACT.Exp, bias=mx[:, tile:tile + 1],
                                     accum_out=sums[:, tile:tile + 1])
            ins.then_inc(s["probs_ready"], 1)

    def attend_dve(dve, i, hs, second):
        causal = ATTEND[i][3]
        mx, sums, inv = st[:, 48:50], st[:, 50:52], st[:, 52:54]
        both_tiles = RA[:, :].rearrange("p (t n) -> p t n", t=TT)
        if second and hs == 0:
            dve.wait_ge(s["probs_turned"], i + 1)
            reach(dve, s["attended"], i)
            dve.tensor_copy(probT[:, :, :].rearrange("p t n -> p (t n)"), RB[:, :]).then_inc(s["probT_ready"], 1)
        if not second and hs == 4:
            dve.wait_ge(s["scores_done"], i + 1)
            reach(dve, s["probs_turned"], i)
            if causal:
                dve.wait_ge(s["vec_loaded"], VEC_MASK)
                dve.scalar_tensor_tensor(sc[:, :, :], both_tiles, RSQ, mask[:, :, :], ALU.mult, ALU.add).then_inc(s["scores_masked"], 1)
            else:
                dve.tensor_scalar(sc[:, :, :], both_tiles, RSQ, None, ALU.mult).then_inc(s["scores_masked"], 1)
            dve.wait_ge(s["scores_masked"], i + 1)
            reach(dve, s["probs_ready"], i)
            dve.tensor_reduce(mx, sc[:, :, :], AX.X, ALU.max).then_inc(s["max_ready"], 1)
            dve.wait_ge(s["max_ready"], 2 * i + 1)
            dve.tensor_scalar(mx, mx, -1.0, None, ALU.mult).then_inc(s["max_ready"], 1)
        if not second and hs == 7:
            dve.wait_ge(s["probs_ready"], i + 1)
            reach(dve, s["att_ready"], i)
            dve.reciprocal(inv, sums).then_inc(s["sums_inverted"], 1)

    HEADS_OF = {BLK_MEM0: (0, stage0, lambda r: mkT[:, 0, 2 * r:2 * r + 2]), BLK_MEM1: (1, stage0, lambda r: mkT[:, 1, 2 * r:2 * r + 2]),
                BLK_IN0 + 3: (2, stage0, lambda r: mqT0[:, 2 * r:2 * r + 2])}
    for n in range(3):
        HEADS_OF[BLK_KV + n] = (3 + n, stage1, lambda r, n=n: kT1[:, 4 * n + 2 * r:4 * n + 2 * r + 2])
        HEADS_OF[BLK_IN1 + n] = (6 + n, stage1, lambda r, n=n: qT1[:, 4 * n + 2 * r:4 * n + 2 * r + 2])
    HEADS_OF[BLK_IN1 + 3] = (9, stage1, lambda r: mqT1[:, 2 * r:2 * r + 2])

    def heads_pe(pe, n, stage, hs, blk):
        if hs in (2, 4):
            r = (hs - 2) // 2
            pe.wait_ge(psum_free, blk + 1)
            reach(pe, s["heads_taken"], 2 * n + r)
            for m in range(2):
                for tile in range(TT):
                    c = (2 * r + m) * P
                    mm = pe.transpose(QB[:, m * S + tile * P:m * S + (tile + 1) * P], stage[:, tile, c:c + P], ident)
            mm.then_inc(s["heads_done"], 1)

    def heads_act(act, n, stage, to, hs, blk):
        if hs == 0:
            ready(act, blk)
            reach(act, s["heads_done"], 2 * n)
            if n == 0:
                act.wait_ge(s["mix_ready"], 4)
            for tile in range(TT):
                ins = act.activation(stage[:, tile], pairs[blk % 2][:, tile], ACT.Copy)
            ins.then_inc(psum_free, 1)
        if hs in (2, 4):
            r = (hs - 2) // 2
            act.wait_ge(s["heads_done"], 2 * n + r + 1)
            act.activation(to(r), QB[:, :].rearrange("p (m n) -> p m n", m=2), ACT.Copy).then_inc(s["heads_taken"], 1)

    RMS = {BLK_OUT: (0, 1.0 / D, EPS, 1.0), BLK_PLE: (1, 0.25 / D, EPS, 0.5)}

    def rms_pool(pool, n):
        _, by, eps, factor = list(RMS.values())[n]
        pool.wait_ge(s["ms_ready"], n + 1)
        pool.tensor_scalar(small[:, 20:22], small[:, 18:20], by, eps, ALU.mult, ALU.add).then_inc(s["ms_rms"], 1)
        pool.wait_ge(s["ms_rms"], 3 * n + 1)
        pool.tensor_tensor(small[:, 22:24], small[:, 20:22], halfpow[:, 0:2], ALU.pow).then_inc(s["ms_rms"], 1)
        pool.wait_ge(s["ms_rms"], 3 * n + 2)
        pool.tensor_scalar(small[:, 24:26], small[:, 22:24], factor, None, ALU.mult).then_inc(s["ms_rms"], 1)

    def rms_dve(dve, n):
        dve.wait_ge(s["mo_summed"], 8 * (n + 1))
        dve.tensor_reduce(small[:, 18:20], small[:, 8:16].rearrange("p (t n) -> p t n", t=TT), AX.X, ALU.add)\
           .then_inc(s["ms_ready"], 1)
        dve.wait_ge(s["ms_rms"], 3 * n + 3)
        dve.wait_ge(s["mo_scaled"], 4 * (n + 1))
        dve.wait_ge(s["vec_loaded"], VEC_POST)
        for c in range(4):
            for tile in range(TT):
                ins = dve.scalar_tensor_tensor(xr[:, tile, cols(c)], mo[:, tile, cols(c)], small[:, 24 + tile:25 + tile],
                                               xr[:, tile, cols(c)], ALU.mult, ALU.add)
            ins.then_inc(s["x_added"], 1)

    def res_dve(dve, blk, n, layer):
        ready(dve, blk)
        for tile in range(TT):
            ins = dve.scalar_tensor_tensor(xr[:, tile, cols(n)], xr[:, tile, cols(n)], ALPHA, pairs[blk % 2][:, tile],
                                           ALU.mult, ALU.add)
        ins.then_inc(psum_free, 1)
        dve.wait_ge(psum_free, blk + 1)
        stats = sgst.rearrange("p (t n k) -> p t n k", t=TT, n=4)
        for tile in range(TT):
            ins = dve.bn_stats(stats[:, tile, n], xr[:, tile, cols(n)])
        ins.then_inc(s["stats_ready"], 1)

    def ln_dve(dve, layer, lnv):
        dve.wait_ge(s["stats_ready"], 4 * (layer + 1))
        stats = sgst.rearrange("p (t n k) -> p t n k", t=TT, n=4)
        for tile in range(TT):
            ins = dve.bn_aggr(small[:, 28 + 2 * tile:30 + 2 * tile], stats[:, tile].rearrange("p n k -> p (n k)"))
        ins.then_inc(s["aggr_ready"], 1)
        for c in range(4):
            dve.wait_ge(s["ln_normed"], 4 * layer + c + 1)
            if c == 0:
                dve.wait_ge(s["vec_loaded"], (VEC_LN0, VEC_LN1)[layer])
            x = xr[:, :, cols(c)]
            dve.tensor_tensor(x, x, tiles(lnv[0][:, cols(c)], NB), ALU.mult).then_inc(s["ln_gain"], 1)
            dve.wait_ge(s["ln_gain"], 4 * layer + c + 1)
            dve.tensor_tensor(x, x, tiles(lnv[1][:, cols(c)], NB), ALU.add).then_inc(s["ln_done"], 1)

    def ln_act(act, layer):
        act.wait_ge(s["ln_pool"], 4 * (layer + 1))
        for c in range(4):
            for tile in range(TT):
                x = xr[:, tile, cols(c)]
                ins = act.activation(x, x, ACT.Identity, scale=small[:, 34 + tile:35 + tile], bias=small[:, 38 + tile:39 + tile])
            ins.then_inc(s["ln_normed"], 1)

    def ln_pool(pool, layer):
        mean, var = (small[:, 28:32].rearrange("p (t k) -> p k t", k=2)[:, k] for k in range(2))
        pool.wait_ge(s["aggr_ready"], layer + 1)
        pool.tensor_scalar(small[:, 32:34], var, LN_EPS, None, ALU.add).then_inc(s["ln_pool"], 1)
        pool.wait_ge(s["ln_pool"], 4 * layer + 1)
        pool.tensor_tensor(small[:, 34:36], small[:, 32:34], halfpow[:, 0:2], ALU.pow).then_inc(s["ln_pool"], 1)
        pool.wait_ge(s["ln_pool"], 4 * layer + 2)
        pool.tensor_tensor(small[:, 36:38], mean, small[:, 34:36], ALU.mult).then_inc(s["ln_pool"], 1)
        pool.wait_ge(s["ln_pool"], 4 * layer + 3)
        pool.tensor_scalar(small[:, 38:40], small[:, 36:38], -1.0, None, ALU.mult).then_inc(s["ln_pool"], 1)

    LNV = [(vec[:, :], ln_b0[:, :]), (ln_vec_a[:, 0], ln_vec_a[:, 1])]
    GATES = {BLK_IN0 + 4: 0, BLK_IN0 + 5: 1, BLK_IN0 + 6: 2, BLK_IN0 + 7: 3,
             BLK_IN1 + 4: 4, BLK_IN1 + 5: 5, BLK_IN1 + 6: 6, BLK_IN1 + 7: 7}

    def gate_act(act, blk, hs):
        stage = stage0 if blk < BLK_KV else stage1
        n = GATES[blk]
        if hs == 0:
            act.wait_ge(psum_ready, blk + 1)
            if n in (0, 4):
                act.wait_ge(s["heads_done"], 6 if n == 0 else 20)
            reach(act, s["mixed_ready"], n)
            for tile in range(TT):
                ins = act.activation(stage[:, tile], pairs[blk % 2][:, tile], ACT.Tanh, scale=0.5)
            ins.then_inc(s["gate_tanh"], 1)

    def gate_dve(dve, blk, hs):
        stage = stage0 if blk < BLK_KV else stage1
        n = GATES[blk]
        if hs == 1:
            dve.wait_ge(s["gate_tanh"], n + 1)
            dve.wait_ge(psum_free, blk)
            for tile in range(TT):
                ins = dve.scalar_tensor_tensor(stage[:, tile], stage[:, tile], 1.0, pairs[blk % 2][:, tile], ALU.add, ALU.mult)
            ins.then_inc(psum_free, 1)
            if n < 3:
                dve.wait_ge(s["pw_ready"], 4)
            elif n == 3:
                dve.wait_ge(s["att_ready"], MEM_HEADS)
            elif n < 7:
                dve.wait_ge(s["att_ready"], MEM_HEADS + 4 * (n - 3))
            else:
                dve.wait_ge(s["att_ready"], len(ATTEND))
            dve.wait_ge(psum_free, blk + 1)
            x = mo[:, :, cols(n % 4)]
            dve.tensor_tensor(x, x, stage[:, :, :], ALU.mult).then_inc(s["mixed_ready"], 1)

    POOL_BLK, MAP_BLK = BLK_IN0 + 3, BLK_IN0 + 4
    POOLED = 6

    def pool_pe(pe, blk, hs):
        if blk == POOL_BLK and hs >= 4 and hs % 4 == 0 and hs < 28:
            r = hs // 4 - 1
            if r == 0:
                pe.wait_ge(psum_free, BLK_IN0 + 3)
                pe.wait_ge(s["vec_loaded"], VEC_BANDS)
            reach(pe, s["pool_ready"], r - 1)
            for m in range(2):
                c = 2 * r + m
                for tile in range(TT):
                    mm = pe.matmul((RA, RB)[r % 2][:, m * S:(m + 1) * S], u0[:, tile, c * P:(c + 1) * P],
                                   bands[:, tile, c // 3], start=(m == 0 and tile == 0), stop=(tile == TT - 1),
                                   skip_group_check=True)
            mm.then_inc(s["pool_done"], 1)
        if blk == MAP_BLK and hs % 8 == 2:
            g = hs // 8
            pe.wait_ge(s["pool_ready"], 6)
            pe.wait_ge(s["pw_loaded"], 32 * (g + 1))
            reach(pe, s["pw_ready"], g)
            for tile in range(TT):
                for k in range(3):
                    mm = pe.matmul((RA, RB)[tile][:, 0:PG], pooled[:, 3 * g + k, tile * P:(tile + 1) * P], pool_w[:, k],
                                   start=(k == 0), stop=(k == 2))
            mm.then_inc(s["pool_done"], 1)

    def pool_act(act, blk, hs):
        if blk == POOL_BLK and hs >= 4 and hs % 4 == 0 and hs < 28:
            r = hs // 4 - 1
            act.wait_ge(s["pool_done"], r + 1)
            act.activation(pooled[:, 2 * r:2 * r + 2].rearrange("p c n -> p (c n)"), (RA, RB)[r % 2][:, :], ACT.Copy)\
               .then_inc(s["pool_ready"], 1)

    def pool_dve(dve, blk, hs):
        if blk == MAP_BLK and hs % 8 == 2:
            g = hs // 8
            dve.wait_ge(s["pool_done"], POOLED + g + 1)
            dve.wait_ge(s["pw_loaded"], 32 * (g + 1))
            for tile in range(TT):
                ins = dve.tensor_tensor(mo[:, tile, g * PG:(g + 1) * PG], (RA, RB)[tile][:, 0:PG], pscale[:, g % 2], ALU.mult)
            ins.then_inc(s["pw_ready"], 1)

    def beside_pe(pe, blk, hs):
        at = 32 * (blk - BLK_GB) + hs
        if blk == BLK_GB:
            group_pe(pe, KC - 1, 1, hs)
        if at == LN0:
            pe.wait_ge(s["u_ready"], KC)
        norm_b_pe(pe, at)
        if BLK_Y + 2 <= blk <= BLK_Y + 8 and blk % 2 == BLK_Y % 2 and hs == 4:
            n = (blk - BLK_Y) // 2 - 1
            turn_pe(pe, TURN_Y3 if n == 3 else TURN_Y, lambda tile, k: mix[:, tile, (k % 4) * P:(k % 4 + 1) * P],
                    lambda g: pe.wait_ge(s["mix_ready"], n + 1), range(2 * n, 2 * n + 2))
        if blk == BLK_Y + 7 and hs >= 2 and hs % 3 == 2 and hs < 26:
            g = hs // 3
            turn_pe(pe, TURN_MEM, lambda tile, k: mem_tok[:, (k // 4) % 2, tile, (k % 4) * P:(k % 4 + 1) * P],
                    lambda g: pe.wait_ge(s[f"mem_loaded{g // 2 % 2}"], 16 * (g // 4 + 1)), range(g, g + 1))
        if blk - 1 in HEADS_OF:
            n, stage, _ = HEADS_OF[blk - 1]
            heads_pe(pe, n, stage, hs, blk - 1)
        if blk == BLK_MEM1 and hs >= 12 and hs % 2 == 0 and hs < 28:
            g = (hs - 12) // 2
            turn_pe(pe, TURN_X1, whole(xr), lambda g: pe.wait_ge(s["x_added"], g // 2 + 1), range(g, g + 1))
        if blk == BLK_PLE and hs == 2:
            pe.wait_ge(s["vec_loaded"], VEC_PLE)
            pe.wait_ge(s["turned_lo"], TURN_X2)
            for k in range(2):
                for tile in range(TT):
                    mm = pe.transpose(QA[:, k * S + tile * P:k * S + (tile + 1) * P], p_tok[:, tile, k * P:(k + 1) * P], ident)
            mm.then_inc(s["e_done"], 1)
        if BLK_PLE <= blk < BLK_PLE + 4 and hs == 16:
            n = blk - BLK_PLE
            pe.wait_ge(s["pT_ready"], 1)
            pe.wait_ge(s["wpp_loaded"], 16 * (n + 1))
            reach(pe, s["pr_ready"], n)
            for tile in range(TT):
                for k in range(2):
                    mm = pe.matmul((RA, RB)[tile][:, :], pT[:, k, tile * P:(tile + 1) * P], wpp[:, k], start=(k == 0), stop=(k == 1))
            mm.then_inc(s["e_done"], 1)
        pool_pe(pe, blk, hs)
        attention(at, lambda i, h, second: attend_pe(pe, i, h, second))

    def before_pe(pe, blk):
        if blk == BLK_Y + 1:
            pe.wait_ge(s["ub_lo_done"], 4)
        if blk == BLK_Y:
            pe.wait_ge(s["oa_lo_done"], HEADS)
        if blk == BLK_MEM0:
            pe.wait_ge(s["turned_lo"], TURN_MEM + 8)
        if blk == BLK_OUT:
            pe.wait_ge(s["turned_lo"], TURN_X1)
        if blk == BLK_PLE:
            pe.wait_ge(s["turned_lo"], TURN_X2)
        if blk in (BLK_IN0, BLK_KV):
            done, base, per = (s["x_added"], TURN_X2, 4) if blk == BLK_IN0 else (s["ln_done"], TURN_H1, 0)
            turn_pe(pe, base, whole(xr), lambda g: pe.wait_ge(done, per + g // 2 + 1))
            pe.wait_ge(s["turned_lo"], base + 8)
        if blk in (BLK_OUT0, BLK_OUT1):
            base, per = (TURN_M0, 0) if blk == BLK_OUT0 else (TURN_M1, 4)
            turn_pe(pe, base, whole(mo), lambda g: pe.wait_ge(s["mixed_ready"], per + g // 2 + 1))
            pe.wait_ge(s["turned_lo"], base + 8)

    def columns_of(blk):
        if BLK_Y <= blk < BLK_MEM0:
            return (oa_hi, oa_lo) if blk % 2 == BLK_Y % 2 else (ub_hi, ub_lo)
        if BLK_MEM0 <= blk < BLK_OUT or BLK_MEM1 <= blk < BLK_PLE:
            return mem_hi, mem_lo
        return in_hi, in_lo

    def tail_pe(pe):
        for blk in range(BLK_GB, BLK_END):
            before_pe(pe, blk)
            pe_block(pe, blk, blk % 2, *columns_of(blk), lambda hs: beside_pe(pe, blk, hs))

    def beside_act(act, blk, hs):
        at = 32 * (blk - BLK_GB) + hs
        done = blk - 1
        if blk == BLK_GB:
            group_act(act, KC - 1, 1, hs)
        if BLK_GB <= done < BLK_GB + 4 and hs == 3:
            n = done - BLK_GB
            act.wait_ge(psum_free, done + 1)
            act.activation(gb[:, :, cols(n)], gb[:, :, cols(n)], ACT.Tanh, scale=0.5).then_inc(s["gb_tanh"], 1)
        if at == LN0:
            act.wait_ge(s["pads_ready"], 2)
        norm_b_act(act, at)
        if BLK_Y + 2 <= blk <= BLK_Y + 8 and blk % 2 == BLK_Y % 2 and hs == 4:
            n = (blk - BLK_Y) // 2 - 1
            turn_act(act, TURN_Y3 if n == 3 else TURN_Y, in_hi, factor=0.5, groups=range(2 * n, 2 * n + 2))
        if blk == BLK_Y + 7 and hs >= 2 and hs % 3 == 2 and hs < 26:
            g = hs // 3
            turn_act(act, TURN_MEM, mem_hi, groups=range(g, g + 1))
        if done in HEADS_OF:
            n, stage, to = HEADS_OF[done]
            heads_act(act, n, stage, to, hs, done)
        if done in (BLK_MEM0 + 1, BLK_MEM1 + 1, BLK_KV + 3, BLK_KV + 4, BLK_KV + 5) and hs == 0:
            ready(act, done)
            for tile in range(TT):
                if done < BLK_PLE:
                    to = mv[:, int(done > BLK_OUT), tile]
                else:
                    to = v1_[:, tile, cols(done - BLK_KV - 3)]
                ins = act.activation(to, pairs[done % 2][:, tile], ACT.Copy)
            ins.then_inc(psum_free, 1)
        if BLK_OUT <= done < BLK_OUT + 4:
            n = done - BLK_OUT
            if hs == 0:
                ready(act, done)
                for tile in range(TT):
                    ins = act.activation(mo[:, tile, cols(n)], pairs[done % 2][:, tile], ACT.Copy)
                ins.then_inc(psum_free, 1)
            if hs == 2:
                act.wait_ge(psum_free, done + 1)
                for tile in range(TT):
                    reach(act, s["mo_summed"], 2 * n + tile)
                    act.activation(junk2[:, :], mo[:, tile, cols(n)], ACT.Square,
                                   accum_out=small[:, 8 + 4 * tile + n:9 + 4 * tile + n]).then_inc(s["mo_summed"], 1)
        if blk == BLK_MEM1 and hs >= 12 and hs % 2 == 0 and hs < 28:
            g = (hs - 12) // 2
            turn_act(act, TURN_X1, in_hi, groups=range(g, g + 1))
        if blk == BLK_PLE and hs == 2:
            act.wait_ge(s["e_done"], 1)
            act.activation(pT[:, :, :].rearrange("p k n -> p (k n)"), QA[:, :], ACT.Copy).then_inc(s["pT_ready"], 1)
        if BLK_PLE <= done < BLK_PLE + 3:
            ple_act(act, done, hs)
        if BLK_IN0 <= done < BLK_IN0 + 3 and hs == 0:
            ready(act, done)
            for tile in range(TT):
                ins = act.activation(u0[:, tile, cols(done - BLK_IN0)], pairs[done % 2][:, tile], ACT.Copy)
            ins.then_inc(psum_free, 1)
        pool_act(act, blk, hs)
        if done in GATES and blk not in (BLK_OUT0, BLK_OUT1):
            gate_act(act, done, hs)
        attention(at, lambda i, h, second: attend_act(act, i, h, second))

    def ple_act(act, done, hs):
        n = done - BLK_PLE
        if hs == 0:
            act.wait_ge(psum_ready, done + 1)
            act.wait_ge(psum_free, done)
            reach(act, s["pr_ready"], n)
            for tile in range(TT):
                ins = act.activation(stage0[:, tile], pairs[done % 2][:, tile], ACT.Tanh, scale=0.5)
            ins.then_inc(psum_free, 1)
        if hs == 2:
            act.wait_ge(s["pr_ready"], n + 1)
            for tile in range(TT):
                act.wait_ge(s["mo_summed"], 8 + 2 * n + tile)
                act.activation(junk2[:, :], mo[:, tile, cols(n)], ACT.Square,
                               accum_out=small[:, 8 + 4 * tile + n:9 + 4 * tile + n]).then_inc(s["mo_summed"], 1)

    def before_act(act, blk):
        if blk == BLK_IN0:
            for hs in (0, 2):
                ple_act(act, blk - 1, hs)
            turn_act(act, TURN_X2, in_hi)
        if blk in (BLK_OUT0, BLK_OUT1):
            gate_act(act, blk - 1, 0)
            turn_act(act, TURN_M0 if blk == BLK_OUT0 else TURN_M1, in_hi, factor=0.5)
        if blk == BLK_KV:
            ln_act(act, 0)
            turn_act(act, TURN_H1, in_hi)

    def tail_act(act):
        for blk in range(BLK_GB, BLK_END):
            before_act(act, blk)
            act_block(act, blk, lambda hs: beside_act(act, blk, hs))
        ln_act(act, 1)

    def beside_dve(dve, blk, hs):
        at = 32 * (blk - BLK_GB) + hs
        done = blk - 1
        if blk == BLK_GB:
            group_dve(dve, KC - 1, 1, hs)
        if BLK_GB <= done < BLK_GB + 4 and hs == 0:
            n = done - BLK_GB
            ready(dve, done)
            if n == 0:
                dve.wait_ge(s["vec_loaded"], VEC_GATE)
                dve.wait_ge(s["u_ready"], KC)
            for tile in range(TT):
                ins = dve.tensor_tensor(gb[:, tile, cols(n)], pairs[done % 2][:, tile], vec[:, cols(n)], ALU.add)
            ins.then_inc(psum_free, 1)
        norm_b_dve(dve, at)
        if BLK_Y <= done < BLK_MEM0 and hs == 0:
            n, second = divmod(done - BLK_Y, 2)
            ready(dve, done)
            if not second:
                dve.wait_ge(s[f"gat_loaded{n % 2}"], 16 * (n // 2 + 1))
                if n:
                    dve.wait_ge(s["turned"], TURN_Y + 2 * n)
                for tile in range(TT):
                    ins = dve.scalar_tensor_tensor(mix[:, tile], gat[:, n % 2, tile], 1.0, pairs[done % 2][:, tile],
                                                   ALU.add, ALU.mult)
                ins.then_inc(psum_free, 1)
            else:
                dve.wait_ge(s["gb_tanh"], 4)
                for tile in range(TT):
                    ins = dve.scalar_tensor_tensor(gb[:, tile, cols(n)], gb[:, tile, cols(n)], 1.0, pairs[done % 2][:, tile],
                                                   ALU.add, ALU.mult)
                ins.then_inc(psum_free, 1)
                dve.wait_ge(psum_free, done + 1)
                dve.tensor_tensor(mix[:, :, :], mix[:, :, :], gb[:, :, cols(n)], ALU.add).then_inc(s["mix_ready"], 1)
        if BLK_Y + 2 <= blk <= BLK_Y + 8 and blk % 2 == BLK_Y % 2 and hs == 4:
            n = (blk - BLK_Y) // 2 - 1
            turn_dve(dve, TURN_Y3 if n == 3 else TURN_Y, in_hi, in_lo, factor=0.5, groups=range(2 * n, 2 * n + 2))
        if blk == BLK_Y + 7 and hs >= 2 and hs % 3 == 2 and hs < 26:
            g = hs // 3
            turn_dve(dve, TURN_MEM, mem_hi, mem_lo, groups=range(g, g + 1))
        if BLK_OUT <= done < BLK_OUT + 4 and hs == 4:
            n = done - BLK_OUT
            dve.wait_ge(s["mo_summed"], 2 * n + 2)
            if n == 0:
                dve.wait_ge(s["vec_loaded"], VEC_POST)
            dve.tensor_tensor(mo[:, :, cols(n)], mo[:, :, cols(n)], tiles(vec[:, cols(n)], NB), ALU.mult)\
               .then_inc(s["mo_scaled"], 1)
        if blk == BLK_MEM1 and hs == 8:
            rms_dve(dve, 0)
        if blk == BLK_MEM1 and hs >= 12 and hs % 2 == 0 and hs < 28:
            g = (hs - 12) // 2
            turn_dve(dve, TURN_X1, in_hi, in_lo, groups=range(g, g + 1))
        if BLK_PLE <= done < BLK_PLE + 3:
            ple_dve(dve, done, hs)
        pool_dve(dve, blk, hs)
        if done in GATES and blk not in (BLK_OUT0, BLK_OUT1):
            gate_dve(dve, done, hs)
        if hs == 0 and (BLK_OUT0 <= done < BLK_OUT0 + 3 or BLK_OUT1 <= done):
            layer = int(done >= BLK_OUT1)
            res_dve(dve, done, done - (BLK_OUT0, BLK_OUT1)[layer], layer)
        attention(at, lambda i, h, second: attend_dve(dve, i, h, second))

    def ple_dve(dve, done, hs):
        n = done - BLK_PLE
        if hs == 1:
            dve.wait_ge(psum_free, done + 1)
            dve.wait_ge(s["e_done"], n + 2)
            dve.wait_ge(s["x_added"], 4)
            for tile in range(TT):
                ins = dve.scalar_tensor_tensor(mo[:, tile, cols(n)], stage0[:, tile], 1.0, (RA, RB)[tile][:, :],
                                               ALU.add, ALU.mult)
            ins.then_inc(s["pr_ready"], 1)
        if hs == 4:
            dve.wait_ge(s["mo_summed"], 8 + 2 * n + 2)
            if n == 0:
                dve.wait_ge(s["vec_loaded"], VEC_PLE)
            dve.tensor_tensor(mo[:, :, cols(n)], mo[:, :, cols(n)], tiles(vec[:, cols(n)], NB), ALU.mult)\
               .then_inc(s["mo_scaled"], 1)

    def before_dve(dve, blk):
        if blk == BLK_IN0:
            for hs in (1, 4):
                ple_dve(dve, blk - 1, hs)
            rms_dve(dve, 1)
            turn_dve(dve, TURN_X2, in_hi, in_lo)
        if blk in (BLK_OUT0, BLK_OUT1):
            gate_dve(dve, blk - 1, 1)
            turn_dve(dve, TURN_M0 if blk == BLK_OUT0 else TURN_M1, in_hi, in_lo, factor=0.5)
        if blk == BLK_KV:
            res_dve(dve, blk - 1, 3, 0)
            ln_dve(dve, 0, LNV[0])
            turn_dve(dve, TURN_H1, in_hi, in_lo)

    def tail_dve(dve):
        for blk in range(BLK_GB, BLK_END):
            before_dve(dve, blk)
            dve_block(dve, blk, lambda hs: beside_dve(dve, blk, hs))
        res_dve(dve, BLK_END - 1, 3, 1)
        ln_dve(dve, 1, LNV[1])

    def tail_pool(pool):
        def load(to, src, done):
            pool.dma_start(to, src).then_inc(s[done], 16)

        def after(**counts):
            for n, count in counts.items():
                reach(pool, s[n], count)

        row_of = lambda a: a.partition_broadcast(P)
        mem = lambda c: load(mem_tok[:, c % 2], tokens(t["mem_2"][0])[:, :, cols(c)], f"mem_loaded{c % 2}")
        gate = lambda n: load(gat[:, n % 2], tokens(gate_a_dram)[:, :, cols(n)], f"gat_loaded{n % 2}")
        after(u_ready=KC, gate_a_stored=16 * KC)
        load(vec[:, :], row_of(t["b_gate"][0, D:2 * D]), "vec_loaded")
        pool.wait_ge(psum_free, BLK_GB + 4)
        mem(0)
        mem(1)
        after(ub_hi_done=4, ln_gated=4)
        gate(0)
        gate(1)
        for n in (2, 3):
            pool.wait_ge(psum_free, BLK_Y + 2 * (n - 2) + 1)
            gate(n)
        for c in (2, 3):
            after(turned=TURN_MEM + 2 * (c - 1))
            mem(c)
        pool.wait_ge(psum_ready, BLK_MEM0)
        load(xr[:, :, :], tokens(t["x"][0]), "vec_loaded")
        after(turned=TURN_MEM + 8)
        load(vec[:, :], row_of(t["g_post"][0]), "vec_loaded")
        rms_pool(pool, 0)
        after(mo_scaled=4)
        load(vec[:, :], row_of(t["g_ple"][0]), "vec_loaded")
        load(p_tok[:, :, :], tokens(t["p"][0, 0]), "vec_loaded")
        for n in range(4):
            after(e_done=n + 1 if n else 0)
            load(wpp[:, :, :], t["w_ple_proj"][0].rearrange("(k p) n -> p k n", p=P)[:, :, cols(n)], "wpp_loaded")
        rms_pool(pool, 1)
        after(mo_scaled=8)
        load(bands[:, :, :, :], t["pool_bands"].rearrange("(t p) g n -> p t g n", p=P), "vec_loaded")
        for g in range(len(POOL_WINDOWS)):
            after(e_done=5, pool_done=POOLED + g if g else 0)
            load(pool_w[:, :, :], t["pool_w_2"][0, g].rearrange("(k p) n -> p k n", p=P), "pw_loaded")
            if g >= 2:
                after(pw_ready=g - 1)
            load(pscale[:, g % 2], row_of(t["pool_scale_2"][0, g * PG:(g + 1) * PG]), "pw_loaded")
        after(pool_done=POOLED)
        load(vec[:, :], row_of(t["ln_g_2"][0]), "vec_loaded")
        load(ln_b0[:, :], row_of(t["ln_b_2"][0]), "vec_loaded")
        ln_pool(pool, 0)
        after(pool_done=POOLED + 4, ln_gain=4)
        load(mask[:, :, :], t["causal_mask"].rearrange("(t p) n -> p t n", p=P), "vec_loaded")
        after(mixed_ready=8, attended=len(ATTEND))
        load(ln_vec_a[:, 0], row_of(t["ln_g_2"][1]), "vec_loaded")
        load(ln_vec_a[:, 1], row_of(t["ln_b_2"][1]), "vec_loaded")
        ln_pool(pool, 1)

    SOURCES = [(w_in, COL_GATE_B + n * NB) for n in range(4)]
    SOURCES += [(square[w], n * NB) for n in range(4) for w in ("w_br_a", "w_br_b")]
    SOURCES += [(w_mem[0], n * NB) for n in range(2)] + [(square["w_out"], n * NB) for n in range(4)]
    SOURCES += [(w_mem[1], n * NB) for n in range(2)] + [(square["w_ple_gate"], n * NB) for n in range(4)]
    SOURCES += [(w_in2[0], n * NB) for n in IN_ORDER] + [(w_out2[0], n * NB) for n in range(4)]
    SOURCES += [(w_kv, n * NB) for n in range(6)]
    SOURCES += [(w_in2[1], n * NB) for n in IN_ORDER] + [(w_out2[1], n * NB) for n in range(4)]
    assert len(SOURCES) == BLK_END - BLK_GB

    def tail_sp(sp):
        for blk, (w, col) in enumerate(SOURCES, BLK_GB):
            load_block(sp, blk, w, col)
            if blk == BLK_GB:
                group_out_sp(sp, KC - 1)
        for c in range(4):
            sp.wait_ge(s["ln_done"], 4 + c + 1)
            sp.dma_start(tokens(out)[:, :, cols(c)], xr[:, :, cols(c)]).then_inc(s["out_stored"], 16)
        sp.wait_ge(s["out_stored"], 64)

    block = ctx.enter_context(nc.Block())

    @block.sync
    def _(sp):
        start_sp(sp)
        load_heads(sp, 0, COL_A, 0)
        decays_sp(sp)
        load_heads(sp, 1, COL_A, 1)
        with sp.Fori(2, HEADS) as h:
            load_heads(sp, BLK_A + h, COL_A, h)
        for j in range(2):
            load_heads(sp, BLK_B + j, COL_B, j)
        group_sp(sp, 0)
        with sp.Fori(2, KC) as j:
            load_heads(sp, BLK_B + j, COL_B, j)
            group_out_sp(sp, j - 2)
            group_sp(sp, j - 1)
        group_out_sp(sp, KC - 2)
        group_sp(sp, KC - 1)
        tail_sp(sp)

    def beside(parts):
        def between(hs):
            for f, n, par in parts:
                f(n, par, hs)
        return between

    @block.tensor
    def _(pe):
        keys = lambda h, par, hs: keys_pe(pe, h, par, hs)
        rule = lambda h, par, hs: rule_pe(pe, h, par, hs)
        group = lambda j, par, hs: group_pe(pe, j, par, hs)
        start_pe(pe)
        pe_block(pe, 0, 0, in_hi, in_lo, lambda hs: decays_pe(pe) if hs == 8 else None)
        pe.wait_ge(s["head_ready"], 1)
        pe_block(pe, 1, 1, in_hi, in_lo, beside([(keys, 0, 0)]))
        heads = lambda h, i: pe_block(pe, h + i, i, in_hi, in_lo, beside([(rule, h + (i - 2), i), (keys, h + (i - 1), 1 - i)]))
        heads(2, 0)
        heads(2, 1)
        with pe.Fori(4, HEADS, 2) as h:
            for i in range(2):
                heads(h, i)
        pe_block(pe, BLK_B, 0, in_hi, in_lo, beside([(rule, HEADS - 2, 0), (keys, HEADS - 1, 1)]))
        pe_block(pe, BLK_B + 1, 1, in_hi, in_lo, beside([(rule, HEADS - 1, 1), (group, 0, 0)]))
        groups = lambda j, i: pe_block(pe, BLK_B + j + i, i, in_hi, in_lo, beside([(group, j + (i - 1), 1 - i)]))
        groups(2, 0)
        groups(2, 1)
        with pe.Fori(4, KC, 2) as j:
            for i in range(2):
                groups(j, i)
        tail_pe(pe)

    @block.scalar
    def _(act):
        keys = lambda h, par, hs: keys_act(act, h, par, hs)
        rule = lambda h, par, hs: rule_act(act, h, par, hs)
        group = lambda j, par, hs: group_act(act, j, par, hs)
        start_act(act)
        for q in range(AHEAD):
            hi_piece(act, 0, q)
        act_block(act, 0, lambda hs: decays_act(act) if hs == 8 else None)
        act_block(act, 1, beside([(keys, 0, 0)]))
        heads = lambda h, i: act_block(act, h + i, beside([(rule, h + (i - 2), i), (keys, h + (i - 1), 1 - i)]))
        heads(2, 0)
        heads(2, 1)
        with act.Fori(4, HEADS, 2) as h:
            for i in range(2):
                heads(h, i)
        act_block(act, BLK_B, beside([(rule, HEADS - 2, 0), (keys, HEADS - 1, 1)]))
        act_block(act, BLK_B + 1, beside([(rule, HEADS - 1, 1), (group, 0, 0)]))
        groups = lambda j, i: act_block(act, BLK_B + j + i, beside([(group, j + (i - 1), 1 - i)]))
        groups(2, 0)
        groups(2, 1)
        with act.Fori(4, KC - 2, 2) as j:
            for i in range(2):
                groups(j, i)
        for j in (KC - 2, KC - 1):
            act_block(act, BLK_B + j, beside([(group, j - 1, 1 - j % 2)]))
        tail_act(act)

    @block.vector
    def _(dve):
        keys = lambda h, par, hs: keys_dve(dve, h, par, hs)
        rule = lambda h, par, hs: rule_dve(dve, h, par, hs)
        group = lambda j, par, hs: group_dve(dve, j, par, hs)
        start_dve(dve)
        for q in range(AHEAD):
            lo_piece(dve, 0, q)
        dve_block(dve, 0, lambda hs: decays_dve(dve) if hs == 8 else None)
        dve.wait_ge(s["gc_stored"], 32)
        dve.wait_ge(s["pads_ready"], 3)
        dve_block(dve, 1, beside([(keys, 0, 0)]))
        heads = lambda h, i: dve_block(dve, h + i, beside([(rule, h + (i - 2), i), (keys, h + (i - 1), 1 - i)]))
        heads(2, 0)
        heads(2, 1)
        with dve.Fori(4, HEADS, 2) as h:
            for i in range(2):
                heads(h, i)
        dve_block(dve, BLK_B, beside([(rule, HEADS - 2, 0), (keys, HEADS - 1, 1)]))
        dve_block(dve, BLK_B + 1, beside([(rule, HEADS - 1, 1), (group, 0, 0)]))
        groups = lambda j, i: dve_block(dve, BLK_B + j + i, beside([(group, j + (i - 1), 1 - i)]))
        groups(2, 0)
        groups(2, 1)
        with dve.Fori(4, KC, 2) as j:
            for i in range(2):
                groups(j, i)
        tail_dve(dve)

    @block.gpsimd
    def _(pool):
        start_pool(pool)
        pool.wait_ge(s["head_ready"], 1)
        keys_pool(pool, 0, 0)
        for h in range(1, 3):
            keys_pool(pool, h, h % 2)
            rule_pool(pool, h - 1)
        with pool.Fori(3, HEADS - 1, 2) as h:
            for i in range(2):
                keys_pool(pool, h + i, 1 - i)
                rule_pool(pool, h + (i - 1))
        keys_pool(pool, HEADS - 1, 1)
        rule_pool(pool, HEADS - 2)
        group_pool(pool, 0, 0)
        rule_pool(pool, HEADS - 1)
        group_pool(pool, 1, 1)
        group_pool(pool, 2, 0)
        with pool.Fori(3, KC - 1, 2) as j:
            for i in range(2):
                group_pool(pool, j + i, 1 - i)
        group_pool(pool, KC - 1, 1)
        tail_pool(pool)


def kernel(**inputs):
    import concourse.bacc as bacc
    from concourse.bass_utils import run_bass_kernel_spmd

    nc = bacc.Bacc("TRN2", target_bir_lowering=False, num_devices=1)
    inputs = dict(inputs, shape_constants=shape_constants(), pool_bands=pool_bands(), causal_mask=causal_mask())
    arrays, t = {}, {}
    for name, value in inputs.items():
        arrays[f"in_{name}_dram"] = np.ascontiguousarray(value)
        t[name] = nc.dram_tensor(f"in_{name}_dram", value.shape, F32, kind="ExternalInput").ap()
    out = nc.dram_tensor("out_0_dram", (1, S, D), F32, kind="ExternalOutput").ap()
    with ExitStack() as ctx:
        program(nc, t, out[0], ctx)
    return run_bass_kernel_spmd(nc, [arrays], core_ids=[0]).results[0]["out_0_dram"]
```

```python
from contextlib import ExitStack

import numpy as np

import concourse.bass as bass
from concourse import mybir

F32 = mybir.dt.float32
F32R = mybir.dt.float32r
ALU = mybir.AluOpType
ACT = mybir.ActivationFunctionType
AX = mybir.AxisListType

P = 128
D = 2048
S = 256
TT = S // P
KC = D // P
NB = 512
UNITS = 4
UK = KC // UNITS
AHEAD = 6
HEADS = 16
LEVELS = 7
SHORT, LONG = 4, 31
EPS, LN_EPS = 1e-6, 1e-5
RSQ = float(P) ** -0.5
POOL_WINDOWS = (2, 4, 8, 16)
PG = 384
MEM_HEADS = 4
MOBA_HEADS = 12
ALPHA = 4.0 ** 0.25

COL_A, COL_BA, COL_B = 0, 4 * D, 4 * D + 2 * HEADS
COL_GATE_B = COL_B + 4 * D

BLK_A = 0
BLK_B = BLK_A + HEADS
BLK_GB = BLK_B + KC
BLK_Y = BLK_GB + 4
BLK_MEM_K0 = BLK_Y + 8
BLK_OUT = BLK_MEM_K0 + 1
BLK_MEM_V0 = BLK_OUT + 4
BLK_PLE = BLK_MEM_V0 + 1
BLK_MEM1 = BLK_PLE + 4
BLK_IN0 = BLK_MEM1 + 2
BLK_OUT0 = BLK_IN0 + 8
BLK_KV = BLK_OUT0 + 4
BLK_IN1 = BLK_KV + 6
BLK_OUT1 = BLK_IN1 + 8
BLK_END = BLK_OUT1 + 4

IN_ORDER = (0, 1, 2, 6, 3, 4, 5, 7)

CH_GPRE, CH_LNG, CH_LNB, CH_BDW = 0, 16, 32, 48
CH_SHORT = 64
CH_LONG = CH_SHORT + SHORT * 3 * HEADS
CH_END = CH_LONG + LONG * KC
ROW_TILES = [(CH_GPRE, 64), (CH_SHORT, 96), (CH_SHORT + 96, 96)] + [(CH_LONG + 124 * i, 124) for i in range(4)]

K_ID, K_TRI, K_ONE, K_LVL = 0, P, 2 * P, 3 * P
K_LVL0T = K_LVL + LEVELS * P
K_END = K_LVL0T + P


def shape_constants():
    i = np.arange(P)
    levels = []
    for m in [1 << n for n in range(LEVELS)]:
        same = (i[:, None] // (2 * m)) == (i[None, :] // (2 * m))
        levels.append(-(same & ((i[:, None] // m) % 2 == 1) & ((i[None, :] // m) % 2 == 0)).astype(np.float32))
    parts = [np.eye(P), i[:, None] <= i[None, :], np.ones((P, P)), *levels, levels[0].T]
    return np.ascontiguousarray(np.concatenate([np.asarray(x, np.float32) for x in parts], axis=1))


def pool_bands():
    s = np.arange(S)
    out = np.zeros((S, len(POOL_WINDOWS), S), np.float32)
    for g, w in enumerate(POOL_WINDOWS):
        lo = np.maximum(s + 1 - w, 0)
        inside = (s[:, None] >= lo[None, :]) & (s[:, None] <= s[None, :])
        out[:, g, :] = inside / (s + 1 - lo)[None, :].astype(np.float32) - np.eye(S, dtype=np.float32)
    return out


def causal_mask():
    i = np.arange(S)
    return np.where(i[None, :] <= i[:, None], 0.0, -1e30).astype(np.float32)


def program(nc, t, out, ctx):
    w_in = t["w_in"][0].rearrange("(k p) n -> p k n", p=P)
    square = {n: t[n][0].rearrange("(k p) n -> p k n", p=P) for n in ("w_br_a", "w_br_b", "w_out", "w_ple_gate")}
    w_in2 = [t["w_in_2"][i].rearrange("(k p) n -> p k n", p=P) for i in range(2)]
    w_out2 = [t["w_out_2"][i].rearrange("(k p) n -> p k n", p=P) for i in range(2)]
    w_mem = [t["w_mem_kv_2"][i].rearrange("(k p) n -> p k n", p=P) for i in range(2)]
    w_kv = t["w_kv_shared_2"].rearrange("(k p) n -> p k n", p=P)
    tokens = lambda a: a.rearrange("(t p) n -> p t n", p=P)

    gc_rows = nc.dram_tensor("gc_rows", (TT * HEADS, P), F32, kind="Internal").ap()
    gate_a_dram = nc.dram_tensor("gate_a_tanh", (S, D), F32, kind="Internal").ap()

    kib = 1024
    spot = [17 * kib]

    def sb(name, shape, dt=F32):
        h = nc.alloc_sbuf_tensor_at(name, shape, dt, offset=spot[0])
        spot[0] += (4 * int(np.prod(shape[1:])) + 31) // 32 * 32
        assert spot[0] <= nc.sbuf_usable_end
        return h

    def region(size):
        at = spot[0]
        spot[0] += size
        return at

    raw = sb("raw", [P, UNITS, UK, NB])
    w_hi = sb("w_hi", [P, 2, UK, NB], F32R)
    w_lo = sb("w_lo", [P, 2, UK, NB], F32R)
    in_hi = sb("in_hi", [P, KC, S], F32R)
    in_lo = sb("in_lo", [P, KC, S], F32R)
    at_a = spot[0]
    oa_hi = sb("oa_hi", [P, KC, S], F32R)
    oa_lo = sb("oa_lo", [P, KC, S], F32R)
    at_b = spot[0]
    ub_hi = sb("ub_hi", [P, KC, S], F32R)
    ub_lo = sb("ub_lo", [P, KC, S], F32R)
    const = sb("const", [P, K_END])
    chan = sb("chan", [P, CH_END])
    head_all = sb("head_all", [P, HEADS, 12])
    half_g = sb("half_g", [P, P])
    small = sb("small", [P, 64])
    x_rms = small[:, 4:4 + TT]
    eps_col = sb("eps_col", [P, 1])
    halfpow = sb("halfpow", [P, 8])
    pool_eps = sb("pool_eps", [P, 8])
    at_g = spot[0]

    spot[0] = at_a
    x_tok = sb("x_tok", [P, TT, D])
    x_squares = sb("x_squares", [P, D])
    spot[0] = at_b
    rows = sb("rows", [P, len(ROW_TILES), P])
    ba_raw = sb("ba_raw", [P, KC, 2 * HEADS])
    ba_hi = sb("ba_hi", [P, KC, 2 * HEADS], F32R)
    ba_lo = sb("ba_lo", [P, KC, 2 * HEADS], F32R)
    sgl = sb("sgl", [P, 16, 32])
    dt_b = sb("dt_b", [P, HEADS])
    alog_b = sb("alog_b", [P, HEADS])
    gcT = sb("gcT", [TT * HEADS, P])
    baT = sb("baT", [2 * HEADS, S])

    spot[0] = at_b
    gc_b = sb("gc_b", [P, TT * HEADS, P])
    proj = sb("proj", [P, TT, NB])
    conv_in = sb("conv_in", [P, 3, SHORT - 1 + S + 1])
    conv = sb("conv", [P, 3, S])
    conv_th = sb("conv_th", [P, 3, S])
    dexp = sb("dexp", [P, TT, P])
    spot[0] = at_g
    tok = sb("tok", [P, TT, 3, P])
    scaled = sb("scaled", [P, TT, 3, P])
    z_th = sb("z_th", [P, TT, P])
    z2 = sb("z2", [P, TT, P])
    at_kq = spot[0]
    kq = sb("kq", [P, 2, TT, 3, P])
    at_ap = spot[0]
    ap = sb("ap", [P, 2, TT, 2, P])
    vb = sb("vb", [P, 2, TT, P])
    kend = sb("kend", [P, 2, P])
    zs = sb("zs", [P, 2, TT, P])
    tri = sb("tri", [P, 2 * TT, P])
    xm = sb("xm", [P, TT, P])
    xmT = sb("xmT", [P, TT, P])
    vn0, s1, r1, vn1, oq = (sb(n, [P, P]) for n in ("vn0", "s1", "r1", "vn1", "oq"))
    o_t = sb("o_t", [P, TT, P])
    og = sb("og", [P, TT, P])
    junk = sb("junk", [P, P])
    cw = sb("cw", [P, SHORT, 3])
    hst = sb("hst", [P, 2, 12])
    ssq = sb("ssq", [P, 2 * TT])
    rn = sb("rn", [P, 2 * TT])
    scal = sb("scal", [P, 12])
    oss = sb("oss", [P, TT])
    orn = sb("orn", [P, TT])

    at_free = spot[0]

    spot[0] = at_b
    zb = sb("zb", [P, KC, S])
    ub = sb("ub", [P, KC, S])
    spot[0] = at_g
    bproj = sb("bproj", [P, TT, NB])
    upad = sb("upad", [P, 2, LONG - 1 + S + 2])
    z2b = sb("z2b", [P, TT, P])
    bg = sb("bg", [P, P])
    cwl = sb("cwl", [P, LONG + 1])
    assert spot[0] <= at_kq
    spot[0] = at_kq
    acc = sb("acc", [P, 2, S])
    glu2 = sb("glu2", [P, TT, P])
    assert spot[0] <= at_kq + 4 * TT * 3 * P
    spot[0] = at_ap
    tap = sb("tap", [P, 2, S])
    assert spot[0] <= at_ap + 4 * TT * 2 * P
    spot[0] = at_free
    bth = sb("bth", [P, TT, 3, P])
    acc_p = sb("acc_p", [P, S])
    assert spot[0] <= nc.sbuf_usable_end

    spot[0] = at_a
    mem_hi = sb("mem_hi", [P, KC, S], F32R)
    mem_lo = sb("mem_lo", [P, KC, S], F32R)
    spot[0] = at_a
    u0 = sb("u0", [P, TT, 3 * NB])
    pooled = sb("pooled", [P, 12, S])
    mqT0 = sb("mqT0", [P, MEM_HEADS, S])
    pscale = sb("pscale", [P, 2, PG])
    spot[0] = at_a
    kT1 = sb("kT1", [P, MOBA_HEADS, S])
    v1_ = sb("v1_", [P, TT, 3 * NB])
    mqT1 = sb("mqT1", [P, MEM_HEADS, S])
    stage1 = sb("stage1", [P, TT, NB])
    assert spot[0] <= at_b
    spot[0] = at_a
    ln_b0 = sb("ln_b0", [P, D])
    spot[0] = at_a
    ln_vec_a = sb("ln_vec_a", [P, 2, D])
    spot[0] = at_b
    mo = sb("mo", [P, TT, D])
    xr = sb("xr", [P, TT, D])
    spot[0] = at_g
    gb = sb("gb", [P, TT, D])
    spot[0] = at_g
    mkT = sb("mkT", [P, 2, MEM_HEADS, S])
    mv = sb("mv", [P, 2, TT, NB])
    at_v = spot[0]
    vec = sb("vec", [P, D])
    spot[0] = at_v
    mem_tok = sb("mem_tok", [P, 2, TT, NB])
    spot[0] = at_v
    bands = sb("bands", [P, TT, len(POOL_WINDOWS), S])
    at_s = spot[0]
    spot[0] = at_v
    pool_w_odd = sb("pool_w_odd", [P, 3, PG])
    spot[0] = at_v
    qT1 = sb("qT1", [P, MOBA_HEADS, S])
    mask = sb("mask", [P, TT, S])
    spot[0] = at_s
    sqb = sb("sqb", [P, 2, 4, S])
    mub = sb("mub", [P, S])
    rsb = sb("rsb", [P, S])
    spot[0] = at_s
    gat = sb("gat", [P, 2, TT, NB])
    mix = sb("mix", [P, TT, NB])
    spot[0] = at_s
    stage0 = sb("stage0", [P, TT, NB])
    wpp = sb("wpp", [P, 2, NB])
    pT = sb("pT", [P, 2, S])
    p_tok = sb("p_tok", [P, TT, S])
    spot[0] -= 4 * TT * S
    junk2 = sb("junk2", [P, NB])
    spot[0] = at_s + 4096
    pool_w_even = sb("pool_w_even", [P, 3, PG])
    sc = sb("sc", [P, TT, S])
    probT = sb("probT", [P, TT, S])
    st = sb("st", [P, 96])
    sgst = st[:, 0:TT * 4 * 6]
    assert spot[0] <= nc.sbuf_usable_end

    pool_w = [pool_w_even, pool_w_odd]

    pairs = [nc.alloc_psum_tensor(f"pair{i}", [P, TT, NB], F32) for i in range(2)]
    QA, QB, RA, RB = (nc.alloc_psum_tensor(n, [P, NB], F32) for n in ("QA", "QB", "RA", "RB"))

    ident, triu = const[:, K_ID:K_ID + P], const[:, K_TRI:K_TRI + P]
    ones = const[:, K_ONE:K_ONE + P]
    level = lambda l: const[:, K_LVL + l * P:K_LVL + (l + 1) * P]
    level0T = const[:, K_LVL0T:K_LVL0T + P]

    def both(x):
        return x.unsqueeze(1).broadcast_to([P, TT, P])

    sem = nc.alloc_semaphore
    w_loaded = [sem(f"w_loaded{u}") for u in range(UNITS)]
    hi_ready = [sem(f"hi_ready{u}") for u in range(UNITS)]
    lo_ready = [sem(f"lo_ready{u}") for u in range(UNITS)]
    chunk_used = sem("chunk_used")
    psum_ready, psum_free = sem("psum_ready"), sem("psum_free")
    names = ("rows_in", "x_in", "ba_in", "rows_cols", "chan_ready", "x_ss", "x_rms", 
             "ba_split", "ba_lo_ready", "ba_done", "baT_copied", "ba_out", "sg_v", "sg_a", "sg_exp", "sg_g", "gc_done", "gc_copied",
             "gcT_done", "gc_stored", "head_ready", "turned", "turned_hi", "turned_lo",
             "pads_ready", "zs_ready", 
             "z_tanh", "z_gated", "qkv_cols", "conv_filled", "cw_staged", "head_staged", "conv_tanh", "silu_done",
             "qkv_tokens", "tok_ready", "norms_summed", "pool_a", "scal_ready", "tok_scaled", "kq_cols", "kq_ready",
             "decay_diff", "decay_exp", "decay_ready", "kk_done", "ap_ready",
             "a_turned", "t_first", "v0_done", "v0_ready", "s1_done", "s1_ready", "kq_s1", "r1_ready", "oq_ready",
             "v1_done", "v1_ready", "o_done", "o_ready", "o_summed", "pool_b", "xT_ready", "og_ready", "og_cols", "oa_hi_done",
             "oa_lo_done",
             "bg_loaded", "gate_biased", "b_tanh", "glu_ready", "gate_a_stored", "b_cols", "b_cols_taken", "cwl_staged",
             "pool_taps", "u_summed", "u_ready", )
    s = {n: sem(n) for n in names}
    tap_done, x_done, x_ready, d_done, t_ready = (sem(n) for n in ("tap_done", "x_done", "x_ready", "d_done", "t_ready"))
    for n in ("gb_tanh", "mean_ready", "centred", "squared", "var_done", 
              "rstd_ready", "ln_scaled", "ln_affine", "ln_tanh", "ln_silu", "ln_gated", "ub_hi_done", "ub_lo_done",
              "gat_loaded0", "gat_loaded1", "mix_ready", "mem_loaded0", "mem_loaded1", "vec_loaded", "heads_done",
              "heads_taken", "mo_summed", "mo_scaled", "ms_ready", "ms_rms", "x_added",
              "pT_ready", "wpp_loaded", "e_done", "pr_ready", 
              "pool_done", "pool_ready", "pw_loaded0", "pw_loaded1", "pw_ready",
              "scores_done", "scores_masked", "max_ready", "probs_ready", "sums_inverted", "probs_turned",
              "probT_ready", "attended", "att_ready", "gate_tanh", "mixed_ready", "stats_ready",
              "aggr_ready", "ln_pool", "ln_gain", "ln_done", "out_stored", ):
        s[n] = sem(n)
    long_tap = [sem(f"long_tap{i}") for i in range(2)]
    tap_ready = [sem(f"tap_ready{i}") for i in range(2)]

    def reach(eng, which, value):
        if not isinstance(value, int) or value > 0:
            eng.wait_ge(which, value)

    def load_unit(sp, blk, u, src):
        reach(sp, lo_ready[u], UK * blk)
        sp.dma_start(raw[:, u], src).then_inc(w_loaded[u], 16)

    def load_heads(sp, blk, base, h):
        for u in range(UNITS):
            reach(sp, lo_ready[u], UK * blk)
            for g in range(4):
                sp.dma_start(raw[:, u, :, g * P:(g + 1) * P],
                             w_in[:, u * UK:(u + 1) * UK, bass.ds(base + g * D + h * P, P)]).then_inc(w_loaded[u], 16)

    def load_block(sp, blk, w, col):
        for u in range(UNITS):
            load_unit(sp, blk, u, w[:, u * UK:(u + 1) * UK, bass.ds(col, NB)])

    def loads(blk):
        if isinstance(blk, int) and blk >= BLK_GB:
            return 64 * BLK_GB + 16 * (blk + 1 - BLK_GB)
        return 64 * blk + 64

    def hi_piece(act, blk, q):
        u = q // UK
        if q % UK == 0:
            act.wait_ge(w_loaded[u], loads(blk))
        if q == 2 * UK - 1:
            reach(act, psum_ready, blk)
        elif q < 2 * UK:
            reach(act, chunk_used, (KC - 1) * blk - (2 * UK - 2 - q))
        else:
            reach(act, chunk_used, (KC - 1) * blk + q - 2 * UK + 1)
        act.activation(w_hi[:, u % 2, q % UK], raw[:, u, q % UK], ACT.Copy).then_inc(hi_ready[u], 1)

    def lo_piece(dve, blk, q):
        u = q // UK
        dve.wait_ge(hi_ready[u], UK * blk + q % UK + 1)
        dve.tensor_tensor(w_lo[:, u % 2, q % UK], raw[:, u, q % UK], w_hi[:, u % 2, q % UK].bitcast(F32), ALU.subtract)\
           .then_inc(lo_ready[u], 1)

    def ahead(blk, q, step):
        if q + AHEAD < KC:
            return blk, q + AHEAD
        return blk + 1, q + AHEAD - KC

    def pe_block(pe, blk, parity, hi, lo, between=None):
        for q in range(KC):
            u = q // UK
            if q == 0:
                reach(pe, psum_free, blk - 1)
            pe.wait_ge(lo_ready[u], UK * blk + q % UK + 1)
            for tile in range(TT):
                o = pairs[parity][:, tile]
                xh, xl = hi[:, q, tile * P:(tile + 1) * P], lo[:, q, tile * P:(tile + 1) * P]
                wh, wl = w_hi[:, u % 2, q % UK], w_lo[:, u % 2, q % UK]
                pe.matmul(o, xh, wh, start=(q == 0), stop=False)
                pe.matmul(o, xh, wl, start=False, stop=False)
                mm = pe.matmul(o, xl, wh, start=False, stop=(q == KC - 1))
                if tile == TT - 1 and q == KC - 1:
                    mm.then_inc(psum_ready, 1)
                elif tile == TT - 1:
                    mm.then_inc(chunk_used, 1)
                if between:
                    between(2 * q + tile)

    def act_block(act, blk, between=None):
        for q in range(KC):
            b, p = ahead(blk, q, 1)
            if not isinstance(b, int) or b < BLK_END:
                hi_piece(act, b, p)
            if between:
                between(2 * q)
                between(2 * q + 1)

    EVENLY = tuple(range(1, 2 * KC, 2))
    BESIDE_HEADS = (1, 3, 6, 7, 9, 12, 13, 15, 18, 19, 21, 23, 25, 27, 29, 31)

    def dve_block(dve, blk, between=None, pieces_after=EVENLY):
        for hs in range(2 * KC):
            if between:
                between(hs)
            if hs in pieces_after:
                b, p = ahead(blk, pieces_after.index(hs), 1)
                if not isinstance(b, int) or b < BLK_END:
                    lo_piece(dve, b, p)

    def keys_pe(pe, h, par, hs):
        if hs == 3:
            pe.wait_ge(psum_free, BLK_A + h + 1)
            reach(pe, s["ap_ready"], h)
            for c in range(3):
                bank = QB[:, 0:S] if c == 2 else QA[:, c * S:(c + 1) * S]
                for tile in range(TT):
                    mm = pe.transpose(bank[:, tile * P:(tile + 1) * P], proj[:, tile, c * P:(c + 1) * P], ident)
            mm.then_inc(s["qkv_cols"], 1)
        if hs == 17:
            pe.wait_ge(s["silu_done"], h + 1)
            for tile in range(TT):
                for c in range(3):
                    mm = pe.transpose((QA, QB)[tile][:, c * P:(c + 1) * P], conv[:, c, tile * P:(tile + 1) * P], ident)
            mm.then_inc(s["qkv_tokens"], 1)
        if hs == 27:
            pe.wait_ge(s["tok_scaled"], h + 1)
            for tile in range(TT):
                for c in range(3):
                    mm = pe.transpose((QA, QB)[tile][:, c * P:(c + 1) * P], scaled[:, tile, c], ident)
            mm.then_inc(s["kq_cols"], 1)
        if hs == 29:
            pe.wait_ge(s["kq_ready"], h + 1)
            for tile in range(TT):
                mm = pe.matmul(QA[:, tile * S:(tile + 1) * S], kq[:, par, tile, 2],
                               kq[:, par, tile, 0:2].rearrange("p c n -> p (c n)"), start=True, stop=True)
            mm.then_inc(s["kk_done"], 1)

    def keys_act(act, h, par, hs):
        if hs == 0:
            act.wait_ge(psum_ready, h + 1 + BLK_A)
            reach(act, s["qkv_cols"], h)
            reach(act, s["z_gated"], h)
            act.activation(proj[:, 0], pairs[par][:, 0], ACT.Copy, scale=x_rms[:, 0:1])
            act.activation(proj[:, 1], pairs[par][:, 1], ACT.Copy, scale=x_rms[:, 1:2]).then_inc(psum_free, 1)
        if hs == 1:
            act.wait_ge(psum_free, BLK_A + h + 1)
            act.activation(z_th[:, :, :], proj[:, :, 3 * P:4 * P], ACT.Tanh, scale=0.5).then_inc(s["z_tanh"], 1)
        if hs == 5:
            act.wait_ge(s["conv_filled"], h + 1)
            act.wait_ge(s["cw_staged"], h + 1)
            reach(act, s["qkv_tokens"], h)
            for c in range(3):
                ins = act.activation(conv[:, c], conv_in[:, c, 0:S], ACT.Copy, scale=cw[:, 0, c:c + 1])
            ins.then_inc(tap_done, 1)
        if hs == 13:
            act.wait_ge(tap_done, SHORT * h + SHORT)
            act.activation(conv_th[:, :, :], conv[:, :, :], ACT.Tanh, scale=0.5).then_inc(s["conv_tanh"], 1)
        if hs == 17:
            act.wait_ge(s["qkv_tokens"], h + 1)
            act.activation(tok[:, 0].rearrange("p c n -> p (c n)"), QA[:, 0:3 * P], ACT.Copy)
            act.activation(tok[:, 1].rearrange("p c n -> p (c n)"), QB[:, 0:3 * P], ACT.Copy)\
               .then_inc(s["tok_ready"], 1)
        if hs == 18:
            act.wait_ge(s["tok_ready"], h + 1)
            reach(act, s["scal_ready"], h)
            for tile in range(TT):
                for c in range(2):
                    reach(act, s["norms_summed"], 4 * h + 2 * tile + c)
                    act.activation(junk[:, :], tok[:, tile, c], ACT.Square,
                                   accum_out=ssq[:, 2 * tile + c:2 * tile + c + 1]).then_inc(s["norms_summed"], 1)
        if hs == 27:
            act.wait_ge(s["kq_cols"], h + 1)
            for tile in range(TT):
                ins = act.activation(kq[:, par, tile].rearrange("p c n -> p (c n)"), (QA, QB)[tile][:, 0:3 * P], ACT.Copy)
            ins.then_inc(s["kq_ready"], 1)
        if hs == 4:
            act.wait_ge(s["decay_diff"], h + 1)
            act.activation(dexp[:, :, :], dexp[:, :, :], ACT.Exp).then_inc(s["decay_exp"], 1)

    def keys_pool(pool, h, par):
        reach(pool, s["og_ready"], h - 1)
        reach(pool, s["ap_ready"], h - 1)
        reach(pool, tap_done, SHORT * h)
        pool.tensor_copy(hst[:, par], head_all[:, bass.ds(h, 1)].rearrange("p a n -> p (a n)"))\
            .then_inc(s["head_staged"], 1)
        taps = chan[:, CH_SHORT:CH_LONG].rearrange("p (k c h) -> p k c h", k=SHORT, c=3)
        pool.tensor_copy(cw[:, :, :], taps[:, :, :, bass.ds(h, 1)].rearrange("p k c a -> p k (c a)"))\
            .then_inc(s["cw_staged"], 1)
        pool.wait_ge(s["norms_summed"], 4 * h + 4)
        reach(pool, s["tok_scaled"], h)
        pool.tensor_tensor(rn[:, :], ssq[:, :], pool_eps[:, 0:4], ALU.add).then_inc(s["pool_a"], 1)
        pool.wait_ge(s["pool_a"], 2 * h + 1)
        pool.tensor_tensor(rn[:, :], rn[:, :], halfpow[:, 0:4], ALU.pow).then_inc(s["pool_a"], 1)
        pool.wait_ge(s["head_staged"], h + 1)
        pool.wait_ge(s["pool_a"], 2 * h + 2)
        r = rn[:, :].rearrange("p (t c) -> p c t", t=TT)
        pool.tensor_tensor(scal[:, 2:4], r[:, 1], hst[:, par, 0:2], ALU.mult)
        pool.tensor_tensor(scal[:, 4:6], r[:, 1], hst[:, par, 10:12], ALU.mult)
        pool.tensor_scalar(scal[:, 0:2], r[:, 0], RSQ, None, ALU.mult)
        pool.tensor_copy(scal[:, 6:8], r[:, 1]).then_inc(s["scal_ready"], 1)

    def keys_dve(dve, h, par, hs):
        if hs == 2:
            dve.wait_ge(s["z_tanh"], h + 1)
            dve.scalar_tensor_tensor(z2[:, :, :], z_th[:, :, :], 1.0, proj[:, :, 3 * P:4 * P], ALU.add, ALU.mult)\
               .then_inc(s["z_gated"], 1)
        if hs == 3:
            dve.wait_ge(s["head_staged"], h + 1)
            reach(dve, s["decay_ready"], h)
            for tile in range(TT):
                ins = dve.tensor_scalar(dexp[:, tile], gc_b[:, bass.ds(tile * HEADS + h, 1)].rearrange("p a n -> p (a n)"),
                                        hst[:, par, 4 + tile:5 + tile], 0.0, ALU.subtract, ALU.min)
            ins.then_inc(s["decay_diff"], 1)
        if hs == 4:
            dve.wait_ge(s["qkv_cols"], h + 1)
            dve.tensor_copy(conv_in[:, 0:2, SHORT - 1:SHORT - 1 + S], QA[:, :].rearrange("p (c n) -> p c n", c=2))
            dve.tensor_copy(conv_in[:, 2, SHORT - 1:SHORT - 1 + S], QB[:, 0:S]).then_inc(s["conv_filled"], 1)
        if hs in (7, 10, 13):
            k = (hs - 4) // 3
            dve.wait_ge(tap_done, SHORT * h + k)
            for c in range(3):
                ins = dve.scalar_tensor_tensor(conv[:, c], conv_in[:, c, k:k + S], cw[:, k, c:c + 1], conv[:, c], ALU.mult, ALU.add)
            ins.then_inc(tap_done, 1)
        if hs == 8:
            dve.wait_ge(s["decay_exp"], h + 1)
            dve.tensor_tensor(dexp[:, :, :], dexp[:, :, :], both(triu), ALU.mult).then_inc(s["decay_ready"], 1)
        if hs == 11:
            dve.wait_ge(s["z_gated"], h + 1)
            reach(dve, s["og_ready"], h - 1)
            dve.tensor_tensor(zs[:, par], z2[:, :, :], both(half_g[:, :]), ALU.mult).then_inc(s["zs_ready"], 1)
        if hs == 15:
            dve.wait_ge(s["conv_tanh"], h + 1)
            dve.scalar_tensor_tensor(conv[:, :, :], conv_th[:, :, :], 1.0, conv[:, :, :], ALU.add, ALU.mult)\
               .then_inc(s["silu_done"], 1)
        if hs == 23:
            dve.wait_ge(s["tok_ready"], h + 1)
            dve.wait_ge(s["scal_ready"], h + 1)
            reach(dve, s["kq_cols"], h)
            for tile in range(TT):
                for c, part, at in ((0, 1, 2), (1, 0, 0), (2, 1, 6)):
                    dve.tensor_scalar(scaled[:, tile, c], tok[:, tile, part], scal[:, at + tile:at + tile + 1], None, ALU.mult)
                dve.tensor_scalar(vb[:, par, tile], tok[:, tile, 2], hst[:, par, 2 + tile:3 + tile], None, ALU.mult)
            dve.tensor_scalar(kend[:, par], tok[:, 0, 1], scal[:, 4:5], None, ALU.mult).then_inc(s["tok_scaled"], 1)
        if hs == 29:
            dve.wait_ge(s["kk_done"], h + 1)
            dve.wait_ge(s["decay_ready"], h + 1)
            dve.tensor_tensor(ap[:, par].rearrange("p t c n -> p c t n"),
                              QA[:, :].rearrange("p (t c n) -> p c t n", t=TT, c=2),
                              dexp[:, :, :].unsqueeze(1).broadcast_to([P, 2, TT, P]), ALU.mult).then_inc(s["ap_ready"], 1)

    X_AT = {2: 1, 5: 2, 8: 3, 11: 4, 14: 5, 17: 6}
    T_AT = {3: 1, 6: 2, 9: 3, 12: 4, 15: 5, 18: 6}

    def every(h, l):
        return LEVELS * h + l + 1

    def inner(h, l):
        return (LEVELS - 1) * h + l

    def rule_pe(pe, h, par, hs):
        if hs == 0:
            pe.wait_ge(s["ap_ready"], h + 1)
            reach(pe, s["oa_lo_done"], h)
            for tile in range(TT):
                mm = pe.transpose(RA[:, tile * P:(tile + 1) * P], ap[:, par, tile, 0], ident)
            mm.then_inc(s["a_turned"], 1)
        if hs in X_AT:
            l = X_AT[hs]
            pe.wait_ge(t_ready, every(h, l - 1))
            for tile in range(TT):
                mm = pe.matmul(RA[:, tile * P:(tile + 1) * P], ap[:, par, tile, 0], tri[:, tile], start=True, stop=True)
            mm.then_inc(x_done, 1)
        if hs == 2:
            pe.wait_ge(t_ready, every(h, 0))
            pe.matmul(RB[:, :], ident, tri[:, :, :].rearrange("p t n -> p (t n)"), start=True, stop=True)
        if hs in T_AT:
            l = T_AT[hs]
            pe.wait_ge(x_ready, every(h, l))
            for tile in range(TT):
                if l < LEVELS - 1:
                    pe.matmul(RB[:, tile * P:(tile + 1) * P], tri[:, TT + tile], xm[:, tile], start=False, stop=True,
                              skip_group_check=True)
                mm = pe.matmul(RB[:, (TT + tile) * P:(TT + tile + 1) * P], xm[:, tile], tri[:, TT + tile], start=False, stop=True,
                               skip_group_check=True)
            mm.then_inc(d_done, 1)
        if hs == 19:
            pe.wait_ge(t_ready, every(h, LEVELS - 1))
            pe.matmul(RA[:, 0:P], tri[:, TT], vb[:, par, 0], start=True, stop=True).then_inc(s["v0_done"], 1)
        if hs == 21:
            pe.wait_ge(s["v0_ready"], h + 1)
            pe.matmul(RA[:, P:2 * P], kend[:, par], vn0[:, :], start=True, stop=True).then_inc(s["s1_done"], 1)
            pe.matmul(RB[:, 0:P], ap[:, par, 0, 1], vn0[:, :], start=True, stop=True)
        if hs == 22:
            pe.wait_ge(s["s1_ready"], h + 1)
            pe.matmul(RB[:, P:2 * P], kq[:, par, 1, 1], s1[:, :], start=True, stop=True)
            pe.matmul(RA[:, 0:P], kq[:, par, 1, 0], s1[:, :], start=True, stop=True).then_inc(s["kq_s1"], 1)
        if hs == 23:
            pe.wait_ge(s["r1_ready"], h + 1)
            pe.matmul(RA[:, P:2 * P], tri[:, TT + 1], r1[:, :], start=True, stop=True).then_inc(s["v1_done"], 1)
        if hs == 24:
            pe.wait_ge(s["v1_ready"], h + 1)
            pe.wait_ge(s["oq_ready"], h + 1)
            pe.matmul(RB[:, 2 * P:3 * P], ap[:, par, 1, 1], vn1[:, :], start=True, stop=True).then_inc(s["o_done"], 1)
        if hs == 31:
            pe.wait_ge(s["og_ready"], h + 1)
            for tile in range(TT):
                mm = pe.transpose(RA[:, tile * P:(tile + 1) * P], og[:, tile], ident)
            mm.then_inc(s["og_cols"], 1)

    def rule_act(act, h, par, hs):
        if hs in T_AT:
            l = T_AT[hs]
            a = 0 if l < LEVELS - 1 else TT
            act.wait_ge(d_done, inner(h, l))
            act.activation(tri[:, a:].rearrange("p t n -> p (t n)"), RB[:, a * P:], ACT.Copy).then_inc(t_ready, 1)
        if hs == 19:
            act.wait_ge(s["v0_done"], h + 1)
            act.activation(vn0[:, :], RA[:, 0:P], ACT.Copy).then_inc(s["v0_ready"], 1)
        if hs == 21:
            act.wait_ge(s["s1_done"], h + 1)
            act.activation(s1[:, :], RA[:, P:2 * P], ACT.Copy).then_inc(s["s1_ready"], 1)
        if hs == 22:
            act.wait_ge(s["kq_s1"], h + 1)
            act.activation(oq[:, :], RB[:, P:2 * P], ACT.Copy, scale=hst[:, par, 7:8]).then_inc(s["oq_ready"], 1)
        if hs == 23:
            act.wait_ge(s["v1_done"], h + 1)
            act.activation(vn1[:, :], RA[:, P:2 * P], ACT.Copy).then_inc(s["v1_ready"], 1)
        if hs == 25:
            act.wait_ge(s["o_ready"], h + 1)
            reach(act, s["pool_b"], 2 * h)
            for tile in range(TT):
                reach(act, s["o_summed"], 2 * h + tile)
                act.activation(og[:, tile], o_t[:, tile], ACT.Square, accum_out=oss[:, tile:tile + 1])\
                   .then_inc(s["o_summed"], 1)
        if hs == 31:
            act.wait_ge(s["og_cols"], h + 1)
            act.activation(oa_hi[:, bass.ds(h, 1)].rearrange("p a n -> p (a n)"), RA[:, 0:S], ACT.Copy)\
               .then_inc(s["oa_hi_done"], 1)

    def rule_pool(pool, h):
        pool.wait_ge(s["o_summed"], 2 * h + 2)
        reach(pool, s["og_ready"], h)
        pool.tensor_tensor(orn[:, :], oss[:, :], pool_eps[:, 4:6], ALU.add).then_inc(s["pool_b"], 1)
        pool.wait_ge(s["pool_b"], 2 * h + 1)
        pool.tensor_tensor(orn[:, :], orn[:, :], halfpow[:, 0:2], ALU.pow).then_inc(s["pool_b"], 1)

    def rule_dve(dve, h, par, hs):
        if hs == 0:
            dve.wait_ge(s["ap_ready"], h + 1)
            reach(dve, s["v1_done"], h)
            dve.tensor_tensor(xmT[:, :, :], ap[:, par, :, 0], both(level0T), ALU.mult).then_inc(s["xT_ready"], 1)
            dve.wait_ge(s["a_turned"], h + 1)
            dve.tensor_tensor(xm[:, :, :], RA[:, 0:S].rearrange("p (t n) -> p t n", t=TT), both(level(0)), ALU.mult)\
               .then_inc(x_ready, 1)
            dve.wait_ge(s["xT_ready"], h + 1)
            dve.tensor_tensor(tri[:, TT:2 * TT], xmT[:, :, :], both(ident), ALU.add).then_inc(s["t_first"], 1)
            dve.wait_ge(x_ready, every(h, 0))
            dve.tensor_tensor(tri[:, 0:TT], xm[:, :, :], both(ident), ALU.add).then_inc(t_ready, 1)
        if hs in X_AT:
            l = X_AT[hs]
            dve.wait_ge(x_done, inner(h, l))
            dve.tensor_tensor(xm[:, :, :], RA[:, 0:S].rearrange("p (t n) -> p t n", t=TT), both(level(l)), ALU.mult)\
               .then_inc(x_ready, 1)
        if hs == 22:
            dve.wait_ge(s["kq_s1"], h + 1)
            dve.scalar_tensor_tensor(r1[:, :], RA[:, 0:P], hst[:, par, 9:10], vb[:, par, 1], ALU.mult, ALU.add)\
               .then_inc(s["r1_ready"], 1)
        if hs == 24:
            dve.wait_ge(s["o_done"], h + 1)
            dve.tensor_copy(o_t[:, 0], RB[:, 0:P])
            dve.tensor_tensor(o_t[:, 1], RB[:, 2 * P:3 * P], oq[:, :], ALU.add).then_inc(s["o_ready"], 1)
        if hs == 29:
            dve.wait_ge(s["pool_b"], 2 * h + 2)
            for tile in range(TT):
                ins = dve.scalar_tensor_tensor(og[:, tile], o_t[:, tile], orn[:, tile:tile + 1], zs[:, par, tile],
                                               ALU.mult, ALU.mult)
            ins.then_inc(s["og_ready"], 1)
        if hs == 31:
            dve.wait_ge(s["oa_hi_done"], h + 1)
            to = bass.ds(h, 1)
            dve.tensor_tensor(oa_lo[:, to].rearrange("p a n -> p (a n)"), RA[:, 0:S],
                              oa_hi[:, to].rearrange("p a n -> p (a n)").bitcast(F32), ALU.subtract)\
               .then_inc(s["oa_lo_done"], 1)

    POOL_TAPS = 8
    DVE_TAPS = LONG - POOL_TAPS

    def group_sp(sp, j):
        if isinstance(j, int) and j == 0:
            sp.wait_ge(s["zs_ready"], HEADS)
        reach(sp, s["gate_biased"], j)
        sp.dma_start(bg[:, :], t["b_gate"][0:1, bass.ds(j * P, P)].rearrange("a n -> (a n)").partition_broadcast(P))\
          .then_inc(s["bg_loaded"], 16)

    def group_out_sp(sp, j):
        sp.wait_ge(s["b_tanh"], j + 1)
        sp.dma_start(tokens(gate_a_dram)[:, :, bass.ds(j * P, P)], bth[:, :, 2]).then_inc(s["gate_a_stored"], 16)

    def group_pe(pe, j, par, hs):
        if hs == 5:
            pe.wait_ge(s["glu_ready"], j + 1)
            reach(pe, s["b_cols_taken"], j)
            for n, src in enumerate((glu2, z2b)):
                for tile in range(TT):
                    mm = pe.transpose(QA[:, n * S + tile * P:n * S + (tile + 1) * P], src[:, tile], ident)
            mm.then_inc(s["b_cols"], 1)

    def group_act(act, j, par, hs):
        if hs == 0:
            act.wait_ge(psum_ready, BLK_B + j + 1)
            reach(act, s["glu_ready"], j)
            if isinstance(j, int) and j == 0:
                act.wait_ge(s["tok_scaled"], HEADS)
                act.wait_ge(s["kq_cols"], HEADS)
            act.activation(bproj[:, 0], pairs[par][:, 0], ACT.Copy, scale=x_rms[:, 0:1])
            act.activation(bproj[:, 1], pairs[par][:, 1], ACT.Copy, scale=x_rms[:, 1:2]).then_inc(psum_free, 1)
        if hs == 1:
            act.wait_ge(s["gate_biased"], j + 1)
            reach(act, s["gate_a_stored"], 16 * j)
            act.activation(bth[:, :, :, :].rearrange("p t c n -> p t (c n)"), bproj[:, :, P:NB], ACT.Tanh, scale=0.5)\
               .then_inc(s["b_tanh"], 1)
        if hs == 5:
            act.wait_ge(s["b_cols"], j + 1)
            reach(act, s["u_ready"], j - 1)
            act.activation(upad[:, par, LONG - 1:LONG - 1 + S], QA[:, 0:S], ACT.Copy, scale=0.5)
            act.activation(zb[:, bass.ds(j, 1)].rearrange("p a n -> p (a n)"), QA[:, S:2 * S], ACT.Copy, scale=0.25)\
               .then_inc(s["b_cols_taken"], 1)
        if 8 <= hs < 8 + 2 * POOL_TAPS and hs % 2 == 0:
            n = (hs - 8) // 2
            k = DVE_TAPS + n
            if n == 0:
                if isinstance(j, int) and j == 0:
                    act.wait_ge(s["oa_lo_done"], HEADS - 1)
                act.wait_ge(s["b_cols_taken"], j + 1)
                act.wait_ge(s["cwl_staged"], j + 1)
            reach(act, s["pool_taps"], (POOL_TAPS - 1) * j + (max(n - 2, 1) if n >= 2 else 0))
            act.activation(tap[:, n % 2], upad[:, par, k:k + S], ACT.Copy, scale=cwl[:, k:k + 1])\
               .then_inc(tap_ready[n % 2], 1)

    def group_pool(pool, j, par):
        if isinstance(j, int) and j == 0:
            pool.wait_ge(s["tok_scaled"], HEADS)
            pool.wait_ge(s["kq_cols"], HEADS)
            pool.memset(upad[:, :, 0:LONG - 1], 0.0).then_inc(s["pads_ready"], 1)
            pool.wait_ge(s["zs_ready"], HEADS)
        reach(pool, s["u_summed"], j)
        reach(pool, s["pool_taps"], (POOL_TAPS - 1) * j)
        taps = chan[:, CH_LONG:CH_END].rearrange("p (k g) -> p k g", g=KC)
        pool.tensor_copy(cwl[:, LONG:LONG + 1], chan[:, bass.ds(CH_BDW + j, 1)])
        pool.tensor_copy(cwl[:, 0:LONG], taps[:, :, bass.ds(j, 1)].rearrange("p k a -> p (k a)")).then_inc(s["cwl_staged"], 1)
        reach(pool, s["u_ready"], j)
        for n in range(1, POOL_TAPS):
            if n == 1:
                pool.wait_ge(tap_ready[0], POOL_TAPS // 2 * j + 1)
            else:
                pool.wait_ge(s["pool_taps"], (POOL_TAPS - 1) * j + n - 1)
            pool.wait_ge(tap_ready[n % 2], POOL_TAPS // 2 * j + n // 2 + 1)
            pool.tensor_tensor(acc_p[:, :], tap[:, 0] if n == 1 else acc_p[:, :], tap[:, n % 2], ALU.add)\
                .then_inc(s["pool_taps"], 1)

    def group_dve(dve, j, par, hs):
        if hs == 0:
            dve.wait_ge(psum_free, BLK_B + j + 1)
            dve.wait_ge(s["bg_loaded"], 16 * j + 16)
            dve.tensor_tensor(bproj[:, :, 3 * P:NB], bproj[:, :, 3 * P:NB], both(bg[:, :]), ALU.add)\
               .then_inc(s["gate_biased"], 1)
        if hs == 2:
            dve.wait_ge(s["b_tanh"], j + 1)
            if isinstance(j, int) and j == 0:
                dve.wait_ge(s["zs_ready"], HEADS)
                dve.wait_ge(s["oa_lo_done"], HEADS - 1)
                dve.wait_ge(s["pads_ready"], 4)
            reach(dve, s["b_cols"], j)
            dve.scalar_tensor_tensor(glu2[:, :, :], bth[:, :, 0], 1.0, bproj[:, :, 0:P], ALU.add, ALU.mult)
            dve.scalar_tensor_tensor(z2b[:, :, :], bth[:, :, 1], 1.0, bproj[:, :, 2 * P:3 * P], ALU.add, ALU.mult)\
               .then_inc(s["glu_ready"], 1)
        if 6 <= hs < 6 + DVE_TAPS:
            k = hs - 6
            src, a = upad[:, par, k:k + S], acc[:, k % 2]
            if k == 0:
                dve.wait_ge(s["b_cols_taken"], j + 1)
                dve.wait_ge(s["cwl_staged"], j + 1)
                reach(dve, s["u_ready"], j)
                dve.tensor_scalar(a, src, cwl[:, 0:1], cwl[:, LONG:LONG + 1], ALU.mult, ALU.add).then_inc(long_tap[0], 1)
            elif k == 1:
                dve.tensor_scalar(a, src, cwl[:, 1:2], None, ALU.mult).then_inc(long_tap[1], 1)
            else:
                n = (DVE_TAPS + 1 - k % 2) // 2
                dve.wait_ge(long_tap[k % 2], n * j + k // 2)
                dve.scalar_tensor_tensor(a, src, cwl[:, k:k + 1], a, ALU.mult, ALU.add).then_inc(long_tap[k % 2], 1)
        if hs == 30:
            dve.wait_ge(long_tap[0], (DVE_TAPS + 1) // 2 * (j + 1))
            dve.wait_ge(long_tap[1], DVE_TAPS // 2 * (j + 1))
            dve.tensor_tensor(acc[:, 0], acc[:, 0], acc[:, 1], ALU.add).then_inc(s["u_summed"], 1)
        if hs == 31:
            dve.wait_ge(s["u_summed"], j + 1)
            dve.wait_ge(s["pool_taps"], (POOL_TAPS - 1) * (j + 1))
            dve.tensor_tensor(ub[:, bass.ds(j, 1)].rearrange("p a n -> p (a n)"), acc[:, 0], acc_p[:, :], ALU.add)\
               .then_inc(s["u_ready"], 1)

    BANKS = (QA, QB, RA, RB)

    def turn_pe(pe, base, src, first_wait, groups=range(KC // 2)):
        for g in groups:
            first_wait(g)
            reach(pe, s["turned_lo"], base + g - 3)
            for k in (2 * g, 2 * g + 1):
                for tile in range(TT):
                    mm = pe.transpose(BANKS[(base + g) % 4][:, (k % 2) * S + tile * P:(k % 2) * S + (tile + 1) * P],
                                      src(tile, k), ident)
            mm.then_inc(s["turned"], 1)

    def turn_act(act, base, hi, scale=None, factor=1.0, groups=range(KC // 2)):
        for g in groups:
            act.wait_ge(s["turned"], base + g + 1)
            if scale is None:
                ins = act.activation(hi[:, 2 * g:2 * g + 2].rearrange("p k n -> p (k n)"), BANKS[(base + g) % 4][:, :], ACT.Copy, scale=factor)
            else:
                for k in range(2):
                    ins = act.activation(hi[:, 2 * g + k], BANKS[(base + g) % 4][:, k * S:(k + 1) * S], ACT.Copy,
                                         scale=scale[:, 2 * g + k:2 * g + k + 1])
            ins.then_inc(s["turned_hi"], 1)

    def turn_dve(dve, base, hi, lo, scale=None, factor=1.0, groups=range(KC // 2)):
        for g in groups:
            dve.wait_ge(s["turned_hi"], base + g + 1)
            if scale is None:
                ins = dve.scalar_tensor_tensor(lo[:, 2 * g:2 * g + 2].rearrange("p k n -> p (k n)"), BANKS[(base + g) % 4][:, :], factor,
                                               hi[:, 2 * g:2 * g + 2].rearrange("p k n -> p (k n)").bitcast(F32),
                                               ALU.mult, ALU.subtract)
            else:
                for k in range(2):
                    ins = dve.scalar_tensor_tensor(lo[:, 2 * g + k], BANKS[(base + g) % 4][:, k * S:(k + 1) * S],
                                                   scale[:, 2 * g + k:2 * g + k + 1], hi[:, 2 * g + k].bitcast(F32),
                                                   ALU.mult, ALU.subtract)
            ins.then_inc(s["turned_lo"], 1)

    def start_sp(sp):
        sp.dma_start(const[:, K_ID:K_ID + P], t["shape_constants"][:, K_ID:K_ID + P]).then_inc(s["rows_in"], 16)
        vecs = [t[n].rearrange("a (r c) -> (a r) c", c=P) for n in ("g_pre", "ln_g", "ln_b", "b_dw")]
        for i, v in enumerate(vecs):
            sp.dma_start(rows[16 * i:16 * (i + 1), 0], v).then_inc(s["rows_in"], 16)
        short = t["w_conv_qkv"][0].rearrange("k (r c) -> (k r) c", c=P)
        long = t["w_dw"][0].rearrange("k (r c) -> (k r) c", c=P)
        for i, (at, n) in enumerate(ROW_TILES[1:], 1):
            src = short[at - CH_SHORT:at - CH_SHORT + n] if at < CH_LONG else long[at - CH_LONG:at - CH_LONG + n]
            sp.dma_start(rows[0:n, i], src).then_inc(s["rows_in"], 16)
        sp.dma_start(ba_raw[:, :, :], w_in[:, :, COL_BA:COL_BA + 2 * HEADS]).then_inc(s["ba_in"], 16)
        sp.dma_start(const[:, P:], t["shape_constants"][:, P:]).then_inc(s["ba_in"], 16)
        sp.dma_start(dt_b[:, :], t["dt_bias"][0].partition_broadcast(P)).then_inc(s["ba_in"], 16)
        sp.dma_start(alog_b[:, :], t["a_log"][0].partition_broadcast(P)).then_inc(s["ba_in"], 16)
        sp.dma_start(half_g[:, :], t["g_dn_out"][0].partition_broadcast(P)).then_inc(s["ba_in"], 16)

    def decays_sp(sp):
        sp.wait_ge(s["gc_copied"], 3)
        sp.dma_start(gc_rows, gcT[:, :]).then_inc(s["gc_stored"], 16)
        sp.wait_ge(s["gc_stored"], 16)
        sp.wait_ge(s["head_ready"], 1)
        sp.wait_ge(s["ba_done"], 2)
        sp.dma_start(gc_b[:, :, :], gc_rows.partition_broadcast(P)).then_inc(s["gc_stored"], 16)

    def start_pe(pe):
        pe.wait_ge(s["rows_in"], 16 * (4 + len(ROW_TILES)))
        for i, (at, n) in enumerate(ROW_TILES):
            reach(pe, s["chan_ready"], i - 1)
            pe.transpose((QA, QB)[i % 2][:, 0:n], rows[0:n, i], ident[0:n, 0:n]).then_inc(s["rows_cols"], 1)
        def first(g):
            if g == 0:
                pe.wait_ge(s["x_in"], 32)
                pe.wait_ge(s["chan_ready"], len(ROW_TILES))
        turn_pe(pe, 0, lambda tile, k: x_tok[:, tile, k * P:(k + 1) * P], first)

    def decays_first_pe(pe):
        pe.wait_ge(s["turned_lo"], KC // 2)
        pe.wait_ge(s["ba_lo_ready"], 1)
        for k in range(KC):
            pe.matmul(RA[0:2 * HEADS, 0:S], ba_hi[:, k], in_hi[:, k], start=(k == 0), stop=False)
            pe.matmul(RA[0:2 * HEADS, 0:S], ba_lo[:, k], in_hi[:, k], start=False, stop=False)
            mm = pe.matmul(RA[0:2 * HEADS, 0:S], ba_hi[:, k], in_lo[:, k], start=False, stop=(k == KC - 1))
        mm.then_inc(s["ba_done"], 1)

    def decays_turn_pe(pe):
        pe.wait_ge(s["baT_copied"], 1)
        for tile in range(TT):
            mm = pe.transpose(RB[:, tile * 2 * HEADS:(tile + 1) * 2 * HEADS], baT[:, tile * P:(tile + 1) * P],
                              ident[0:2 * HEADS, 0:2 * HEADS])
        mm.then_inc(s["ba_done"], 1)

    def decays_pe(pe):
        pe.wait_ge(s["sg_g"], 1)
        pe.matmul(QA[:, 0:2 * HEADS], triu, sgl[:, 15], start=True, stop=True)
        pe.matmul(QB[:, 0:2 * HEADS], ones, sgl[:, 15], start=True, stop=True).then_inc(s["gc_done"], 1)
        pe.wait_ge(s["gc_copied"], 1)
        pe.transpose(QA[0:TT * HEADS, 0:P], sgl[:, 0], ident).then_inc(s["gcT_done"], 1)

    def start_act(act):
        for tile in range(TT):
            act.dma_start(x_tok[:, tile], tokens(t["x"][0])[:, tile]).then_inc(s["x_in"], 16)
        act.wait_ge(s["chan_ready"], len(ROW_TILES))
        turn_act(act, 0, in_hi, scale=chan[:, CH_GPRE:CH_GPRE + KC])

    def decays_first_act(act):
        act.wait_ge(s["ba_in"], 80)
        act.activation(ba_hi[:, :, :], ba_raw[:, :, :], ACT.Copy).then_inc(s["ba_split"], 1)
        for tile in range(TT):
            reach(act, s["x_ss"], tile)
            act.activation(x_squares[:, :], x_tok[:, tile], ACT.Square, accum_out=small[:, tile:tile + 1])\
               .then_inc(s["x_ss"], 1)

    def decays_act(act):
        v = lambda i: sgl[:, i]
        act.wait_ge(s["ba_out"], 1)
        act.activation(v(2), v(1), ACT.Exp, scale=-1.0).then_inc(s["sg_a"], 1)
        act.wait_ge(s["ba_in"], 80)
        act.activation(v(14)[:, 0:HEADS], alog_b[:, :], ACT.Exp).then_inc(s["sg_a"], 1)
        act.activation(v(13), v(7), ACT.Tanh, scale=0.5).then_inc(s["sg_a"], 1)
        act.wait_ge(s["sg_exp"], 1)
        act.activation(v(5), v(3), ACT.Ln).then_inc(s["sg_a"], 1)
        act.wait_ge(s["gc_copied"], 2)
        hv = head_all[:, :, :].rearrange("p h (k t) -> p k t h", t=TT)
        w = lambda i: sgl[:, i].rearrange("p (t h) -> p t h", t=TT)
        act.activation(hv[:, 3], w(0), ACT.Exp).then_inc(s["sg_a"], 1)
        act.activation(hv[:, 5], w(1), ACT.Exp).then_inc(s["sg_a"], 1)

    def start_pool(pool):
        pool.memset(halfpow[:, :], -0.5).then_inc(s["pads_ready"], 1)
        pool.memset(eps_col[:, :], EPS).then_inc(s["pads_ready"], 1)
        pool.memset(pool_eps[:, 0:4], 4 * EPS)
        pool.memset(pool_eps[:, 4:6], P * EPS)
        pool.memset(conv_in[:, :, 0:SHORT - 1], 0.0).then_inc(s["pads_ready"], 1)
        pool.wait_ge(s["pads_ready"], 1)
        pool.wait_ge(s["x_ss"], TT)
        pool.tensor_scalar(small[:, 2:4], small[:, 0:2], 1.0 / D, EPS, ALU.mult, ALU.add).then_inc(s["x_rms"], 1)
        pool.wait_ge(s["x_rms"], 1)
        pool.tensor_tensor(small[:, 4:6], small[:, 2:4], halfpow[:, 0:2], ALU.pow).then_inc(s["x_rms"], 1)

    def start_dve(dve):
        for i, (at, n) in enumerate(ROW_TILES):
            dve.wait_ge(s["rows_cols"], i + 1)
            dve.tensor_copy(chan[:, at:at + n], (QA, QB)[i % 2][:, 0:n]).then_inc(s["chan_ready"], 1)
        turn_dve(dve, 0, in_hi, in_lo, scale=chan[:, CH_GPRE:CH_GPRE + KC])

    def decays_first_dve(dve):
        dve.wait_ge(s["ba_split"], 1)
        dve.tensor_tensor(ba_lo[:, :, :], ba_raw[:, :, :], ba_hi[:, :, :].bitcast(F32), ALU.subtract)\
           .then_inc(s["ba_lo_ready"], 1)

    def decays_dve(dve):
        n = [0]

        def then(ins):
            n[0] += 1
            ins.then_inc(s["sg_v"], 1)
            dve.wait_ge(s["sg_v"], n[0])

        v = lambda i: sgl[:, i]
        w = lambda i: sgl[:, i].rearrange("p (t h) -> p t h", t=TT)
        dve.wait_ge(s["ba_done"], 1)
        dve.tensor_copy(baT[:, :], RA[0:2 * HEADS, 0:S]).then_inc(s["baT_copied"], 1)
        dve.wait_ge(s["ba_done"], 2)
        dve.wait_ge(s["ba_in"], 80)
        dve.wait_ge(s["x_rms"], 2)
        for tile in range(TT):
            bank = RB[:, tile * 2 * HEADS:(tile + 1) * 2 * HEADS]
            dve.tensor_scalar(w(7)[:, tile], bank[:, 0:HEADS], x_rms[:, tile:tile + 1], None, ALU.mult)
            ins = dve.scalar_tensor_tensor(w(0)[:, tile], bank[:, HEADS:2 * HEADS], x_rms[:, tile:tile + 1], dt_b[:, :],
                                           ALU.mult, ALU.add)
        then(ins)
        dve.tensor_scalar(v(12), v(0), 0.0, None, ALU.max)
        dve.scalar_tensor_tensor(v(1), v(0), -1.0, v(0), ALU.mult, ALU.max).then_inc(s["ba_out"], 1)
        then(dve.tensor_scalar(half_g[:, :], half_g[:, :], 0.5 * float(P) ** 0.5, None, ALU.mult))
        dve.wait_ge(s["sg_a"], 1)
        dve.tensor_scalar(v(3), v(2), 1.0, None, ALU.add).then_inc(s["sg_exp"], 1)
        dve.wait_ge(s["sg_exp"], 1)
        then(dve.tensor_scalar(v(4), v(3), -1.0, None, ALU.add))
        then(dve.tensor_scalar(v(6), v(4), 0.0, None, ALU.is_equal))
        then(dve.tensor_tensor(v(8), v(4), v(6), ALU.add))
        then(dve.reciprocal(v(9), v(8)))
        then(dve.tensor_tensor(v(10), v(9), v(2), ALU.mult))
        dve.wait_ge(s["sg_a"], 4)
        then(dve.tensor_tensor(v(11), v(10), v(5), ALU.mult))
        then(dve.tensor_tensor(v(8), v(6), v(2), ALU.mult))
        then(dve.tensor_tensor(v(11), v(11), v(8), ALU.add))
        then(dve.tensor_tensor(v(11), v(11), v(12), ALU.add))
        dve.scalar_tensor_tensor(w(15), w(11), -1.0, v(14)[:, 0:HEADS].unsqueeze(1).broadcast_to([P, TT, HEADS]),
                                 ALU.mult, ALU.mult).then_inc(s["sg_g"], 1)
        hv = head_all[:, :, :].rearrange("p h (k t) -> p k t h", t=TT)
        dve.tensor_scalar(hv[:, 0], w(13), 0.5, 0.5, ALU.mult, ALU.add)
        dve.tensor_scalar(hv[:, 1], w(13), 0.25, 0.25, ALU.mult, ALU.add)
        dve.wait_ge(s["gc_done"], 1)
        dve.tensor_copy(v(0), QA[:, 0:2 * HEADS]).then_inc(s["gc_copied"], 1)
        dve.wait_ge(s["gc_copied"], 1)
        dve.tensor_copy(hv[:, 2], w(0))
        dve.tensor_tensor(v(1), QB[:, 0:2 * HEADS], v(0), ALU.subtract).then_inc(s["gc_copied"], 1)
        dve.wait_ge(s["gcT_done"], 1)
        dve.tensor_copy(gcT[:, :], QA[0:TT * HEADS, 0:P]).then_inc(s["gc_copied"], 1)
        dve.wait_ge(s["sg_a"], 6)
        dve.tensor_scalar(hv[:, 4], hv[:, 3], -1.0, None, ALU.mult).then_inc(s["head_ready"], 1)

    def ready(eng, blk):
        eng.wait_ge(psum_ready, blk + 1)
        eng.wait_ge(psum_free, blk)

    VEC_GATE, VEC_POST, VEC_PLE, VEC_BANDS, VEC_LN0, VEC_MASK, VEC_LN1 = (16 * n for n in (1, 3, 5, 6, 8, 9, 11))
    whole = lambda x: (lambda tile, k: x[:, tile, k * P:(k + 1) * P])
    four = lambda a: a.rearrange("p k n -> p (k n)")
    cols = lambda n: slice(n * NB, (n + 1) * NB)
    row = lambda x: x.unsqueeze(1).broadcast_to([P, 4, S])
    tiles = lambda x, n: x.unsqueeze(1).broadcast_to([P, TT, n])

    TURN_Y, TURN_MEM, TURN_Y3, TURN_X1, TURN_X2, TURN_M0, TURN_H1, TURN_M1 = 8, 14, 16, 24, 32, 40, 48, 56

    X_TURNS = {BLK_MEM_V0: (0, TURN_X1), BLK_MEM1: (1, TURN_X2)}

    LN0 = 32

    def norm_b_pe(pe, at):
        at -= LN0
        if 2 <= at < 6:
            c = at - 2
            for j in range(4 * c, 4 * c + 4):
                mm = pe.matmul(QA[:, 0:S], ones, ub[:, j], start=(j == 0), stop=(j == KC - 1))
            if c == 3:
                mm.then_inc(s["var_done"], 1)
        if 10 <= at < 18 and at % 2 == 0:
            c = (at - 10) // 2
            pe.wait_ge(s["squared"], c + 1)
            for n in range(4):
                mm = pe.matmul(QB[:, 0:S], ones, sqb[:, c % 2, n], start=(c + n == 0), stop=(c == 3 and n == 3))
            mm.then_inc(s["var_done"], 1)

    def norm_b_act(act, at):
        at -= LN0
        if at == 6:
            act.wait_ge(s["var_done"], 1)
            act.activation(mub[:, :], QA[:, 0:S], ACT.Copy, scale=1.0 / D).then_inc(s["mean_ready"], 1)
        if 8 <= at < 16 and at % 2 == 0:
            c = (at - 8) // 2
            act.wait_ge(s["centred"], c + 1)
            reach(act, s["var_done"], c if c >= 2 else 0)
            act.activation(sqb[:, c % 2], ub[:, 4 * c:4 * c + 4], ACT.Square).then_inc(s["squared"], 1)
        if at == 18:
            act.wait_ge(s["var_done"], 5)
            act.activation(rsb[:, :], QB[:, 0:S], ACT.Sqrt, scale=1.0 / D, bias=eps_col[:, :]).then_inc(s["mean_ready"], 1)
        if at >= 22 and (at - 22) % 8 == 0 and at < 22 + 32:
            c = (at - 22) // 8
            act.wait_ge(s["ln_scaled"], c + 1)
            for j in range(4 * c, 4 * c + 4):
                ins = act.activation(ub[:, j], ub[:, j], ACT.Identity, scale=chan[:, CH_LNG + j:CH_LNG + j + 1],
                                     bias=chan[:, CH_LNB + j:CH_LNB + j + 1])
            ins.then_inc(s["ln_affine"], 1)
        if at >= 24 and (at - 24) % 8 == 0 and at < 24 + 32:
            c = (at - 24) // 8
            act.wait_ge(s["ln_affine"], c + 1)
            reach(act, s["ln_silu"], c - 1)
            act.activation(sqb[:, c % 2], ub[:, 4 * c:4 * c + 4], ACT.Tanh, scale=0.5).then_inc(s["ln_tanh"], 1)
        if at >= 30 and (at - 30) % 8 == 0 and at < 30 + 32:
            c = (at - 30) // 8
            act.wait_ge(s["ln_gated"], c + 1)
            act.activation(ub_hi[:, 4 * c:4 * c + 4], ub[:, 4 * c:4 * c + 4], ACT.Copy).then_inc(s["ub_hi_done"], 1)

    def norm_b_dve(dve, at):
        at -= LN0
        if 7 <= at < 15 and at % 2 == 1:
            c = (at - 7) // 2
            dve.wait_ge(s["mean_ready"], 1)
            dve.tensor_tensor(ub[:, 4 * c:4 * c + 4], ub[:, 4 * c:4 * c + 4], row(mub[:, :]), ALU.subtract)\
               .then_inc(s["centred"], 1)
        if at == 18:
            dve.wait_ge(s["mean_ready"], 2)
            dve.reciprocal(rsb[:, :], rsb[:, :]).then_inc(s["rstd_ready"], 1)
        if at >= 20 and (at - 20) % 8 == 0 and at < 20 + 32:
            c = (at - 20) // 8
            dve.wait_ge(s["rstd_ready"], 1)
            dve.tensor_tensor(ub[:, 4 * c:4 * c + 4], ub[:, 4 * c:4 * c + 4], row(rsb[:, :]), ALU.mult)\
               .then_inc(s["ln_scaled"], 1)
        if at >= 26 and (at - 26) % 8 == 0 and at < 26 + 32:
            c = (at - 26) // 8
            x = ub[:, 4 * c:4 * c + 4]
            dve.wait_ge(s["ln_tanh"], c + 1)
            dve.scalar_tensor_tensor(four(x), four(sqb[:, c % 2]), 1.0, four(x), ALU.add, ALU.mult).then_inc(s["ln_silu"], 1)
        if at >= 28 and (at - 28) % 8 == 0 and at < 28 + 32:
            c = (at - 28) // 8
            x = ub[:, 4 * c:4 * c + 4]
            dve.wait_ge(s["ln_silu"], c + 1)
            dve.tensor_tensor(x, x, zb[:, 4 * c:4 * c + 4], ALU.mult).then_inc(s["ln_gated"], 1)
        if at >= 32 and (at - 32) % 8 == 0 and at < 32 + 32:
            c = (at - 32) // 8
            dve.wait_ge(s["ub_hi_done"], c + 1)
            dve.tensor_tensor(ub_lo[:, 4 * c:4 * c + 4], ub[:, 4 * c:4 * c + 4], ub_hi[:, 4 * c:4 * c + 4].bitcast(F32),
                              ALU.subtract).then_inc(s["ub_lo_done"], 1)

    def mem_head(layer, m):
        q = (mqT0, mqT1)[layer]
        return q[:, m], mkT[:, layer, m], lambda tile: mv[:, layer, tile, m * P:(m + 1) * P], False, 3 * NB + m * P

    def moba_head(m):
        return qT1[:, m], kT1[:, m], lambda tile: v1_[:, tile, m * P:(m + 1) * P], True, m * P

    ATTEND = [mem_head(0, m) for m in range(MEM_HEADS)] + [moba_head(m) for m in range(MOBA_HEADS)] \
        + [mem_head(1, m) for m in range(MEM_HEADS)]
    PERIOD = 8
    ATT_AT = {0: (BLK_IN0 + 5, 0, MEM_HEADS), 1: (BLK_IN1 + 3, MEM_HEADS, len(ATTEND) - MEM_HEADS)}

    def attention(at, step):
        for blk, first, n in ATT_AT.values():
            p, hs = divmod(at - 32 * (blk - BLK_GB), PERIOD)
            for second in (True, False):
                if at >= 32 * (blk - BLK_GB) and 0 <= p - second < n:
                    step(first + p - second, hs, second)

    def attend_pe(pe, i, hs, second):
        q, k, v, causal, to = ATTEND[i]
        if second and hs == 1:
            pe.wait_ge(s["probs_ready"], i + 1)
            reach(pe, s["probT_ready"], i)
            for key in range(TT):
                for tile in range(TT):
                    mm = pe.transpose(RB[:, key * S + tile * P:key * S + (tile + 1) * P], sc[:, tile, key * P:(key + 1) * P], ident)
            mm.then_inc(s["probs_turned"], 1)
        if second and hs == 4:
            pe.wait_ge(s["probT_ready"], i + 1)
            reach(pe, s["att_ready"], i)
            for tile in range(TT):
                n = tile + 1 if causal else TT
                for key in range(n):
                    mm = pe.matmul(QA[:, tile * P:(tile + 1) * P], probT[:, key, tile * P:(tile + 1) * P], v(key),
                                   start=(key == 0), stop=(key == n - 1))
            mm.then_inc(s["attended"], 1)
        if not second and hs == 4:
            reach(pe, s["scores_masked"], i)
            if i == 0:
                pe.wait_ge(s["heads_taken"], 6)
                pe.wait_ge(s["pw_ready"], len(POOL_WINDOWS))
            if i == MEM_HEADS:
                pe.wait_ge(s["heads_taken"], 16)
            if i == 2 * MEM_HEADS:
                pe.wait_ge(s["heads_taken"], 18)
            if i == len(ATTEND) - MEM_HEADS:
                pe.wait_ge(s["heads_taken"], 20)
            for tile in range(TT):
                mm = pe.matmul(RA[:, tile * S:(tile + 1) * S], q[:, tile * P:(tile + 1) * P], k, start=True, stop=True)
            mm.then_inc(s["scores_done"], 1)

    def attend_act(act, i, hs, second):
        to = ATTEND[i][4]
        mx, sums, inv = st[:, 48:50], st[:, 50:52], st[:, 52:54]
        if second and hs == 4:
            act.wait_ge(s["attended"], i + 1)
            act.wait_ge(s["sums_inverted"], i + 1)
            for tile in range(TT):
                ins = act.activation(mo[:, tile, to:to + P], QA[:, tile * P:(tile + 1) * P], ACT.Copy, scale=inv[:, tile:tile + 1])
            ins.then_inc(s["att_ready"], 1)
        if not second and hs == 5:
            act.wait_ge(s["max_ready"], 2 * i + 2)
            reach(act, s["sums_inverted"], i)
            for tile in range(TT):
                ins = act.activation(sc[:, tile], sc[:, tile], ACT.Exp, bias=mx[:, tile:tile + 1],
                                     accum_out=sums[:, tile:tile + 1])
            ins.then_inc(s["probs_ready"], 1)

    def attend_dve(dve, i, hs, second):
        causal = ATTEND[i][3]
        mx, sums, inv = st[:, 48:50], st[:, 50:52], st[:, 52:54]
        both_tiles = RA[:, :].rearrange("p (t n) -> p t n", t=TT)
        if second and hs == 1:
            dve.wait_ge(s["probs_turned"], i + 1)
            reach(dve, s["attended"], i)
            dve.tensor_copy(probT[:, :, :].rearrange("p t n -> p (t n)"), RB[:, :]).then_inc(s["probT_ready"], 1)
        if not second and hs == 4:
            dve.wait_ge(s["scores_done"], i + 1)
            reach(dve, s["probs_turned"], i)
            if causal:
                dve.wait_ge(s["vec_loaded"], VEC_MASK)
                dve.scalar_tensor_tensor(sc[:, :, :], both_tiles, RSQ, mask[:, :, :], ALU.mult, ALU.add).then_inc(s["scores_masked"], 1)
            else:
                dve.tensor_scalar(sc[:, :, :], both_tiles, RSQ, None, ALU.mult).then_inc(s["scores_masked"], 1)
            dve.wait_ge(s["scores_masked"], i + 1)
            reach(dve, s["probs_ready"], i)
            dve.tensor_reduce(mx, sc[:, :, :], AX.X, ALU.max).then_inc(s["max_ready"], 1)
            dve.wait_ge(s["max_ready"], 2 * i + 1)
            dve.tensor_scalar(mx, mx, -1.0, None, ALU.mult).then_inc(s["max_ready"], 1)
        if not second and hs == 7:
            dve.wait_ge(s["probs_ready"], i + 1)
            reach(dve, s["att_ready"], i)
            dve.reciprocal(inv, sums).then_inc(s["sums_inverted"], 1)

    HEADS_OF = {BLK_MEM_K0: (0, stage0, lambda r: mkT[:, 0, 2 * r:2 * r + 2]), BLK_MEM1: (1, stage0, lambda r: mkT[:, 1, 2 * r:2 * r + 2]),
                BLK_IN0 + 3: (2, stage0, lambda r: mqT0[:, 2 * r:2 * r + 2])}
    for n in range(3):
        HEADS_OF[BLK_KV + n] = (3 + n, stage1, lambda r, n=n: kT1[:, 4 * n + 2 * r:4 * n + 2 * r + 2])
        HEADS_OF[BLK_IN1 + n] = (6 + n, stage1, lambda r, n=n: qT1[:, 4 * n + 2 * r:4 * n + 2 * r + 2])
    HEADS_OF[BLK_IN1 + 3] = (9, stage1, lambda r: mqT1[:, 2 * r:2 * r + 2])

    def heads_pe(pe, n, stage, hs, blk):
        if hs in (2, 4):
            r = (hs - 2) // 2
            pe.wait_ge(psum_free, blk + 1)
            reach(pe, s["heads_taken"], 2 * n + r)
            if n == 1 and r == 0:
                pe.wait_ge(s["turned_lo"], TURN_X2 + 8)
            for m in range(2):
                for tile in range(TT):
                    c = (2 * r + m) * P
                    mm = pe.transpose(QB[:, m * S + tile * P:m * S + (tile + 1) * P], stage[:, tile, c:c + P], ident)
            mm.then_inc(s["heads_done"], 1)

    def heads_act(act, n, stage, to, hs, blk):
        if hs == 0:
            ready(act, blk)
            reach(act, s["heads_done"], 2 * n)
            if n == 0:
                act.wait_ge(s["mix_ready"], 4)
            for tile in range(TT):
                ins = act.activation(stage[:, tile], pairs[blk % 2][:, tile], ACT.Copy)
            ins.then_inc(psum_free, 1)
        if hs in (2, 4):
            r = (hs - 2) // 2
            act.wait_ge(s["heads_done"], 2 * n + r + 1)
            act.activation(to(r), QB[:, :].rearrange("p (m n) -> p m n", m=2), ACT.Copy).then_inc(s["heads_taken"], 1)

    RMS = {BLK_OUT: (0, 1.0 / D, EPS, 1.0), BLK_PLE: (1, 0.25 / D, EPS, 0.5)}

    def rms_pool(pool, n):
        _, by, eps, factor = list(RMS.values())[n]
        pool.wait_ge(s["ms_ready"], n + 1)
        pool.tensor_scalar(small[:, 20:22], small[:, 18:20], by, eps, ALU.mult, ALU.add).then_inc(s["ms_rms"], 1)
        pool.wait_ge(s["ms_rms"], 3 * n + 1)
        pool.tensor_tensor(small[:, 22:24], small[:, 20:22], halfpow[:, 0:2], ALU.pow).then_inc(s["ms_rms"], 1)
        pool.wait_ge(s["ms_rms"], 3 * n + 2)
        pool.tensor_scalar(small[:, 24:26], small[:, 22:24], factor, None, ALU.mult).then_inc(s["ms_rms"], 1)

    def rms_dve(dve, n):
        dve.wait_ge(s["mo_summed"], 8 * (n + 1))
        dve.tensor_reduce(small[:, 18:20], small[:, 8:16].rearrange("p (t n) -> p t n", t=TT), AX.X, ALU.add)\
           .then_inc(s["ms_ready"], 1)
        dve.wait_ge(s["ms_rms"], 3 * n + 3)
        dve.wait_ge(s["mo_scaled"], 4 * (n + 1))
        dve.wait_ge(s["vec_loaded"], VEC_POST)
        for c in range(4):
            for tile in range(TT):
                ins = dve.scalar_tensor_tensor(xr[:, tile, cols(c)], mo[:, tile, cols(c)], small[:, 24 + tile:25 + tile],
                                               xr[:, tile, cols(c)], ALU.mult, ALU.add)
            ins.then_inc(s["x_added"], 1)

    def res_dve(dve, blk, n, layer):
        ready(dve, blk)
        for tile in range(TT):
            ins = dve.scalar_tensor_tensor(xr[:, tile, cols(n)], xr[:, tile, cols(n)], ALPHA, pairs[blk % 2][:, tile],
                                           ALU.mult, ALU.add)
        ins.then_inc(psum_free, 1)
        dve.wait_ge(psum_free, blk + 1)
        stats = sgst.rearrange("p (t n k) -> p t n k", t=TT, n=4)
        for tile in range(TT):
            ins = dve.bn_stats(stats[:, tile, n], xr[:, tile, cols(n)])
        ins.then_inc(s["stats_ready"], 1)

    def ln_dve(dve, layer, lnv):
        dve.wait_ge(s["stats_ready"], 4 * (layer + 1))
        stats = sgst.rearrange("p (t n k) -> p t n k", t=TT, n=4)
        for tile in range(TT):
            ins = dve.bn_aggr(small[:, 28 + 2 * tile:30 + 2 * tile], stats[:, tile].rearrange("p n k -> p (n k)"))
        ins.then_inc(s["aggr_ready"], 1)
        dve.wait_ge(s["aggr_ready"], layer + 1)
        dve.wait_ge(s["vec_loaded"], (VEC_LN0, VEC_LN1)[layer])

    def ln_first_dve(dve, layer, lnv, c):
        for tile in range(TT):
            x = xr[:, tile, cols(c)]
            ins = dve.scalar_tensor_tensor(x, x, small[:, 28 + 2 * tile:29 + 2 * tile], lnv[0][:, cols(c)],
                                           ALU.subtract, ALU.mult)
        ins.then_inc(s["ln_gain"], 1)

    def ln_last_dve(dve, layer, lnv, c):
        dve.wait_ge(s["ln_gain"], 4 * layer + c + 1)
        dve.wait_ge(s["ln_pool"], 2 * (layer + 1))
        for tile in range(TT):
            x = xr[:, tile, cols(c)]
            ins = dve.scalar_tensor_tensor(x, x, small[:, 34 + tile:35 + tile], lnv[1][:, cols(c)], ALU.mult, ALU.add)
        ins.then_inc(s["ln_done"], 1)

    def ln_pool(pool, layer):
        var = small[:, 28:32].rearrange("p (t k) -> p k t", k=2)[:, 1]
        pool.wait_ge(s["aggr_ready"], layer + 1)
        pool.tensor_scalar(small[:, 32:34], var, LN_EPS, None, ALU.add).then_inc(s["ln_pool"], 1)
        pool.wait_ge(s["ln_pool"], 2 * layer + 1)
        pool.tensor_tensor(small[:, 34:36], small[:, 32:34], halfpow[:, 0:2], ALU.pow).then_inc(s["ln_pool"], 1)

    LNV = [(vec[:, :], ln_b0[:, :]), (ln_vec_a[:, 0], ln_vec_a[:, 1])]
    GATES = {BLK_IN0 + 4: 0, BLK_IN0 + 5: 1, BLK_IN0 + 6: 2, BLK_IN0 + 7: 3,
             BLK_IN1 + 4: 4, BLK_IN1 + 5: 5, BLK_IN1 + 6: 6, BLK_IN1 + 7: 7}

    def gate_act(act, blk, hs):
        stage = stage0 if blk < BLK_KV else stage1
        n = GATES[blk]
        if hs == 2:
            act.wait_ge(psum_ready, blk + 1)
            if n in (0, 4):
                act.wait_ge(s["heads_done"], 6 if n == 0 else 20)
            reach(act, s["mixed_ready"], n)
            for tile in range(TT):
                ins = act.activation(stage[:, tile], pairs[blk % 2][:, tile], ACT.Tanh, scale=0.5)
            ins.then_inc(s["gate_tanh"], 1)

    def gate_dve(dve, blk, hs):
        stage = stage0 if blk < BLK_KV else stage1
        n = GATES[blk]
        if hs == 5:
            dve.wait_ge(s["gate_tanh"], n + 1)
            dve.wait_ge(psum_free, blk)
            for tile in range(TT):
                ins = dve.scalar_tensor_tensor(stage[:, tile], stage[:, tile], 1.0, pairs[blk % 2][:, tile], ALU.add, ALU.mult)
            ins.then_inc(psum_free, 1)
            if n < 3:
                dve.wait_ge(s["pw_ready"], 4)
            elif n == 3:
                dve.wait_ge(s["att_ready"], MEM_HEADS)
            elif n < 7:
                dve.wait_ge(s["att_ready"], MEM_HEADS + 4 * (n - 3))
            else:
                dve.wait_ge(s["att_ready"], len(ATTEND))
            dve.wait_ge(psum_free, blk + 1)
            x = mo[:, :, cols(n % 4)]
            dve.tensor_tensor(x, x, stage[:, :, :], ALU.mult).then_inc(s["mixed_ready"], 1)

    POOL_BLK, MAP_BLK = BLK_IN0 + 3, BLK_IN0 + 4
    POOLED = 6

    def pool_pe(pe, blk, hs):
        if blk == POOL_BLK and hs >= 4 and hs % 4 == 0 and hs < 28:
            r = hs // 4 - 1
            if r == 0:
                pe.wait_ge(psum_free, BLK_IN0 + 3)
                pe.wait_ge(s["vec_loaded"], VEC_BANDS)
            reach(pe, s["pool_ready"], r - 1)
            for m in range(2):
                c = 2 * r + m
                for tile in range(TT):
                    mm = pe.matmul((RA, RB)[r % 2][:, m * S:(m + 1) * S], u0[:, tile, c * P:(c + 1) * P],
                                   bands[:, tile, c // 3], start=(m == 0 and tile == 0), stop=(tile == TT - 1),
                                   skip_group_check=True)
            mm.then_inc(s["pool_done"], 1)
        if blk == MAP_BLK and hs % 8 == 2:
            g = hs // 8
            pe.wait_ge(s["pool_ready"], 6)
            pe.wait_ge(s[f"pw_loaded{g % 2}"], 32 * (g // 2 + 1))
            reach(pe, s["pw_ready"], g)
            for tile in range(TT):
                for k in range(3):
                    mm = pe.matmul((RA, RB)[tile][:, 0:PG], pooled[:, 3 * g + k, tile * P:(tile + 1) * P], pool_w[g % 2][:, k],
                                   start=(k == 0), stop=(k == 2))
            mm.then_inc(s["pool_done"], 1)

    def pool_act(act, blk, hs):
        if blk == POOL_BLK and hs >= 4 and hs % 4 == 0 and hs < 28:
            r = hs // 4 - 1
            act.wait_ge(s["pool_done"], r + 1)
            act.activation(pooled[:, 2 * r:2 * r + 2].rearrange("p c n -> p (c n)"), (RA, RB)[r % 2][:, :], ACT.Copy)\
               .then_inc(s["pool_ready"], 1)

    def pool_dve(dve, blk, hs):
        if blk == MAP_BLK and hs % 8 == 2:
            g = hs // 8
            dve.wait_ge(s["pool_done"], POOLED + g + 1)
            dve.wait_ge(s[f"pw_loaded{g % 2}"], 32 * (g // 2 + 1))
            for tile in range(TT):
                ins = dve.tensor_tensor(mo[:, tile, g * PG:(g + 1) * PG], (RA, RB)[tile][:, 0:PG], pscale[:, g % 2], ALU.mult)
            ins.then_inc(s["pw_ready"], 1)

    OWN = {BLK_OUT0: (TURN_M0, mo, "mixed_ready", 0, 0.5), BLK_KV: (TURN_H1, xr, "ln_done", 0, 1.0),
           BLK_OUT1: (TURN_M1, mo, "mixed_ready", 4, 0.5)}

    OWN_AT = {0: 1, 3: 2, 7: 3, 11: 4, 15: 5, 19: 6, 23: 7}

    def own_pe(pe, blk, g):
        base, src, what, per, _ = OWN[blk]
        turn_pe(pe, base, whole(src), lambda g: pe.wait_ge(s[what], per + g // 2 + 1), range(g, g + 1))

    def own_act(act, blk, g):
        turn_act(act, OWN[blk][0], in_hi, factor=OWN[blk][4], groups=range(g, g + 1))

    def own_dve(dve, blk, g):
        turn_dve(dve, OWN[blk][0], in_hi, in_lo, factor=OWN[blk][4], groups=range(g, g + 1))

    def beside_pe(pe, blk, hs):
        at = 32 * (blk - BLK_GB) + hs
        if blk == BLK_GB:
            group_pe(pe, KC - 1, 1, hs)
        if at == LN0:
            pe.wait_ge(s["u_ready"], KC)
        norm_b_pe(pe, at)
        if BLK_Y + 2 <= blk <= BLK_Y + 8 and blk % 2 == BLK_Y % 2 and hs == 4:
            n = (blk - BLK_Y) // 2 - 1
            turn_pe(pe, TURN_Y3 if n == 3 else TURN_Y, lambda tile, k: mix[:, tile, (k % 4) * P:(k % 4 + 1) * P],
                    lambda g: pe.wait_ge(s["mix_ready"], n + 1), range(2 * n, 2 * n + 2))
        if blk == BLK_Y + 7 and hs >= 2 and hs % 3 == 2 and hs < 26:
            g = hs // 3
            turn_pe(pe, TURN_MEM, lambda tile, k: mem_tok[:, (k // 4) % 2, tile, (k % 4) * P:(k % 4 + 1) * P],
                    lambda g: pe.wait_ge(s[f"mem_loaded{g // 2 % 2}"], 16 * (g // 4 + 1)), range(g, g + 1))
        if blk - 1 in HEADS_OF:
            n, stage, _ = HEADS_OF[blk - 1]
            heads_pe(pe, n, stage, hs, blk - 1)
        if blk in X_TURNS and hs >= 12 and hs % 2 == 0 and hs < 28:
            g = (hs - 12) // 2
            n, base = X_TURNS[blk]
            turn_pe(pe, base, whole(xr), lambda g: pe.wait_ge(s["x_added"], 4 * n + g // 2 + 1), range(g, g + 1))
        if blk == BLK_PLE and hs == 2:
            pe.wait_ge(s["vec_loaded"], VEC_PLE)
            pe.wait_ge(s["turned_lo"], TURN_X2)
            for k in range(2):
                for tile in range(TT):
                    mm = pe.transpose(QA[:, k * S + tile * P:k * S + (tile + 1) * P], p_tok[:, tile, k * P:(k + 1) * P], ident)
            mm.then_inc(s["e_done"], 1)
        if BLK_PLE <= blk < BLK_PLE + 4 and hs == 16:
            n = blk - BLK_PLE
            pe.wait_ge(s["pT_ready"], 1)
            pe.wait_ge(s["wpp_loaded"], 16 * (n + 1))
            reach(pe, s["pr_ready"], n)
            for tile in range(TT):
                for k in range(2):
                    mm = pe.matmul((RA, RB)[tile][:, :], pT[:, k, tile * P:(tile + 1) * P], wpp[:, k], start=(k == 0), stop=(k == 1))
            mm.then_inc(s["e_done"], 1)
        if blk in OWN and hs in OWN_AT:
            own_pe(pe, blk, OWN_AT[hs])
        if blk in OWN and hs % 4 == 3 and hs < 28:
            pe.wait_ge(s["turned_lo"], OWN[blk][0] + (hs + 1) // 4 + 1)
        pool_pe(pe, blk, hs)
        attention(at, lambda i, h, second: attend_pe(pe, i, h, second))

    def before_pe(pe, blk):
        if blk == BLK_Y + 1:
            pe.wait_ge(s["ub_lo_done"], 4)
        if blk == BLK_Y:
            pe.wait_ge(s["oa_lo_done"], HEADS)
        if blk == BLK_MEM_K0:
            pe.wait_ge(s["turned_lo"], TURN_MEM + 8)
        if blk == BLK_OUT:
            pe.wait_ge(s["turned_lo"], TURN_X1)
        if blk == BLK_PLE:
            pe.wait_ge(s["turned_lo"], TURN_X2)
        if blk == BLK_IN0:
            pe.wait_ge(s["turned_lo"], TURN_X2 + 8)
        if blk in OWN:
            own_pe(pe, blk, 0)
            pe.wait_ge(s["turned_lo"], OWN[blk][0] + 1)

    def columns_of(blk):
        if BLK_Y <= blk < BLK_MEM_K0:
            return (oa_hi, oa_lo) if blk % 2 == BLK_Y % 2 else (ub_hi, ub_lo)
        if blk in (BLK_MEM_K0, BLK_MEM_V0, BLK_MEM1, BLK_MEM1 + 1):
            return mem_hi, mem_lo
        return in_hi, in_lo

    def tail_pe(pe):
        for blk in range(BLK_GB, BLK_END):
            before_pe(pe, blk)
            pe_block(pe, blk, blk % 2, *columns_of(blk), lambda hs: beside_pe(pe, blk, hs))

    def beside_act(act, blk, hs):
        at = 32 * (blk - BLK_GB) + hs
        done = blk - 1
        if blk == BLK_GB:
            group_act(act, KC - 1, 1, hs)
        if BLK_GB <= done < BLK_GB + 4 and hs == 3:
            n = done - BLK_GB
            act.wait_ge(psum_free, done + 1)
            act.activation(gb[:, :, cols(n)], gb[:, :, cols(n)], ACT.Tanh, scale=0.5).then_inc(s["gb_tanh"], 1)
        if at == LN0:
            act.wait_ge(s["pads_ready"], 2)
        norm_b_act(act, at)
        if BLK_Y + 2 <= blk <= BLK_Y + 8 and blk % 2 == BLK_Y % 2 and hs == 4:
            n = (blk - BLK_Y) // 2 - 1
            turn_act(act, TURN_Y3 if n == 3 else TURN_Y, in_hi, factor=0.5, groups=range(2 * n, 2 * n + 2))
        if blk == BLK_Y + 7 and hs >= 2 and hs % 3 == 2 and hs < 26:
            g = hs // 3
            turn_act(act, TURN_MEM, mem_hi, groups=range(g, g + 1))
        if done in HEADS_OF:
            n, stage, to = HEADS_OF[done]
            heads_act(act, n, stage, to, hs, done)
        if done in (BLK_MEM_V0, BLK_MEM1 + 1, BLK_KV + 3, BLK_KV + 4, BLK_KV + 5) and hs == 0:
            ready(act, done)
            for tile in range(TT):
                if done < BLK_IN0:
                    to = mv[:, int(done > BLK_PLE), tile]
                else:
                    to = v1_[:, tile, cols(done - BLK_KV - 3)]
                ins = act.activation(to, pairs[done % 2][:, tile], ACT.Copy)
            ins.then_inc(psum_free, 1)
        if BLK_OUT <= done < BLK_OUT + 4:
            n = done - BLK_OUT
            if hs == 0:
                ready(act, done)
                for tile in range(TT):
                    ins = act.activation(mo[:, tile, cols(n)], pairs[done % 2][:, tile], ACT.Copy)
                ins.then_inc(psum_free, 1)
            if hs == 2:
                act.wait_ge(psum_free, done + 1)
                for tile in range(TT):
                    reach(act, s["mo_summed"], 2 * n + tile)
                    act.activation(junk2[:, :], mo[:, tile, cols(n)], ACT.Square,
                                   accum_out=small[:, 8 + 4 * tile + n:9 + 4 * tile + n]).then_inc(s["mo_summed"], 1)
        if blk in X_TURNS and hs >= 12 and hs % 2 == 0 and hs < 28:
            g = (hs - 12) // 2
            turn_act(act, X_TURNS[blk][1], in_hi, groups=range(g, g + 1))
        if blk == BLK_PLE and hs == 2:
            act.wait_ge(s["e_done"], 1)
            act.activation(pT[:, :, :].rearrange("p k n -> p (k n)"), QA[:, :], ACT.Copy).then_inc(s["pT_ready"], 1)
        if BLK_PLE <= done < BLK_PLE + 4:
            ple_act(act, done, hs)
        if BLK_IN0 <= done < BLK_IN0 + 3 and hs == 0:
            ready(act, done)
            for tile in range(TT):
                ins = act.activation(u0[:, tile, cols(done - BLK_IN0)], pairs[done % 2][:, tile], ACT.Copy)
            ins.then_inc(psum_free, 1)
        pool_act(act, blk, hs)
        if done in GATES:
            gate_act(act, done, hs)
        if blk in OWN and hs in OWN_AT:
            own_act(act, blk, OWN_AT[hs])
        attention(at, lambda i, h, second: attend_act(act, i, h, second))

    def ple_act(act, done, hs):
        n = done - BLK_PLE
        if hs == 0:
            act.wait_ge(psum_ready, done + 1)
            act.wait_ge(psum_free, done)
            reach(act, s["pr_ready"], n)
            for tile in range(TT):
                ins = act.activation(stage0[:, tile], pairs[done % 2][:, tile], ACT.Tanh, scale=0.5)
            ins.then_inc(psum_free, 1)
        if hs == 2:
            act.wait_ge(s["pr_ready"], n + 1)
            for tile in range(TT):
                act.wait_ge(s["mo_summed"], 8 + 2 * n + tile)
                act.activation(junk2[:, :], mo[:, tile, cols(n)], ACT.Square,
                               accum_out=small[:, 8 + 4 * tile + n:9 + 4 * tile + n]).then_inc(s["mo_summed"], 1)

    def before_act(act, blk):
        if blk in OWN:
            own_act(act, blk, 0)

    def tail_act(act):
        for blk in range(BLK_GB, BLK_END):
            before_act(act, blk)
            act_block(act, blk, lambda hs: beside_act(act, blk, hs))

    def beside_dve(dve, blk, hs):
        at = 32 * (blk - BLK_GB) + hs
        done = blk - 1
        if blk == BLK_GB:
            group_dve(dve, KC - 1, 1, hs)
        if BLK_GB <= done < BLK_GB + 4 and hs == 0:
            n = done - BLK_GB
            ready(dve, done)
            if n == 0:
                dve.wait_ge(s["vec_loaded"], VEC_GATE)
                dve.wait_ge(s["u_ready"], KC)
            for tile in range(TT):
                ins = dve.scalar_tensor_tensor(gb[:, tile, cols(n)], pairs[done % 2][:, tile], x_rms[:, tile:tile + 1],
                                               vec[:, cols(n)], ALU.mult, ALU.add)
            ins.then_inc(psum_free, 1)
        norm_b_dve(dve, at)
        if BLK_Y <= done < BLK_MEM_K0 and hs == 0:
            n, second = divmod(done - BLK_Y, 2)
            ready(dve, done)
            if not second:
                dve.wait_ge(s[f"gat_loaded{n % 2}"], 16 * (n // 2 + 1))
                if n:
                    dve.wait_ge(s["turned"], TURN_Y + 2 * n)
                for tile in range(TT):
                    ins = dve.scalar_tensor_tensor(mix[:, tile], gat[:, n % 2, tile], 1.0, pairs[done % 2][:, tile],
                                                   ALU.add, ALU.mult)
                ins.then_inc(psum_free, 1)
            else:
                dve.wait_ge(s["gb_tanh"], 4)
                for tile in range(TT):
                    ins = dve.scalar_tensor_tensor(gb[:, tile, cols(n)], gb[:, tile, cols(n)], 1.0, pairs[done % 2][:, tile],
                                                   ALU.add, ALU.mult)
                ins.then_inc(psum_free, 1)
                dve.wait_ge(psum_free, done + 1)
                dve.tensor_tensor(mix[:, :, :], mix[:, :, :], gb[:, :, cols(n)], ALU.add).then_inc(s["mix_ready"], 1)
        if BLK_Y + 2 <= blk <= BLK_Y + 8 and blk % 2 == BLK_Y % 2 and hs == 4:
            n = (blk - BLK_Y) // 2 - 1
            turn_dve(dve, TURN_Y3 if n == 3 else TURN_Y, in_hi, in_lo, factor=0.5, groups=range(2 * n, 2 * n + 2))
        if blk == BLK_Y + 7 and hs >= 2 and hs % 3 == 2 and hs < 26:
            g = hs // 3
            turn_dve(dve, TURN_MEM, mem_hi, mem_lo, groups=range(g, g + 1))
        if BLK_OUT <= done < BLK_OUT + 4 and hs == 4:
            n = done - BLK_OUT
            dve.wait_ge(s["mo_summed"], 2 * n + 2)
            if n == 0:
                dve.wait_ge(s["vec_loaded"], VEC_POST)
            dve.tensor_tensor(mo[:, :, cols(n)], mo[:, :, cols(n)], tiles(vec[:, cols(n)], NB), ALU.mult)\
               .then_inc(s["mo_scaled"], 1)
        if blk in X_TURNS and hs == 8:
            rms_dve(dve, X_TURNS[blk][0])
        if blk in X_TURNS and hs >= 12 and hs % 2 == 0 and hs < 28:
            g = (hs - 12) // 2
            turn_dve(dve, X_TURNS[blk][1], in_hi, in_lo, groups=range(g, g + 1))
        if BLK_PLE <= done < BLK_PLE + 4:
            ple_dve(dve, done, hs)
        pool_dve(dve, blk, hs)
        if done in GATES:
            gate_dve(dve, done, hs)
        if blk == BLK_KV and hs in (0, 6, 13):
            ln_first_dve(dve, 0, LNV[0], 1 + (0, 6, 13).index(hs))
        if blk == BLK_KV and hs in (1, 8, 15):
            ln_last_dve(dve, 0, LNV[0], 1 + (1, 8, 15).index(hs))
        if blk in OWN and hs in OWN_AT:
            own_dve(dve, blk, OWN_AT[hs])
        if hs == 0 and (BLK_OUT0 <= done < BLK_OUT0 + 3 or BLK_OUT1 <= done):
            layer = int(done >= BLK_OUT1)
            res_dve(dve, done, done - (BLK_OUT0, BLK_OUT1)[layer], layer)
        attention(at, lambda i, h, second: attend_dve(dve, i, h, second))

    def ple_dve(dve, done, hs):
        n = done - BLK_PLE
        if hs == 1:
            dve.wait_ge(psum_free, done + 1)
            dve.wait_ge(s["e_done"], n + 2)
            dve.wait_ge(s["x_added"], 4)
            for tile in range(TT):
                ins = dve.scalar_tensor_tensor(mo[:, tile, cols(n)], stage0[:, tile], 1.0, (RA, RB)[tile][:, :],
                                               ALU.add, ALU.mult)
            ins.then_inc(s["pr_ready"], 1)
        if hs == 4:
            dve.wait_ge(s["mo_summed"], 8 + 2 * n + 2)
            if n == 0:
                dve.wait_ge(s["vec_loaded"], VEC_PLE)
            dve.tensor_tensor(mo[:, :, cols(n)], mo[:, :, cols(n)], tiles(vec[:, cols(n)], NB), ALU.mult)\
               .then_inc(s["mo_scaled"], 1)

    def before_dve(dve, blk):
        if blk == BLK_KV:
            res_dve(dve, blk - 1, 3, 0)
            ln_dve(dve, 0, LNV[0])
            ln_first_dve(dve, 0, LNV[0], 0)
            ln_last_dve(dve, 0, LNV[0], 0)
        if blk in OWN:
            own_dve(dve, blk, 0)

    def tail_dve(dve):
        for blk in range(BLK_GB, BLK_END):
            before_dve(dve, blk)
            dve_block(dve, blk, lambda hs: beside_dve(dve, blk, hs))
        res_dve(dve, BLK_END - 1, 3, 1)
        ln_dve(dve, 1, LNV[1])
        ln_first_dve(dve, 1, LNV[1], 0)
        for c in range(4):
            if c < 3:
                ln_first_dve(dve, 1, LNV[1], c + 1)
            ln_last_dve(dve, 1, LNV[1], c)

    def tail_pool(pool):
        def load(to, src, done):
            pool.dma_start(to, src).then_inc(s[done], 16)

        def after(**counts):
            for n, count in counts.items():
                reach(pool, s[n], count)

        row_of = lambda a: a.partition_broadcast(P)
        mem = lambda c: load(mem_tok[:, c % 2], tokens(t["mem_2"][0])[:, :, cols(c)], f"mem_loaded{c % 2}")
        gate = lambda n: load(gat[:, n % 2], tokens(gate_a_dram)[:, :, cols(n)], f"gat_loaded{n % 2}")
        after(u_ready=KC, gate_a_stored=16 * KC)
        load(vec[:, :], row_of(t["b_gate"][0, D:2 * D]), "vec_loaded")
        pool.wait_ge(psum_free, BLK_GB + 4)
        mem(0)
        mem(1)
        after(ub_hi_done=4, ln_gated=4)
        gate(0)
        gate(1)
        for n in (2, 3):
            pool.wait_ge(psum_free, BLK_Y + 2 * (n - 2) + 1)
            gate(n)
        for c in (2, 3):
            after(turned=TURN_MEM + 2 * (c - 1))
            mem(c)
        pool.wait_ge(psum_ready, BLK_MEM_K0)
        load(xr[:, :, :], tokens(t["x"][0]), "vec_loaded")
        after(turned=TURN_MEM + 8)
        load(vec[:, :], row_of(t["g_post"][0]), "vec_loaded")
        rms_pool(pool, 0)
        after(mo_scaled=4)
        load(vec[:, :], row_of(t["g_ple"][0]), "vec_loaded")
        load(p_tok[:, :, :], tokens(t["p"][0, 0]), "vec_loaded")
        for n in range(4):
            after(e_done=n + 1 if n else 0)
            load(wpp[:, :, :], t["w_ple_proj"][0].rearrange("(k p) n -> p k n", p=P)[:, :, cols(n)], "wpp_loaded")
        rms_pool(pool, 1)
        after(mo_scaled=8)
        load(bands[:, :, :, :], t["pool_bands"].rearrange("(t p) g n -> p t g n", p=P), "vec_loaded")
        pool.wait_ge(psum_ready, BLK_IN0)
        for g in range(len(POOL_WINDOWS)):
            after(e_done=5, pool_done=POOLED + max(g - 1, 0) if g else 0)
            load(pool_w[g % 2][:, :, :], t["pool_w_2"][0, g].rearrange("(k p) n -> p k n", p=P), f"pw_loaded{g % 2}")
            if g >= 2:
                after(pw_ready=g - 1)
            load(pscale[:, g % 2], row_of(t["pool_scale_2"][0, g * PG:(g + 1) * PG]), f"pw_loaded{g % 2}")
        after(pool_done=POOLED + 4)
        load(vec[:, :], row_of(t["ln_g_2"][0]), "vec_loaded")
        load(ln_b0[:, :], row_of(t["ln_b_2"][0]), "vec_loaded")
        ln_pool(pool, 0)
        after(pool_done=POOLED + 4, ln_gain=4)
        load(mask[:, :, :], t["causal_mask"].rearrange("(t p) n -> p t n", p=P), "vec_loaded")
        after(mixed_ready=8, attended=len(ATTEND))
        load(ln_vec_a[:, 0], row_of(t["ln_g_2"][1]), "vec_loaded")
        load(ln_vec_a[:, 1], row_of(t["ln_b_2"][1]), "vec_loaded")
        ln_pool(pool, 1)

    SOURCES = [(w_in, COL_GATE_B + n * NB) for n in range(4)]
    SOURCES += [(square[w], n * NB) for n in range(4) for w in ("w_br_a", "w_br_b")]
    SOURCES += [(w_mem[0], 0)] + [(square["w_out"], n * NB) for n in range(4)] + [(w_mem[0], NB)]
    SOURCES += [(square["w_ple_gate"], n * NB) for n in range(4)] + [(w_mem[1], n * NB) for n in range(2)]
    SOURCES += [(w_in2[0], n * NB) for n in IN_ORDER] + [(w_out2[0], n * NB) for n in range(4)]
    SOURCES += [(w_kv, n * NB) for n in range(6)]
    SOURCES += [(w_in2[1], n * NB) for n in IN_ORDER] + [(w_out2[1], n * NB) for n in range(4)]
    assert len(SOURCES) == BLK_END - BLK_GB

    def tail_sp(sp):
        for blk, (w, col) in enumerate(SOURCES, BLK_GB):
            load_block(sp, blk, w, col)
            if blk == BLK_GB:
                group_out_sp(sp, KC - 1)
        for c in range(4):
            sp.wait_ge(s["ln_done"], 4 + c + 1)
            sp.dma_start(tokens(out)[:, :, cols(c)], xr[:, :, cols(c)]).then_inc(s["out_stored"], 16)
        sp.wait_ge(s["out_stored"], 64)

    block = ctx.enter_context(nc.Block())

    @block.sync
    def _(sp):
        start_sp(sp)
        load_heads(sp, 0, COL_A, 0)
        decays_sp(sp)
        load_heads(sp, 1, COL_A, 1)
        with sp.Fori(2, HEADS) as h:
            load_heads(sp, BLK_A + h, COL_A, h)
        for j in range(2):
            load_heads(sp, BLK_B + j, COL_B, j)
        group_sp(sp, 0)
        with sp.Fori(2, KC) as j:
            load_heads(sp, BLK_B + j, COL_B, j)
            group_out_sp(sp, j - 2)
            group_sp(sp, j - 1)
        group_out_sp(sp, KC - 2)
        group_sp(sp, KC - 1)
        tail_sp(sp)

    def decays_beside(first, then, eng, turn=None):
        def between(hs):
            if hs == 2:
                first(eng)
            if hs == 6 and turn:
                turn(eng)
            if hs == (14 if turn else 5):
                then(eng)
        return between

    def beside(parts):
        def between(hs):
            for f, n, par in parts:
                f(n, par, hs)
        return between

    @block.tensor
    def _(pe):
        keys = lambda h, par, hs: keys_pe(pe, h, par, hs)
        rule = lambda h, par, hs: rule_pe(pe, h, par, hs)
        group = lambda j, par, hs: group_pe(pe, j, par, hs)
        start_pe(pe)
        pe_block(pe, 0, 0, in_hi, in_lo, decays_beside(decays_first_pe, decays_pe, pe, decays_turn_pe))
        pe.wait_ge(s["head_ready"], 1)
        pe_block(pe, 1, 1, in_hi, in_lo, beside([(keys, 0, 0)]))
        heads = lambda h, i: pe_block(pe, h + i, i, in_hi, in_lo, beside([(rule, h + (i - 2), i), (keys, h + (i - 1), 1 - i)]))
        heads(2, 0)
        heads(2, 1)
        with pe.Fori(4, HEADS, 2) as h:
            for i in range(2):
                heads(h, i)
        pe_block(pe, BLK_B, 0, in_hi, in_lo, beside([(rule, HEADS - 2, 0), (keys, HEADS - 1, 1)]))
        pe_block(pe, BLK_B + 1, 1, in_hi, in_lo, beside([(rule, HEADS - 1, 1), (group, 0, 0)]))
        groups = lambda j, i: pe_block(pe, BLK_B + j + i, i, in_hi, in_lo, beside([(group, j + (i - 1), 1 - i)]))
        groups(2, 0)
        groups(2, 1)
        with pe.Fori(4, KC, 2) as j:
            for i in range(2):
                groups(j, i)
        tail_pe(pe)

    @block.scalar
    def _(act):
        keys = lambda h, par, hs: keys_act(act, h, par, hs)
        rule = lambda h, par, hs: rule_act(act, h, par, hs)
        group = lambda j, par, hs: group_act(act, j, par, hs)
        start_act(act)
        for q in range(AHEAD):
            hi_piece(act, 0, q)
        act_block(act, 0, decays_beside(decays_first_act, decays_act, act))
        act.wait_ge(s["x_rms"], 2)
        act_block(act, 1, beside([(keys, 0, 0)]))
        heads = lambda h, i: act_block(act, h + i, beside([(rule, h + (i - 2), i), (keys, h + (i - 1), 1 - i)]))
        heads(2, 0)
        heads(2, 1)
        with act.Fori(4, HEADS, 2) as h:
            for i in range(2):
                heads(h, i)
        act_block(act, BLK_B, beside([(rule, HEADS - 2, 0), (keys, HEADS - 1, 1)]))
        act_block(act, BLK_B + 1, beside([(rule, HEADS - 1, 1), (group, 0, 0)]))
        groups = lambda j, i: act_block(act, BLK_B + j + i, beside([(group, j + (i - 1), 1 - i)]))
        groups(2, 0)
        groups(2, 1)
        with act.Fori(4, KC - 2, 2) as j:
            for i in range(2):
                groups(j, i)
        for j in (KC - 2, KC - 1):
            act_block(act, BLK_B + j, beside([(group, j - 1, 1 - j % 2)]))
        tail_act(act)

    @block.vector
    def _(dve):
        keys = lambda h, par, hs: keys_dve(dve, h, par, hs)
        rule = lambda h, par, hs: rule_dve(dve, h, par, hs)
        group = lambda j, par, hs: group_dve(dve, j, par, hs)
        start_dve(dve)
        for q in range(AHEAD):
            lo_piece(dve, 0, q)
        dve_block(dve, 0, decays_beside(decays_first_dve, decays_dve, dve))
        dve.wait_ge(s["gc_stored"], 32)
        dve.wait_ge(s["pads_ready"], 3)
        dve_block(dve, 1, beside([(keys, 0, 0)]))
        heads = lambda h, i: dve_block(dve, h + i, beside([(rule, h + (i - 2), i), (keys, h + (i - 1), 1 - i)]), BESIDE_HEADS)
        heads(2, 0)
        heads(2, 1)
        with dve.Fori(4, HEADS, 2) as h:
            for i in range(2):
                heads(h, i)
        dve_block(dve, BLK_B, beside([(rule, HEADS - 2, 0), (keys, HEADS - 1, 1)]))
        dve_block(dve, BLK_B + 1, beside([(rule, HEADS - 1, 1), (group, 0, 0)]))
        groups = lambda j, i: dve_block(dve, BLK_B + j + i, beside([(group, j + (i - 1), 1 - i)]))
        groups(2, 0)
        groups(2, 1)
        with dve.Fori(4, KC, 2) as j:
            for i in range(2):
                groups(j, i)
        tail_dve(dve)

    @block.gpsimd
    def _(pool):
        start_pool(pool)
        pool.wait_ge(s["head_ready"], 1)
        keys_pool(pool, 0, 0)
        for h in range(1, 3):
            keys_pool(pool, h, h % 2)
            rule_pool(pool, h - 1)
        with pool.Fori(3, HEADS - 1, 2) as h:
            for i in range(2):
                keys_pool(pool, h + i, 1 - i)
                rule_pool(pool, h + (i - 1))
        keys_pool(pool, HEADS - 1, 1)
        rule_pool(pool, HEADS - 2)
        group_pool(pool, 0, 0)
        rule_pool(pool, HEADS - 1)
        group_pool(pool, 1, 1)
        group_pool(pool, 2, 0)
        with pool.Fori(3, KC - 1, 2) as j:
            for i in range(2):
                group_pool(pool, j + i, 1 - i)
        group_pool(pool, KC - 1, 1)
        tail_pool(pool)


def kernel(**inputs):
    import concourse.bacc as bacc
    from concourse.bass_utils import run_bass_kernel_spmd

    nc = bacc.Bacc("TRN2", target_bir_lowering=False, num_devices=1)
    inputs = dict(inputs, shape_constants=shape_constants(), pool_bands=pool_bands(), causal_mask=causal_mask())
    arrays, t = {}, {}
    for name, value in inputs.items():
        arrays[f"in_{name}_dram"] = np.ascontiguousarray(value)
        t[name] = nc.dram_tensor(f"in_{name}_dram", value.shape, F32, kind="ExternalInput").ap()
    out = nc.dram_tensor("out_0_dram", (1, S, D), F32, kind="ExternalOutput").ap()
    with ExitStack() as ctx:
        program(nc, t, out[0], ctx)
    return run_bass_kernel_spmd(nc, [arrays], core_ids=[0]).results[0]["out_0_dram"]
```
